# Optimizing a Trainium2 kernel written in Bass

```python
import math
import jax, jax.numpy as jnp
from jax import lax
import numpy as np

D_MODEL = 1024
BATCH = 1
SEQ = 256
DEPTH = 2

N_A = DEPTH // 2
N_B = DEPTH - N_A
CONV_WIDTH = 31
N_HEADS = 8
HEAD_DIM = 64
V_DIM = 2 * HEAD_DIM
QK_WIDTH = 2 * N_HEADS * HEAD_DIM
V_WIDTH = N_HEADS * V_DIM
N_BUCKETS = 32
MAX_DISTANCE = 128
Q_BLOCK = 128
N_EXPERTS = 16
N_GROUPS = 4
EXPERTS_PER_GROUP = N_EXPERTS // N_GROUPS
TOP_K = 2
D_EXPERT = 512
ALPHA = (2.0 * DEPTH) ** 0.25
BETA = (8.0 * DEPTH) ** -0.25
LN_EPS = 1e-5


def layer_norm(x, g, b):
    xf = x.astype(jnp.float32)
    mu = jnp.mean(xf, -1, keepdims=True)
    var = jnp.mean(jnp.square(xf - mu), -1, keepdims=True)
    return ((xf - mu) * lax.rsqrt(var + LN_EPS) * g.astype(jnp.float32) + b.astype(jnp.float32)).astype(x.dtype)

def conformer_conv(x, w_pw1, b_pw1, w_dw, b_dw, g, b, w_pw2, b_pw2):
    h = x @ w_pw1 + b_pw1
    a, gate = jnp.split(h, 2, axis=-1)
    h = a * jax.nn.sigmoid(gate)
    h = lax.conv_general_dilated(
        h, w_dw[:, None, :].astype(h.dtype), window_strides=(1,),
        padding=[(CONV_WIDTH - 1, 0)],
        dimension_numbers=("NWC", "WIO", "NWC"),
        feature_group_count=D_MODEL) + b_dw
    h = jax.nn.silu(layer_norm(h, g, b))
    return h @ w_pw2 + b_pw2

def t5_bucket(n):
    n = jnp.maximum(n, 0)
    max_exact = N_BUCKETS // 2
    nf = jnp.maximum(n, 1).astype(jnp.float32)
    large = max_exact + (jnp.log(nf / max_exact) / math.log(MAX_DISTANCE / max_exact)
                         * (N_BUCKETS - max_exact)).astype(jnp.int32)
    large = jnp.minimum(large, N_BUCKETS - 1)
    return jnp.where(n < max_exact, n, large)

def diff_attention(x, k1, k2, v, w_q, lam_params, subln_g, w_o, rel_bias, layer_idx):
    bsz, seq, _ = x.shape
    n_blk = seq // Q_BLOCK
    lambda_init = 0.8 - 0.6 * math.exp(-0.3 * layer_idx)
    lp = lam_params.astype(jnp.float32)
    lam = jnp.exp(jnp.sum(lp[0] * lp[1])) - jnp.exp(jnp.sum(lp[2] * lp[3])) + lambda_init
    q = (x @ w_q).reshape(bsz, n_blk, Q_BLOCK, 2, N_HEADS, HEAD_DIM)
    q = jnp.transpose(q, (3, 1, 0, 4, 2, 5))
    scale = HEAD_DIM ** -0.5
    k_pos = jnp.arange(seq)

    def block(args):
        qb1, qb2, i = args
        q_pos = i * Q_BLOCK + jnp.arange(Q_BLOCK)
        rel = q_pos[:, None] - k_pos[None, :]
        bias = jnp.transpose(jnp.take(rel_bias, t5_bucket(rel), axis=0), (2, 0, 1)).astype(jnp.float32)
        causal = rel >= 0

        def probs(qb, k):
            s = jnp.einsum("bhqd,bhkd->bhqk", qb, k).astype(jnp.float32) * scale + bias
            return jax.nn.softmax(jnp.where(causal, s, -jnp.inf), axis=-1)

        a = probs(qb1, k1) - lam * probs(qb2, k2)
        return jnp.einsum("bhqk,bhkv->bhqv", a.astype(v.dtype), v)

    out = lax.map(block, (q[0], q[1], jnp.arange(n_blk)))
    out = jnp.transpose(out, (1, 0, 3, 2, 4)).reshape(bsz, seq, N_HEADS, V_DIM)
    of = out.astype(jnp.float32)
    of = of * lax.rsqrt(jnp.mean(jnp.square(of), -1, keepdims=True) + LN_EPS) * subln_g.astype(jnp.float32)
    of = of * (1.0 - lambda_init)
    return of.astype(x.dtype).reshape(bsz, seq, V_WIDTH) @ w_o

def grouped_moe(x, router_w, router_bias, w_gate, w_up, w_down):
    bsz, seq, d = x.shape
    x2 = x.reshape(-1, d)
    aff = jax.nn.sigmoid((x2 @ router_w).astype(jnp.float32))
    sel = (aff + router_bias.astype(jnp.float32)).reshape(-1, N_GROUPS, EXPERTS_PER_GROUP)
    grp_score = jnp.sum(lax.top_k(sel, 2)[0], -1)
    g_idx = jnp.argmax(grp_score, -1)
    in_grp = jnp.take_along_axis(sel, g_idx[:, None, None], axis=1)[:, 0]
    _, local = lax.top_k(in_grp, TOP_K)
    e_idx = g_idx[:, None] * EXPERTS_PER_GROUP + local
    w = jnp.take_along_axis(aff, e_idx, -1)
    w = w / jnp.sum(w, -1, keepdims=True)
    gates = jnp.sum(jax.nn.one_hot(e_idx, N_EXPERTS, dtype=jnp.float32) * w[..., None], axis=1)

    def step(acc, ew):
        g_e, wg_e, wu_e, wd_e = ew
        h = jax.nn.silu(x2 @ wg_e) * (x2 @ wu_e)
        return acc + (h @ wd_e) * g_e[:, None].astype(x2.dtype), None

    out, _ = lax.scan(step, jnp.zeros_like(x2), (gates.T, w_gate, w_up, w_down))
    return out.reshape(bsz, seq, d)

def first_inputs(seed: int = 0) -> dict:
    key = jax.random.key(seed)
    ks = jax.random.split(key, 32)
    nrm = jax.random.normal
    D, f32 = D_MODEL, jnp.float32
    w_kv_k = nrm(ks[9], (D, QK_WIDTH), f32) * D ** -0.5
    w_kv_v = nrm(ks[10], (D, V_WIDTH), f32) * D ** -0.5 * BETA
    return {
        "x": nrm(ks[0], (BATCH, SEQ, D), f32),
        "a_w_pw1": nrm(ks[1], (N_A, D, 2 * D), f32) * D ** -0.5,
        "a_b_pw1": 0.02 * nrm(ks[2], (N_A, 2 * D), f32),
        "a_w_dw": nrm(ks[3], (N_A, CONV_WIDTH, D), f32) * CONV_WIDTH ** -0.5,
        "a_b_dw": 0.02 * nrm(ks[4], (N_A, D), f32),
        "a_ln_g": 1.0 + 0.02 * nrm(ks[5], (N_A, D), f32),
        "a_ln_b": 0.02 * nrm(ks[6], (N_A, D), f32),
        "a_w_pw2": nrm(ks[7], (N_A, D, D), f32) * D ** -0.5 * BETA,
        "a_b_pw2": 0.02 * nrm(ks[8], (N_A, D), f32),
        "w_kv": jnp.concatenate([w_kv_k, w_kv_v], axis=1),
        "b_w_q": nrm(ks[11], (N_B, D, QK_WIDTH), f32) * D ** -0.5,
        "b_lambda": 0.1 * nrm(ks[12], (N_B, 4, HEAD_DIM), f32),
        "b_subln_g": 1.0 + 0.02 * nrm(ks[13], (N_B, V_DIM), f32),
        "b_w_o": nrm(ks[14], (N_B, V_WIDTH, D), f32) * V_WIDTH ** -0.5 * BETA,
        "rel_bias": 0.5 * nrm(ks[15], (N_BUCKETS, N_HEADS), f32),
        "ln_mix_g": 1.0 + 0.02 * nrm(ks[16], (DEPTH, D), f32),
        "ln_mix_b": 0.02 * nrm(ks[17], (DEPTH, D), f32),
        "ln_ffn_g": 1.0 + 0.02 * nrm(ks[18], (DEPTH, D), f32),
        "ln_ffn_b": 0.02 * nrm(ks[19], (DEPTH, D), f32),
        "router_w": nrm(ks[20], (D, N_EXPERTS), f32) * D ** -0.5,
        "router_bias": 0.01 * nrm(ks[21], (N_EXPERTS,), f32),
        "moe_w_gate": nrm(ks[22], (DEPTH, N_EXPERTS, D, D_EXPERT), f32) * D ** -0.5,
        "moe_w_up": nrm(ks[23], (DEPTH, N_EXPERTS, D, D_EXPERT), f32) * D ** -0.5,
        "moe_w_down": nrm(ks[24], (DEPTH, N_EXPERTS, D_EXPERT, D), f32) * D_EXPERT ** -0.5 * BETA,
    }

def first_block(x, a_w_pw1, a_b_pw1, a_w_dw, a_b_dw, a_ln_g, a_ln_b, a_w_pw2, a_b_pw2,
              w_kv, b_w_q, b_lambda, b_subln_g, b_w_o, rel_bias,
              ln_mix_g, ln_mix_b, ln_ffn_g, ln_ffn_b,
              router_w, router_bias, moe_w_gate, moe_w_up, moe_w_down):
    bsz, seq, _ = x.shape
    k1 = k2 = v = None
    for l in range(DEPTH):
        if l < N_A:
            mix = conformer_conv(x, a_w_pw1[l], a_b_pw1[l], a_w_dw[l], a_b_dw[l],
                                 a_ln_g[l], a_ln_b[l], a_w_pw2[l], a_b_pw2[l])
        else:
            if l == N_A:
                kv = x @ w_kv
                k = kv[..., :QK_WIDTH].reshape(bsz, seq, 2, N_HEADS, HEAD_DIM)
                k = jnp.transpose(k, (2, 0, 3, 1, 4))
                k1, k2 = k[0], k[1]
                v = jnp.transpose(kv[..., QK_WIDTH:].reshape(bsz, seq, N_HEADS, V_DIM), (0, 2, 1, 3))
            j = l - N_A
            mix = diff_attention(x, k1, k2, v, b_w_q[j], b_lambda[j], b_subln_g[j], b_w_o[j], rel_bias, l)
        x = layer_norm(ALPHA * x + mix, ln_mix_g[l], ln_mix_b[l])
        ffn = grouped_moe(x, router_w, router_bias, moe_w_gate[l], moe_w_up[l], moe_w_down[l])
        x = layer_norm(ALPHA * x + ffn, ln_ffn_g[l], ln_ffn_b[l])
    return x


DEPTH_2 = 1

N_META = 16
SSD_HEAD_DIM = 64
SSD_INNER = D_MODEL
SSD_HEADS = SSD_INNER // SSD_HEAD_DIM
SSD_GROUPS = 2
SSD_STATE = 128
SSD_CONV = 4
CHUNK = 128
SB_HEAD_DIM = 64
SB_WIDTH = D_MODEL
SB_HEADS = SB_WIDTH // SB_HEAD_DIM
MIX_WIDTH = SSD_INNER + SB_WIDTH
D_FF = 256 * ((8 * D_MODEL // 3 + 255) // 256)
FFN_CONV = 3
EPS = 1e-6

XBC_WIDTH = SSD_INNER + 2 * SSD_GROUPS * SSD_STATE
OFF_Z = 0
OFF_XBC = OFF_Z + SSD_INNER
OFF_DT = OFF_XBC + XBC_WIDTH
OFF_Q = OFF_DT + SSD_HEADS
OFF_K = OFF_Q + SB_WIDTH
OFF_V = OFF_K + SB_WIDTH
IN_COLS = OFF_V + SB_WIDTH


def rms_norm(x, g):
    x32 = x.astype(jnp.float32)
    y = x32 * lax.rsqrt(jnp.mean(x32 * x32, axis=-1, keepdims=True) + EPS)
    return (y * g.astype(jnp.float32)).astype(x.dtype)

def causal_dwconv(x, w, b):
    K = w.shape[0]
    L = x.shape[1]
    xp = jnp.pad(x, ((0, 0), (K - 1, 0), (0, 0)))
    y = b
    for k in range(K):
        y = y + xp[:, k:k + L] * w[k]
    return y

def ssd_mixer(z, xbc, dt_raw, conv_w, conv_b, dt_bias, a_log, d_skip, norm_g):
    out_dtype = z.dtype
    Bsz, L, _ = xbc.shape
    H, P, G, N = SSD_HEADS, SSD_HEAD_DIM, SSD_GROUPS, SSD_STATE
    J = H // G
    f32 = jnp.float32
    xbc = jax.nn.silu(causal_dwconv(xbc, conv_w, conv_b)).astype(f32)
    xs = xbc[..., :SSD_INNER].reshape(Bsz, L, H, P)
    Bm = xbc[..., SSD_INNER:SSD_INNER + G * N].reshape(Bsz, L, G, N)
    Cm = xbc[..., SSD_INNER + G * N:].reshape(Bsz, L, G, N)
    dt = jax.nn.softplus(dt_raw.astype(f32) + dt_bias.astype(f32))
    A = -jnp.exp(a_log.astype(f32))

    pad = CHUNK - N_META
    Lp = L + pad
    nc = Lp // CHUNK

    def front_pad(t):
        return jnp.pad(t, ((0, 0), (pad, 0)) + ((0, 0),) * (t.ndim - 2))

    Xdt = front_pad(xs * dt[..., None]).reshape(Bsz, nc, CHUNK, G, J, P)
    Adt = front_pad(dt * A).reshape(Bsz, nc, CHUNK, G, J).transpose(0, 3, 4, 1, 2)
    Bc = front_pad(Bm).reshape(Bsz, nc, CHUNK, G, N)
    Cc = front_pad(Cm).reshape(Bsz, nc, CHUNK, G, N)

    Acs = jnp.cumsum(Adt, axis=-1)
    causal = jnp.tril(jnp.ones((CHUNK, CHUNK), dtype=bool))
    seg = Acs[..., :, None] - Acs[..., None, :]
    Ldec = jnp.where(causal, jnp.exp(jnp.where(causal, seg, 0.0)), 0.0)

    CB = jnp.einsum('bclgn,bcsgn->bgcls', Cc, Bc)
    y_diag = jnp.einsum('bgcls,bgjcls,bcsgjp->bclgjp', CB, Ldec, Xdt)

    decay_states = jnp.exp(Acs[..., -1:] - Acs)
    states = jnp.einsum('bclgn,bgjcl,bclgjp->bcgjpn', Bc, decay_states, Xdt)
    chunk_decay = jnp.exp(Acs[..., -1])

    def step(carry, inp):
        st, dec = inp
        return carry * dec[..., None, None] + st, carry

    init = jnp.zeros((Bsz, G, J, P, N), f32)
    _, prev = lax.scan(step, init, (states.transpose(1, 0, 2, 3, 4, 5),
                                    chunk_decay.transpose(3, 0, 1, 2)))
    prev = prev.transpose(1, 0, 2, 3, 4, 5)

    y_off = jnp.einsum('bclgn,bcgjpn,bgjcl->bclgjp', Cc, prev, jnp.exp(Acs))

    y = (y_diag + y_off).reshape(Bsz, Lp, H, P)[:, pad:]
    y = y + xs * d_skip.astype(f32)[:, None]
    y = y.reshape(Bsz, L, SSD_INNER) * jax.nn.silu(z.astype(f32))
    return rms_norm(y, norm_g).astype(out_dtype)

def stick_breaking_attention(q, k, v):
    out_dtype = q.dtype
    Bsz, L, H, D = q.shape
    f32 = jnp.float32
    scale = 1.0 / math.sqrt(D)
    pad = Q_BLOCK - N_META
    Lp = L + pad
    nb = Lp // Q_BLOCK
    padw = ((0, 0), (pad, 0), (0, 0), (0, 0))
    qp = jnp.pad(q.astype(f32), padw)
    kp = jnp.pad(k.astype(f32), padw)
    vp = jnp.pad(v.astype(f32), padw)
    qb = qp.reshape(Bsz, nb, Q_BLOCK, H, D).transpose(1, 0, 2, 3, 4)
    key_pos = jnp.arange(Lp)

    def block(args):
        i, qi = args
        q_pos = i * Q_BLOCK + jnp.arange(Q_BLOCK)
        valid = (key_pos[None, :] < q_pos[:, None]) & (key_pos[None, :] >= pad)
        zlog = jnp.einsum('bqhd,bkhd->bhqk', qi, kp) * scale
        log_beta = jax.nn.log_sigmoid(zlog)
        log_keep = jnp.where(valid, log_beta - zlog, 0.0)
        after = lax.cumsum(log_keep, axis=3, reverse=True) - log_keep
        w = jnp.where(valid, jnp.exp(log_beta + after), 0.0)
        return jnp.einsum('bhqk,bkhd->bqhd', w, vp)

    o = lax.map(block, (jnp.arange(nb), qb))
    o = o.transpose(1, 0, 2, 3, 4).reshape(Bsz, Lp, H, D)[:, pad:]
    return o.astype(out_dtype)

def second_inputs(seed: int = 0) -> dict:
    key = jax.random.key(seed)
    ks = jax.random.split(key, 20)
    f32 = jnp.float32

    def gain(k, n):
        return 1.0 + 0.05 * jax.random.normal(k, (DEPTH_2, n), f32)

    dt0 = jnp.exp(jax.random.uniform(ks[5], (DEPTH_2, SSD_HEADS), f32,
                                     math.log(1e-3), math.log(1e-1)))
    dt_bias = dt0 + jnp.log(-jnp.expm1(-dt0))
    return {
        "x": jax.random.normal(ks[0], (BATCH, SEQ, D_MODEL), f32),
        "meta_tokens": jax.random.normal(ks[1], (N_META, D_MODEL), f32),
        "mix_pre_g": gain(ks[2], D_MODEL),
        "w_in": jax.random.normal(ks[3], (DEPTH_2, D_MODEL, IN_COLS), f32) * D_MODEL ** -0.5,
        "ssd_conv_w": jax.random.normal(ks[4], (DEPTH_2, SSD_CONV, XBC_WIDTH), f32) * SSD_CONV ** -0.5,
        "ssd_conv_b": 0.01 * jax.random.normal(ks[6], (DEPTH_2, XBC_WIDTH), f32),
        "ssd_dt_bias": dt_bias,
        "ssd_a_log": jnp.log(jax.random.uniform(ks[7], (DEPTH_2, SSD_HEADS), f32, 1.0, 16.0)),
        "ssd_d": 1.0 + 0.1 * jax.random.normal(ks[8], (DEPTH_2, SSD_HEADS), f32),
        "ssd_norm_g": gain(ks[9], SSD_INNER),
        "sb_norm_g": gain(ks[10], SB_WIDTH),
        "w_out": jax.random.normal(ks[11], (DEPTH_2, MIX_WIDTH, D_MODEL), f32) * MIX_WIDTH ** -0.5,
        "mix_post_g": gain(ks[12], D_MODEL),
        "ffn_pre_g": gain(ks[13], D_MODEL),
        "w_up": jax.random.normal(ks[14], (DEPTH_2, D_MODEL, 2 * D_FF), f32) * D_MODEL ** -0.5,
        "ffn_conv_w": jax.random.normal(ks[15], (DEPTH_2, FFN_CONV, D_FF), f32) * FFN_CONV ** -0.5,
        "ffn_conv_b": 0.01 * jax.random.normal(ks[16], (DEPTH_2, D_FF), f32),
        "w_down": jax.random.normal(ks[17], (DEPTH_2, D_FF, D_MODEL), f32) * D_FF ** -0.5,
        "ffn_post_g": gain(ks[18], D_MODEL),
    }

def second_block(x, meta_tokens, mix_pre_g, w_in, ssd_conv_w, ssd_conv_b, ssd_dt_bias,
              ssd_a_log, ssd_d, ssd_norm_g, sb_norm_g, w_out, mix_post_g, ffn_pre_g,
              w_up, ffn_conv_w, ffn_conv_b, w_down, ffn_post_g):
    Bsz = x.shape[0]
    meta = jnp.broadcast_to(meta_tokens.astype(x.dtype)[None], (Bsz, N_META, x.shape[-1]))
    h = jnp.concatenate([meta, x], axis=1)
    L = h.shape[1]
    for l in range(DEPTH_2):
        xn = rms_norm(h, mix_pre_g[l])
        proj = xn @ w_in[l]
        z = proj[..., OFF_Z:OFF_XBC]
        xbc = proj[..., OFF_XBC:OFF_DT]
        dt_raw = proj[..., OFF_DT:OFF_Q]
        q = proj[..., OFF_Q:OFF_K].reshape(Bsz, L, SB_HEADS, SB_HEAD_DIM)
        k = proj[..., OFF_K:OFF_V].reshape(Bsz, L, SB_HEADS, SB_HEAD_DIM)
        v = proj[..., OFF_V:IN_COLS].reshape(Bsz, L, SB_HEADS, SB_HEAD_DIM)
        y_ssd = ssd_mixer(z, xbc, dt_raw, ssd_conv_w[l], ssd_conv_b[l], ssd_dt_bias[l],
                          ssd_a_log[l], ssd_d[l], ssd_norm_g[l])
        y_sb = rms_norm(stick_breaking_attention(q, k, v).reshape(Bsz, L, SB_WIDTH), sb_norm_g[l])
        mix = jnp.concatenate([y_ssd, y_sb], axis=-1) @ w_out[l]
        h = h + rms_norm(mix, mix_post_g[l])
        xn = rms_norm(h, ffn_pre_g[l])
        gu = xn @ w_up[l]
        g = causal_dwconv(gu[..., :D_FF], ffn_conv_w[l], ffn_conv_b[l])
        f = (jax.nn.gelu(g, approximate=True) * gu[..., D_FF:]) @ w_down[l]
        h = h + rms_norm(f, ffn_post_g[l])
    return h[:, N_META:]


def setup_inputs(seed=0):
    out = dict(first_inputs(seed))
    for name, value in second_inputs(seed + 1).items():
        if name != "x":
            out[name + "_2"] = value
    return out


def reference(
    x, a_w_pw1, a_b_pw1, a_w_dw, a_b_dw, a_ln_g, a_ln_b, a_w_pw2, a_b_pw2, w_kv, b_w_q,
    b_lambda, b_subln_g, b_w_o, rel_bias, ln_mix_g, ln_mix_b, ln_ffn_g, ln_ffn_b, router_w,
    router_bias, moe_w_gate, moe_w_up, moe_w_down, meta_tokens_2, mix_pre_g_2, w_in_2,
    ssd_conv_w_2, ssd_conv_b_2, ssd_dt_bias_2, ssd_a_log_2, ssd_d_2, ssd_norm_g_2, sb_norm_g_2,
    w_out_2, mix_post_g_2, ffn_pre_g_2, w_up_2, ffn_conv_w_2, ffn_conv_b_2, w_down_2,
    ffn_post_g_2,
):
    x = first_block(
        x, a_w_pw1, a_b_pw1, a_w_dw, a_b_dw, a_ln_g, a_ln_b, a_w_pw2, a_b_pw2, w_kv, b_w_q,
        b_lambda, b_subln_g, b_w_o, rel_bias, ln_mix_g, ln_mix_b, ln_ffn_g, ln_ffn_b, router_w,
        router_bias, moe_w_gate, moe_w_up, moe_w_down,
    )
    return second_block(
        x, meta_tokens_2, mix_pre_g_2, w_in_2, ssd_conv_w_2, ssd_conv_b_2, ssd_dt_bias_2,
        ssd_a_log_2, ssd_d_2, ssd_norm_g_2, sb_norm_g_2, w_out_2, mix_post_g_2, ffn_pre_g_2,
        w_up_2, ffn_conv_w_2, ffn_conv_b_2, w_down_2, ffn_post_g_2,
    )


_drawn_inputs = setup_inputs


def setup_inputs(seed=0):
    import zlib

    import numpy as np

    out = dict(_drawn_inputs(seed))
    spreads = {}
    factors = {'b_subln_g': 2.852, 'ssd_conv_b_2': 6.832, 'ffn_conv_b_2': 8.0}
    for name, (base, spread) in spreads.items():
        noise = np.random.default_rng([zlib.crc32(name.encode()), seed]).standard_normal(out[name].shape)
        drawn = base * np.exp(spread * noise) if base else spread * noise
        out[name] = __import__('jax').numpy.asarray(drawn.astype(out[name].dtype))
    for name, factor in factors.items():
        out[name] = (out[name] * factor).astype(out[name].dtype)
    return out
```

```python
import math
from contextlib import ExitStack

import numpy as np

import concourse.bass as bass
from concourse import mybir

ARENA = 16640
F32 = mybir.dt.float32
ALU = mybir.AluOpType
ACT = mybir.ActivationFunctionType
AX_X = mybir.AxisListType.X

P = 128
D = 1024
KC = D // P
SEQ = 256
META = 16
L = META + SEQ
DEPTH = 2
ALPHA = (2.0 * DEPTH) ** 0.25
LN_EPS = 1e-5
TAPS = 31
HEADS, HD = 8, 64
N_BUCKETS, MAX_DISTANCE = 32, 128
LAMBDA_INIT = 0.8 - 0.6 * math.exp(-0.3 * 1)
MASKED = -1e30
EXPERTS, GROUPS, PER_GROUP, DE = 16, 4, 4, 512
RING = 6
BANKS = 4
TILE_AT, TILE_N = (0, META, META + P), (META, P, P)

SSD_HEADS, SSD_GROUPS, STATE, SSD_TAPS = 16, 2, 128, 4
XBC = D + 2 * SSD_GROUPS * STATE
XC = XBC // P
SB_HEADS = 16
EPS = 1e-6
D_FF = 2816
FC = D_FF // P
FFN_TAPS = 3
OFF_XBC = D
OFF_DT = OFF_XBC + XBC
OFF_Q = OFF_DT + SSD_HEADS
OFF_K, OFF_V = OFF_Q + D, OFF_Q + 2 * D

VEC_ROWS = [
    [("a_w_dw", 0, 128)],
    [("a_w_dw", 128, 120), ("a_b_dw", 0, 8)],
    [("a_ln_g", 0, 8), ("a_ln_b", 0, 8), ("a_b_pw1", 0, 16), ("mix_pre_g_2", 0, 8), ("ssd_norm_g_2", 0, 8),
     ("sb_norm_g_2", 0, 8), ("ffn_pre_g_2", 0, 8), ("ssd_conv_w_2", 0, SSD_TAPS * XC), ("ssd_conv_b_2", 0, XC)],
    [("ffn_conv_w_2", 0, FFN_TAPS * FC), ("ffn_conv_b_2", 0, FC)],
]
VEC_COL = {}
for _tile, _rows in enumerate(VEC_ROWS):
    _at = 0
    for _name, _first, _n in _rows:
        VEC_COL.setdefault(_name, _tile * P + _at)
        _at += _n

JOBS = [
    ("vec", 1), ("relb", 1), ("conv_xT", 4), ("glu", 8), ("conv_mean", 1), ("conv_var", 1), ("pw2", 4), ("mix0_xT", 4),
    ("route0", 1), ("moe0", 96), ("ffn0_xT", 4),
    ("att_k", 8), ("att_v", 4), ("att_q", 8), ("att_heads", 3 * 16), ("att_T", 4), ("att_o", 4),
    ("mix1_xT", 4), ("route1", 1), ("moe1", 96), ("ffn1_xT", 0),
    ("pre_xT", 6), ("z", 6), ("xbc", XC), ("dt", 1), ("ssd", 3 * 11 + 2 * 2 + 2 * 2), ("y_T", 6),
    ("sb_q", 8), ("sb_k", 8), ("sb_v", 6), ("sb_heads", SB_HEADS), ("sb_T", 6), ("w_out", 6),
    ("ffn_T", 6), ("up", 2 * FC),
]


def first_jobs():
    at, out = 0, {}
    for name, n in JOBS:
        out[name] = at
        at += n
    return out


def t5_bucket(n):
    exact = N_BUCKETS // 2
    nf = np.maximum(n, 1).astype(np.float32)
    large = exact + (np.log(nf / np.float32(exact)) / np.float32(math.log(MAX_DISTANCE / exact))
                     * np.float32(N_BUCKETS - exact)).astype(np.int32)
    return np.where(n < exact, n, np.minimum(large, N_BUCKETS - 1))


def bucket_table():
    table = np.zeros((N_BUCKETS, 3 * P), np.float32)
    j = np.arange(SEQ)
    table[t5_bucket(SEQ - 1 - j), j] = 1.0
    return table


class Chain:

    def __init__(self, eng, sem):
        self.eng, self.sem, self.n = eng, sem, 0

    def __call__(self, ins):
        self.n += 1
        ins.then_inc(self.sem, 1)
        self.eng.wait_ge(self.sem, self.n)


def program(nc, a, out, stop=None):
    ctx = ExitStack()

    def sb(name, *shape):
        return ctx.enter_context(nc.sbuf_tensor(name, list(shape), F32))

    def sem(name):
        return ctx.enter_context(nc.semaphore(name))

    FJ = first_jobs()
    ring = sb("ring", P, RING, 4096)
    x_nat = sb("x_nat", P, 3, D)
    xT = sb("xT", P, KC, L)
    norm_rows = sb("norm_rows", P, 2, 2, D)
    vec = sb("vec", P, 4 * P)
    ident = sb("ident", P, P)
    ones = sb("ones", P, P)
    router_w = sb("router_w", P, KC, EXPERTS)
    router_b = sb("router_b", P, EXPERTS)
    gates = sb("gates", P, 2, EXPERTS)
    eps_cols = sb("eps_cols", P, 2)
    lam_rows = sb("lam_rows", P, 4, HD)
    subln_rows = sb("subln_rows", P, 2 * HD)
    rel_w = sb("rel_w", N_BUCKETS, HEADS)
    flip = sb("flip", P, P)
    upto, neg_from, neg_ones = sb("upto", P, P), sb("neg_from", P, P), sb("neg_ones", P, P)
    ssd_rows = sb("ssd_rows", P, 3, SSD_HEADS)
    w_dt = sb("w_dt", P, KC, SSD_HEADS)
    dts = sb("dts", P, 10, 3 * SSD_HEADS)
    small = sb("small", P, 64)
    stats = sb("stats", P, 3, 2, 6)
    arena = sb("arena", P, ARENA)

    psum = ctx.enter_context(nc.psum_tensor("psum", [P, 8, 512], F32))
    rel_scratch = nc.dram_tensor("rel_scratch", (HEADS, 3 * P), F32).ap()

    slot_loaded = [sem(f"slot_loaded{i}") for i in range(RING)]
    job_done = sem("job_done")
    bank_free = [sem(f"bank_free{i}") for i in range(BANKS)]
    stage_left = sem("stage_left")
    consts_loaded = sem("consts_loaded")
    consts_made = sem("consts_made")
    norm_loaded = [sem("norm_loaded0"), sem("norm_loaded1")]
    output_written = sem("output_written")
    var_ready, std_ready = sem("var_ready"), sem("std_ready")
    dve_step, act_step = Chain(nc.vector, sem("dve_step")), Chain(nc.scalar, sem("act_step"))
    pool_step = Chain(nc.gpsimd, sem("pool_step"))

    def carve(at, *shape):
        n = int(np.prod(shape))
        assert at + n <= ARENA, (at, n)
        flat = arena[:, at:at + n]
        if len(shape) == 1:
            return flat
        names = "abcd"[:len(shape)]
        return flat.rearrange(f"p ({' '.join(names)}) -> p {' '.join(names)}", **dict(zip(names, shape)))

    def column(name, i):
        at = VEC_COL[name] + i
        return vec[:, at:at + 1]

    def bank(j):
        return psum[:, j % BANKS, :]

    def take_bank(j):
        if j >= BANKS:
            nc.tensor.wait_ge(bank_free[j % BANKS], j // BANKS)

    def job_ready(eng, j):
        eng.wait_ge(job_done, j + 1)

    def all_read_out(eng, j):
        for b in range(BANKS):
            eng.wait_ge(bank_free[b], (j - b + BANKS - 1) // BANKS)

    def products(dst, pairs):
        for n, (lhsT, rhs) in enumerate(pairs):
            last = nc.tensor.matmul(dst, lhsT, rhs, start=(n == 0), stop=(n == len(pairs) - 1))
        return last

    def columns_of(w, at, n=512):
        return w[:, at:at + n].rearrange("(k p) n -> p k n", p=P)

    units = []

    def add_units(name, srcs, last_jobs):
        first = len(units)
        for s, j in zip(srcs, last_jobs):
            units.append((s, ("job", j)))
        unit_at[name] = first

    unit_at = {}
    w_pw1 = a["a_w_pw1"][0]
    add_units("pw1", [columns_of(w_pw1, c) for c in (0, D, 512, D + 512)],
              [FJ["glu"] + n for n in (3, 3, 7, 7)])
    add_units("pw2", [columns_of(a["a_w_pw2"][0], c) for c in (0, 512)], [FJ["pw2"] + n for n in (1, 3)])

    def add_moe(layer):
        unit_at[f"moe{layer}"] = len(units)
        for e in range(EXPERTS):
            jobs_g = FJ[f"moe{layer}"] + 3 * (2 * e + 1) - 1
            units.append((("gate", layer, e), ("job", jobs_g)))
            units.append((("up", layer, e), ("job", jobs_g + 2)))
            units.append((("down", layer, e), ("down", layer, 2 * e + 2)))

    add_moe(0)
    w_kv, w_q, w_o = a["w_kv"], a["b_w_q"][0], a["b_w_o"][0]
    add_units("w_k", [columns_of(w_kv, c) for c in (0, 512)], [FJ["att_k"] + n for n in (3, 7)])
    add_units("w_v", [columns_of(w_kv, c) for c in (D, D + 512)], [FJ["att_v"] + n for n in (1, 3)])
    add_units("w_q", [columns_of(w_q, c) for c in (0, 512)], [FJ["att_q"] + n for n in (3, 7)])
    add_units("w_o", [columns_of(w_o, c) for c in (0, 512)], [FJ["att_o"] + n for n in (1, 3)])
    add_moe(1)
    w_in, w_out, w_up, w_down = a["w_in_2"][0], a["w_out_2"][0], a["w_up_2"][0], a["w_down_2"][0]
    add_units("w_z", [columns_of(w_in, c) for c in (0, 512)], [FJ["z"] + n for n in (2, 5)])
    add_units("w_xbc", [columns_of(w_in, OFF_XBC + c) for c in (0, 512, 1024)], [FJ["xbc"] + n for n in (3, 7, 11)])
    add_units("w_sb_q", [columns_of(w_in, OFF_Q + c) for c in (0, 512)], [FJ["sb_q"] + n for n in (3, 7)])
    add_units("w_sb_k", [columns_of(w_in, OFF_K + c) for c in (0, 512)], [FJ["sb_k"] + n for n in (3, 7)])
    add_units("w_sb_v", [columns_of(w_in, OFF_V + c) for c in (0, 512)], [FJ["sb_v"] + n for n in (2, 5)])
    add_units("w_out", [columns_of(w_out[part * D:part * D + D], half * 512) for half in range(2) for part in range(2)],
              [FJ["w_out"] + n for n in (2, 2, 5, 5)])
    add_units("w_up", [(columns_of(w_up, 2 * P * n, 2 * P), columns_of(w_up, D_FF + 2 * P * n, 2 * P))
                       for n in range(FC // 2)], [FJ["up"] + 4 * n + 3 for n in range(FC // 2)])
    unit_at["w_down"] = len(units)
    for n in range((FC + 3) // 4):
        rows_n = min(4, FC - 4 * n)
        units.append((("rows", w_down[4 * n * P:(4 * n + rows_n) * P].rearrange("(k p) n -> p k n", p=P), rows_n),
                      ("last",)))

    def slot(u):
        return ring[:, u % RING, :]

    def slot_k(u, n=512):
        return slot(u).rearrange("p (k n) -> p k n", n=n)

    def loads_of(u):
        return 16 * sum(2 if isinstance(units[v][0], tuple) and not isinstance(units[v][0][0], str) else 1
                        for v in range(u % RING, u + 1, RING))

    def unit_ready(u):
        nc.tensor.wait_ge(slot_loaded[u % RING], loads_of(u))

    block = ctx.enter_context(nc.Block())

    down_done = [sem("down_done0"), sem("down_done1")]

    @block.sync
    def _(sp):
        def slot_freed(u, i=0):
            if u < RING:
                return
            free = units[u - RING][1]
            if free[0] == "job":
                sp.wait_ge(job_done, free[1] + 1 + 12 * i)
            else:
                sp.wait_ge(down_done[free[1]], free[2] + 4 * i)

        def load(u, src, dst=None):
            sp.dma_start(slot_k(u) if dst is None else dst, src).then_inc(slot_loaded[u % RING], 16)

        def load_expert(u, kind, layer, e):
            if kind == "down":
                src = a["moe_w_down"][layer, e if isinstance(e, int) else bass.ds(e, 1)]
                src = src.rearrange("(k p) n -> p k n" if isinstance(e, int) else "a (k p) n -> p (a k) n", p=P)
                load(u, src, slot_k(u, D))
            else:
                src = a[f"moe_w_{kind}"][layer, e if isinstance(e, int) else bass.ds(e, 1)]
                src = src.rearrange("(k p) n -> p k n" if isinstance(e, int) else "a (k p) n -> p (a k) n", p=P)
                load(u, src)

        u = 0
        until = len(units)
        if stop is not None:
            until = {'constants': 6, 'conformer': 6, 'mix_norm0': 6}.get(stop, until)
            if stop in ('moe0', 'ffn_norm0'):
                until = 54
            if stop in ('attention', 'mix_norm1'):
                until = unit_at['moe1']
            if stop in ('moe1', 'ffn_norm1', 'pre_norm', 'inner', 'ssd', 'ssd_norm'):
                until = unit_at['w_sb_q']
            if stop in ('stick_breaking', 'sb_norm'):
                until = unit_at['w_out']
            if stop in ('mix_post', 'ffn_pre'):
                until = unit_at['w_up']
        while u < until:
            src = units[u][0]
            if isinstance(src, tuple) and src[0] == "gate" and src[2] == 2:
                with sp.Fori(0, EXPERTS // 2 - 1) as i:
                    for n in range(RING):
                        slot_freed(u + n, i)
                        load_expert(u + n, units[u + n][0][0], src[1], i * 2 + 2 + n // 3)
                u += 3 * (EXPERTS - 2)
                continue
            slot_freed(u)
            if isinstance(src, tuple) and src[0] in ("gate", "up", "down"):
                load_expert(u, *src)
            elif isinstance(src, tuple) and src[0] == "rows":
                load(u, src[1], slot_k(u, D)[:, 0:src[2], :])
            elif isinstance(src, tuple):
                for side in range(2):
                    sp.dma_start(slot_k(u)[:, :, side * 256:side * 256 + 256], src[side]).then_inc(
                        slot_loaded[u % RING], 16)
            else:
                load(u, src)
            u += 1

    stages = []
    left = [0]
    norm_count = [0, 0]
    compute = (nc.tensor, nc.scalar, nc.vector, nc.gpsimd)

    def stage(f):
        stages.append(f)
        return f

    def next_stage():
        n = left[0] = left[0] + 1

        def meet(eng):
            eng.drain().then_inc(stage_left, 1)
            eng.wait_ge(stage_left, len(compute) * n)

        block.tensor(meet)
        block.scalar(meet)
        block.vector(meet)
        block.gpsimd(meet)

    def transposes_pe(first, tiles, src, ready=None):
        j = first
        for t in tiles:
            n = TILE_N[t]
            if ready is not None:
                ready(t)
            for half in range(2):
                take_bank(j)
                for c in range(4):
                    at = (4 * half + c) * P
                    last = nc.tensor.transpose(bank(j)[:, c * P:c * P + n], src(t)[0:n, at:at + P], ident[0:n, 0:n])
                last.then_inc(job_done, 1)
                j += 1

    def transposes_out(first, tiles, dst, gain=None):
        act = nc.scalar
        j = first
        for t in tiles:
            n, at = TILE_N[t], TILE_AT[t]
            for half in range(2):
                job_ready(act, j)
                src = bank(j).rearrange("p (c t) -> p c t", c=4)[:, :, 0:n]
                if gain is None:
                    act.activation(dst[:, 4 * half:4 * half + 4, at:at + n], src, ACT.Copy).then_inc(
                        bank_free[j % BANKS], 1)
                else:
                    for c in range(4):
                        last = act.activation(dst[:, 4 * half + c, at:at + n], src[:, c, :], ACT.Copy,
                                              scale=column(gain, 4 * half + c))
                    last.then_inc(bank_free[j % BANKS], 1)
                j += 1

    def load_norm(k, gain, bias=None):
        act = nc.scalar
        norm_count[k % 2] += 32
        act.dma_start(norm_rows[:, k % 2, 0, :], gain.partition_broadcast(P)).then_inc(norm_loaded[k % 2], 16)
        b = gain if bias is None else bias
        act.dma_start(norm_rows[:, k % 2, 1, :], b.partition_broadcast(P)).then_inc(norm_loaded[k % 2], 16)

    rsqrt_n = [0]

    def next_sqrt():
        rsqrt_n[0] += 1
        return rsqrt_n[0]

    def sqrt_of(act, values, scale, eps, n):
        act.wait_ge(var_ready, n)
        p = values.shape[0]
        bias = eps_cols[0:p, 0:1] if eps == LN_EPS else eps_cols[0:p, 1:2]
        act.activation(values, values, ACT.Sqrt, bias=bias, scale=scale).then_inc(std_ready, 1)

    def reciprocal_of(dve, values, n):
        dve.wait_ge(std_ready, n)
        dve_step(dve.reciprocal(values, values))

    def layer_norm(k, name, normed, last=False):
        mean_var = small[:, 2:6].rearrange("p (t s) -> p t s", s=2)
        root = next_sqrt()

        @block.vector
        def _(dve):
            dve.wait_ge(norm_loaded[k % 2], 32 * (k // 2 + 1))
            for t in (1, 2):
                for half in range(2):
                    dve_last = dve.bn_stats(stats[:, t, half, :], x_nat[:, t, half * 512:half * 512 + 512])
                dve_step(dve_last)
            for t in (1, 2):
                dve_last = dve.bn_aggr(small[:, 2 * t:2 * t + 2], stats[:, t, :, :])
            dve_last.then_inc(var_ready, 1)
            reciprocal_of(dve, mean_var[:, :, 1], root)
            for t in (1, 2):
                dve_step(dve.tensor_scalar(x_nat[:, t, :], x_nat[:, t, :], small[:, 2 * t:2 * t + 1],
                                           small[:, 2 * t + 1:2 * t + 2], ALU.subtract, ALU.mult))
                dve_step(dve.tensor_tensor(x_nat[:, t, :], x_nat[:, t, :], norm_rows[:, k % 2, 0, :], ALU.mult))
                dve.tensor_tensor(x_nat[:, t, :], x_nat[:, t, :], norm_rows[:, k % 2, 1, :], ALU.add).then_inc(
                    normed, 1)

        block.scalar(lambda act: sqrt_of(act, mean_var[:, :, 1], 1.0, LN_EPS, root))
        if last:
            return

        @block.tensor
        def _(pe):
            transposes_pe(FJ[name], (1, 2), lambda t: x_nat[:, t, :], lambda t: pe.wait_ge(normed, t))

        @block.scalar
        def _(act):
            transposes_out(FJ[name], (1, 2), xT)

    def project_natural(first, u0, lhs, tiles, k_chunks, bias=None):
        j = first
        for half in range(2):
            unit_ready(u0 + half)
            for t in tiles:
                n, at = TILE_N[t], TILE_AT[t]
                take_bank(j)
                pairs = [(lhs[:, k, at:at + n], slot_k(u0 + half)[:, k, :]) for k in range(k_chunks)]
                if bias is not None:
                    pairs.append((ones[0:1, 0:n], bias[:, half * 512:half * 512 + 512]))
                products(bank(j)[0:n, :], pairs).then_inc(job_done, 1)
                j += 1

    def add_residual(first, tiles=(1, 2)):
        j = first
        for half in range(2):
            for t in tiles:
                job_ready(nc.vector, j)
                xs = x_nat[:, t, half * 512:half * 512 + 512]
                ins = nc.vector.scalar_tensor_tensor(xs, xs, ALPHA, bank(j), ALU.mult, ALU.add)
                ins.then_inc(bank_free[j % BANKS], 1)
                j += 1
        return ins

    rows = carve(0, 4, P)
    b_pw2 = arena[0:1, 8000:8000 + D]
    buckets = arena[0:N_BUCKETS, 9100:9100 + 3 * P]
    by_distance = arena[0:HEADS, 9500:9500 + 3 * P]
    inputs_loaded = sem("inputs_loaded")
    INPUT_DMAS = 13
    rel_written = sem("rel_written")
    rows_cleared = sem("rows_cleared")

    @stage
    def constants():
        @block.gpsimd
        def _(pool):
            pool_step(pool.memset(ident[:, :], 0.0))
            pool_step(pool.affine_select(out=ident[:, :], in_=ident[:, :], compare_op=ALU.not_equal, fill=1.0, base=0,
                                         pattern=[[-1, P]], channel_multiplier=1))
            pool.memset(rows[:, :, :], 0.0).then_inc(rows_cleared, 1)
            pool_step(pool.memset(ones[:, :], 1.0))
            pool_step(pool.memset(flip[:, :], 0.0))
            pool_step(pool.affine_select(out=flip[:, :], in_=flip[:, :], compare_op=ALU.not_equal, fill=1.0,
                                         base=1 - P, pattern=[[1, P]], channel_multiplier=1))
            pool_step(pool.memset(by_distance, MASKED))
            pool_step(pool.memset(upto[:, :], 1.0))
            pool_step(pool.affine_select(out=upto[:, :], in_=upto[:, :], compare_op=ALU.is_ge, fill=0.0,
                                         base=0, pattern=[[1, P]], channel_multiplier=-1))
            pool_step(pool.memset(neg_ones[:, :], -1.0))
            pool_step(pool.affine_select(out=neg_from[:, :], in_=neg_ones[:, :], compare_op=ALU.is_ge, fill=0.0,
                                         base=0, pattern=[[-1, P]], channel_multiplier=1))
            pool_step(pool.memset(eps_cols[:, 0:1], LN_EPS))
            pool_step(pool.memset(eps_cols[:, 1:2], EPS))
            pool.nop().then_inc(consts_made, 1)

        @block.scalar
        def _(act):
            act.wait_ge(rows_cleared, 1)
            for tile, parts in enumerate(VEC_ROWS):
                at = 0
                for name, first, n in parts:
                    src = a[name]
                    src = src.rearrange("a b (c p) -> (a b c) p" if len(src.shape) == 3 else "a (c p) -> (a c) p", p=P)
                    act.dma_start(rows[at:at + n, tile, :], src[first:first + n, :]).then_inc(consts_loaded, 16)
                    at += n
            act.dma_start(router_w[:, :, :], a["router_w"].rearrange("(k p) n -> p k n", p=P)).then_inc(
                inputs_loaded, 16)
            act.dma_start(router_b[:, :], a["router_bias"].partition_broadcast(P)).then_inc(inputs_loaded, 16)
            act.dma_start(b_pw2, a["a_b_pw2"]).then_inc(inputs_loaded, 16)
            act.dma_start(x_nat[:, 1:3, :], a["x"][0].rearrange("(t p) n -> p t n", p=P)).then_inc(inputs_loaded, 16)
            for n, name in enumerate(("ssd_dt_bias_2", "ssd_a_log_2", "ssd_d_2")):
                act.dma_start(ssd_rows[:, n, :], a[name][0].partition_broadcast(P)).then_inc(inputs_loaded, 16)
            act.dma_start(w_dt[:, :, :], a["w_in_2"][0][:, OFF_DT:OFF_Q].rearrange("(k p) n -> p k n", p=P),
                          ).then_inc(inputs_loaded, 16)
            act.dma_start(x_nat[0:META, 0, :], a["meta_tokens_2"]).then_inc(inputs_loaded, 16)
            act.dma_start(lam_rows[:, :, :], a["b_lambda"][0].partition_broadcast(P)).then_inc(inputs_loaded, 16)
            act.dma_start(subln_rows[:, :], a["b_subln_g"][0].partition_broadcast(P)).then_inc(inputs_loaded, 16)
            act.dma_start(rel_w[:, :], a["rel_bias"]).then_inc(inputs_loaded, 16)
            act.dma_start(buckets, a["buckets"]).then_inc(inputs_loaded, 16)
            load_norm(0, a["ln_mix_g"][0], a["ln_mix_b"][0])
            job_ready(act, FJ["vec"])
            act.activation(vec[:, :], bank(FJ["vec"]), ACT.Copy).then_inc(bank_free[FJ["vec"] % BANKS], 1)
            job_ready(act, FJ["relb"])
            act.activation(by_distance[:, 0:SEQ], bank(FJ["relb"])[0:HEADS, 0:SEQ], ACT.Copy).then_inc(
                bank_free[FJ["relb"] % BANKS], 1)
            act.wait_ge(bank_free[FJ["relb"] % BANKS], 1)
            act.dma_start(rel_scratch, by_distance).then_inc(rel_written, 16)
            transposes_out(FJ["conv_xT"], (1, 2), xT)

        @block.tensor
        def _(pe):
            pe.wait_ge(consts_made, 1)
            pe.wait_ge(consts_loaded, 16 * sum(len(r) for r in VEC_ROWS))
            take_bank(FJ["vec"])
            for tile in range(4):
                last = pe.transpose(bank(FJ["vec"])[:, tile * P:tile * P + P], rows[:, tile, :], ident[:, :])
            last.then_inc(job_done, 1)
            pe.wait_ge(inputs_loaded, INPUT_DMAS * 16)
            take_bank(FJ["relb"])
            products(bank(FJ["relb"])[0:HEADS, 0:3 * P], [(rel_w[:, :], buckets)]).then_inc(job_done, 1)
            transposes_pe(FJ["conv_xT"], (1, 2), lambda t: x_nat[:, t, :])

    PAD = TAPS - 1
    glu = carve(0, KC, PAD + SEQ)
    conv = carve(2400, KC, SEQ)
    squares = carve(4500, KC, SEQ)
    sig = carve(6600, 2, SEQ)
    mean_b, rstd_b = carve(7200, SEQ), carve(7500, SEQ)
    sig_ready, glu_ready, conv_step = sem("sig_ready"), sem("glu_ready"), sem("conv_step")
    conv_ready, centred, squared, conv_normed, act_ready = (
        sem("conv_ready"), sem("centred"), sem("squared"), sem("conv_normed"), sem("conv_activated"))

    @stage
    def conformer():
        root = next_sqrt()

        @block.tensor
        def _(pe):
            for n in range(KC):
                j, pair = FJ["glu"] + n, n // 4
                take_bank(j)
                for side in range(2):
                    u = 2 * pair + side
                    unit_ready(u)
                    last = products(bank(j)[:, side * SEQ:side * SEQ + SEQ],
                                    [(slot_k(u)[:, k, (n % 4) * P:(n % 4) * P + P], xT[:, k, META:L])
                                     for k in range(KC)])
                last.then_inc(job_done, 1)
            j = FJ["conv_mean"]
            take_bank(j)
            pe.wait_ge(conv_ready, 1)
            products(bank(j)[:, 0:SEQ], [(ones[:, :], conv[:, c, :]) for c in range(KC)]).then_inc(job_done, 1)
            j = FJ["conv_var"]
            take_bank(j)
            pe.wait_ge(squared, 1)
            products(bank(j)[:, 0:SEQ], [(ones[:, :], squares[:, c, :]) for c in range(KC)]).then_inc(job_done, 1)
            pe.wait_ge(act_ready, KC)
            j = FJ["pw2"]
            for half in range(2):
                unit_ready(unit_at["pw2"] + half)
                for t in (0, 1):
                    take_bank(j)
                    pairs = [(conv[:, k, t * P:t * P + P], slot_k(unit_at["pw2"] + half)[:, k, :]) for k in range(KC)]
                    pairs.append((ones[0:1, :], b_pw2[:, half * 512:half * 512 + 512]))
                    products(bank(j), pairs).then_inc(job_done, 1)
                    j += 1

        @block.scalar
        def _(act):
            for n in range(KC):
                j = FJ["glu"] + n
                job_ready(act, j)
                if n >= 2:
                    act.wait_ge(glu_ready, n - 1)
                act.activation(sig[:, n % 2, :], bank(j)[:, SEQ:2 * SEQ], ACT.Sigmoid,
                               bias=column("a_b_pw1", KC + n)).then_inc(sig_ready, 1)
            act.wait_ge(centred, 1)
            act.activation(squares[:, :, :], conv[:, :, :], ACT.Square).then_inc(squared, 1)
            sqrt_of(act, rstd_b, 1.0 / D, LN_EPS, root)
            act.wait_ge(conv_normed, 1)
            for c in range(KC):
                act.activation(conv[:, c, :], conv[:, c, :], ACT.Silu, bias=column("a_ln_b", c),
                               scale=column("a_ln_g", c)).then_inc(act_ready, 1)

        @block.vector
        def _(dve):
            dve_step(dve.memset(glu[:, :, 0:PAD], 0.0))
            for n in range(KC):
                j = FJ["glu"] + n
                dve.wait_ge(sig_ready, n + 1)
                dve.scalar_tensor_tensor(glu[:, n, PAD:PAD + SEQ], bank(j)[:, 0:SEQ], column("a_b_pw1", n),
                                         sig[:, n % 2, :], ALU.add, ALU.mult).then_inc(glu_ready, 1)
                dve.wait_ge(glu_ready, n + 1)
                dve.nop().then_inc(bank_free[j % BANKS], 1)
            for tap in range(TAPS):
                for c in range(KC):
                    n = tap * KC + c
                    src = glu[:, c, tap:tap + SEQ]
                    w = column("a_w_dw", tap * KC + c)
                    if tap == 0:
                        ins = dve.tensor_scalar(conv[:, c, :], src, w, column("a_b_dw", c), ALU.mult, ALU.add)
                    else:
                        dve.wait_ge(conv_step, n - KC + 1)
                        ins = dve.scalar_tensor_tensor(conv[:, c, :], src, w, conv[:, c, :], ALU.mult, ALU.add)
                    ins.then_inc(conv_step, 1)
            dve.wait_ge(conv_step, TAPS * KC)
            dve.nop().then_inc(conv_ready, 1)
            j = FJ["conv_mean"]
            job_ready(dve, j)
            ins = dve.tensor_scalar(mean_b, bank(j)[:, 0:SEQ], 1.0 / D, None, ALU.mult)
            dve_step(ins)
            dve.nop().then_inc(bank_free[j % BANKS], 1)
            dve.tensor_tensor(conv[:, :, :], conv[:, :, :], mean_b.unsqueeze(1).broadcast_to([P, KC, SEQ]),
                              ALU.subtract).then_inc(centred, 1)
            j = FJ["conv_var"]
            job_ready(dve, j)
            dve.tensor_copy(rstd_b, bank(j)[:, 0:SEQ]).then_inc(var_ready, 1)
            reciprocal_of(dve, rstd_b, root)
            dve.nop().then_inc(bank_free[j % BANKS], 1)
            dve.tensor_tensor(conv[:, :, :], conv[:, :, :], rstd_b.unsqueeze(1).broadcast_to([P, KC, SEQ]),
                              ALU.mult).then_inc(conv_normed, 1)
            add_residual(FJ["pw2"])

    normed = [sem(f"normed{k}") for k in range(4)]

    @stage
    def mix_norm0():
        layer_norm(0, "mix0_xT", normed[0])

    aff, sel = carve(0, 2, EXPERTS), carve(40, 2, EXPERTS)
    beats = carve(80, 2, EXPERTS)
    cmp = carve(120, 2, GROUPS)
    group_score, group_lost = carve(140, 2, GROUPS), carve(150, 2, GROUPS)
    total = carve(160, 2)
    gate_cell = carve(170, 4)
    silu_g = carve(200, 2, DE)
    hid = carve(1300, 2, DE)
    hidT = carve(2400, 2, DE)
    zeros = carve(3500, 512)

    def moe_stage(layer):
        route_aff, routed = sem(f"route_aff{layer}"), sem(f"routed{layer}")
        silu_ready, hid_ready, hidT_ready = (sem(f"silu_ready{layer}"), sem(f"hid_ready{layer}"),
                                             sem(f"hidT_ready{layer}"))
        cell_ready, zeroed, acc_ready = sem(f"cell_ready{layer}"), sem(f"zeroed{layer}"), sem(f"moe_sum{layer}")
        B = FJ[f"moe{layer}"]
        U = unit_at[f"moe{layer}"]
        STEPS = 2 * EXPERTS

        def job_g(s):
            return B + (3 * s - 1 if s else 0)

        def job_u(s):
            return B + (3 * s + 1 if s else 1)

        def job_t(s):
            return B + 3 * s + 3 if s < STEPS - 1 else B + 3 * STEPS - 1

        def over_pairs(eng, step):
            for s in range(4):
                step(s, 0)
            with eng.Fori(0, EXPERTS // 2 - 1) as i:
                for s in range(4, 8):
                    step(s, i)

        @block.scalar
        def _(act):
            j = FJ[f"route{layer}"]
            job_ready(act, j)
            act.activation(aff[:, :, :], bank(j)[:, 0:2 * EXPERTS].rearrange("p (t e) -> p t e", t=2),
                           ACT.Sigmoid).then_inc(route_aff, 1)

            def turned(s, i):
                act.wait_ge(job_done, job_t(s) + 1 + i * 12)
                if s >= 2:
                    act.wait_ge(down_done[layer], s - 1 + i * 4)
                act.activation(hidT[:, s % 2, :], bank(job_t(s)), ACT.Copy).then_inc(hidT_ready, 1)

            def step(s, i):
                act.wait_ge(job_done, job_g(s) + 1 + i * 12)
                if s >= 2:
                    act.wait_ge(hid_ready, s - 1 + i * 4)
                act.activation(silu_g[:, s % 2, :], bank(job_g(s)), ACT.Silu).then_inc(silu_ready, 1)
                if s >= 1:
                    turned(s - 1, i)

            over_pairs(act, step)
            turned(STEPS - 1, 0)

        @block.vector
        def _(dve):
            dve.memset(zeros, 0.0).then_inc(zeroed, 1)
            if layer == 0:
                dve.wait_ge(inputs_loaded, INPUT_DMAS * 16)
            dve.wait_ge(route_aff, 1)
            dve_step(dve.tensor_tensor(sel, aff, router_b[:, :].unsqueeze(1).broadcast_to([P, 2, EXPERTS]),
                                       ALU.add))
            j = FJ[f"route{layer}"]
            dve.nop().then_inc(bank_free[j % BANKS], 1)
            dve_step(dve.memset(beats, 0.0))
            sg = sel.rearrange("p t (g e) -> p t g e", g=GROUPS)
            bg = beats.rearrange("p t (g e) -> p t g e", g=GROUPS)
            first = True
            for hi in range(PER_GROUP):
                for lo in range(hi):
                    dve_step(dve.tensor_tensor(cmp, sg[:, :, :, lo], sg[:, :, :, hi], ALU.is_ge))
                    dve_step(dve.tensor_tensor(bg[:, :, :, hi], bg[:, :, :, hi], cmp, ALU.add))
                    dve_step(dve.scalar_tensor_tensor(bg[:, :, :, lo], bg[:, :, :, lo], 1.0, cmp, ALU.add,
                                                      ALU.subtract))
                    if first:
                        dve_step(dve.tensor_tensor(group_score, sg[:, :, :, lo], sg[:, :, :, hi], ALU.add))
                        first = False
                    else:
                        dve_step(dve.tensor_tensor(cmp, sg[:, :, :, lo], sg[:, :, :, hi], ALU.add))
                        dve_step(dve.tensor_tensor(group_score, group_score, cmp, ALU.max))
            dve_step(dve.memset(group_lost, 0.0))
            for hi in range(GROUPS):
                for lo in range(hi):
                    s_lo, s_hi = group_score[:, :, lo:lo + 1], group_score[:, :, hi:hi + 1]
                    c1 = cmp[:, :, 0:1]
                    dve_step(dve.tensor_tensor(c1, s_lo, s_hi, ALU.is_ge))
                    dve_step(dve.tensor_tensor(group_lost[:, :, hi:hi + 1], group_lost[:, :, hi:hi + 1], c1, ALU.add))
                    dve_step(dve.scalar_tensor_tensor(group_lost[:, :, lo:lo + 1], group_lost[:, :, lo:lo + 1], 1.0,
                                                      c1, ALU.add, ALU.subtract))
            dve_step(dve.tensor_scalar(group_lost, group_lost, 0.5, None, ALU.is_lt))
            dve_step(dve.tensor_scalar(beats, beats, 1.5, None, ALU.is_lt))
            dve_step(dve.tensor_tensor(bg, bg, group_lost.unsqueeze(3).broadcast_to([P, 2, GROUPS, PER_GROUP]),
                                       ALU.mult))
            dve_step(dve.tensor_tensor(gates[:, :, :], beats, aff, ALU.mult))
            dve_step(dve.tensor_reduce(total, gates[:, :, :], AX_X, ALU.add))
            dve_step(dve.reciprocal(total, total))
            dve_step(dve.tensor_tensor(gates[:, :, :], gates[:, :, :],
                                       total.unsqueeze(2).broadcast_to([P, 2, EXPERTS]), ALU.mult))

            def step(s, i):
                e = s // 2 if isinstance(i, int) else None
                src = gates[:, s % 2, e:e + 1] if e is not None else gates[:, s % 2, bass.ds(i * 2 + s // 2, 1)]
                dve.tensor_copy(gate_cell[:, s % 4:s % 4 + 1], src).then_inc(cell_ready, 1)
                dve.wait_ge(silu_ready, s + 1 + i * 4)
                dve.wait_ge(job_done, job_u(s) + 1 + i * 12)
                dve.wait_ge(cell_ready, s + 1 + i * 4)
                if s >= 2:
                    dve.wait_ge(job_done, job_t(s - 2) + 1 + i * 12)
                dve.scalar_tensor_tensor(hid[:, s % 2, :], bank(job_u(s)), gate_cell[:, s % 4:s % 4 + 1],
                                         silu_g[:, s % 2, :], ALU.mult, ALU.mult).then_inc(hid_ready, 1)

            over_pairs(dve, step)
            dve.wait_ge(acc_ready, 1)
            for t in (1, 2):
                for half in range(2):
                    xs = x_nat[:, t, half * 512:half * 512 + 512]
                    ins = dve.scalar_tensor_tensor(xs, xs, ALPHA, psum[:, BANKS + 2 * (t - 1) + half, :],
                                                   ALU.mult, ALU.add)

        def freed(pe, s, i, what):
            pass

        @block.tensor
        def _(pe):
            j = FJ[f"route{layer}"]
            take_bank(j)
            for t in (1, 2):
                at = TILE_AT[t]
                last = products(bank(j)[:, (t - 1) * EXPERTS:t * EXPERTS],
                                [(xT[:, k, at:at + P], router_w[:, k, :]) for k in range(KC)])
            last.then_inc(job_done, 1)
            pe.wait_ge(zeroed, 1)
            for b in range(BANKS, 8):
                pe.matmul(psum[:, b, :], zeros[:, 0:P], zeros, start=True, stop=True)

            def wait_unit(u, i):
                pe.wait_ge(slot_loaded[u % RING], 16 * (u // RING + 1) + i * 16)

            def consumed(s, i, what):
                if what == "g" and s >= 2:
                    pe.wait_ge(hid_ready, s - 1 + i * 4)
                if what == "t" and s >= 2:
                    pe.wait_ge(silu_ready, s + i * 4)
                if what == "u" and s >= 2:
                    pe.wait_ge(hidT_ready, s - 1 + i * 4)

            def down(s, i, s_unit):
                u = U + 3 * (s_unit // 2) + 2
                if s_unit % 2 == 0:
                    wait_unit(u, i)
                pe.wait_ge(hidT_ready, s + 1 + i * 4)
                for half in range(2):
                    for k in range(DE // P):
                        last = pe.matmul(psum[:, BANKS + 2 * (s % 2) + half, :], hidT[:, s % 2, k * P:k * P + P],
                                         slot_k(u, D)[:, k, half * 512:half * 512 + 512], start=False, stop=True,
                                         skip_group_check=True)
                last.then_inc(down_done[layer], 1)

            def turn(s, i):
                pe.wait_ge(hid_ready, s + 1 + i * 4)
                for k in range(DE // P):
                    last = pe.transpose(bank(job_t(s))[:, k * P:k * P + P], hid[:, s % 2, k * P:k * P + P],
                                        ident[:, :])
                last.then_inc(job_done, 1)

            def step(s, i):
                t, u = s % 2, U + 3 * (s // 2)
                at = TILE_AT[t + 1]
                consumed(s, i, "g")
                if t == 0:
                    wait_unit(u, i)
                products(bank(job_g(s)), [(xT[:, k, at:at + P], slot_k(u)[:, k, :]) for k in range(KC)]).then_inc(
                    job_done, 1)
                if s >= 1:
                    consumed(s, i, "t")
                    turn(s - 1, i)
                consumed(s, i, "u")
                if t == 0:
                    wait_unit(u + 1, i)
                products(bank(job_u(s)), [(xT[:, k, at:at + P], slot_k(u + 1)[:, k, :]) for k in range(KC)]).then_inc(
                    job_done, 1)
                if s >= 1:
                    down(s - 1, i, s - 1)

            for b in range(BANKS):
                n = (B - 1 - b) // BANKS + 1 if B > b else 0
                if n > 0:
                    pe.wait_ge(bank_free[b], n)
            over_pairs(pe, step)
            s = STEPS - 1
            turn(s, 0)
            down(s, 0, s)
            pe.wait_ge(hidT_ready, STEPS)
            for b in range(BANKS):
                n = sum(1 for j in range(B, B + 96) if j % BANKS == b)
                pe.nop().then_inc(bank_free[b], n)
            pe.matmul(psum[:, 7, :], zeros[:, 0:P], zeros, start=False, stop=True,
                      skip_group_check=True).then_inc(acc_ready, 1)

    @stage
    def moe0():
        moe_stage(0)

    @stage
    def ffn_norm0():
        layer_norm(1, "ffn0_xT", normed[1])

    kT, qT = carve(0, KC, SEQ), carve(2048, KC, SEQ)
    v_nat = carve(4096, 2, D)
    bias = carve(6144, HEADS, SEQ)
    o_nat = carve(8192, 2, D)
    oT = carve(10240, KC, L)
    probs, mixed, mixedT = carve(12416, 2, 2, SEQ), carve(13440, 2, SEQ), carve(13952, 2, SEQ)
    neg_lam = small[:, 8:9]
    bias_loaded = sem("bias_loaded")
    lam_summed, lam_exp = sem("lam_summed"), sem("lam_exp")
    max_ready, probs_ready, mixed_ready, mixedT_ready, o_ready = (
        sem("max_ready"), sem("probs_ready"), sem("mixed_ready"), sem("mixedT_ready"), sem("o_ready"))
    o_squared, o_summed, o_normed = sem("o_squared"), sem("o_summed"), sem("o_normed")
    PAIRS = 2 * HEADS

    def att_jobs():
        order = {}
        for n in range(PAIRS + 2):
            for kind, m in (("scores", n), ("turn", n - 1), ("values", n - 2)):
                if 0 <= m < PAIRS:
                    order[kind, m] = FJ["att_heads"] + len(order)
        return order

    AJ = att_jobs()

    @stage
    def attention():
        root = next_sqrt()

        @block.tensor
        def _(pe):
            def channels(first, u0, src):
                for c in range(KC):
                    j = first + c
                    if c % 4 == 0:
                        unit_ready(u0 + c // 4)
                    take_bank(j)
                    products(bank(j)[:, 0:SEQ], [(slot_k(u0 + c // 4)[:, k, (c % 4) * P:(c % 4) * P + P],
                                                  src[:, k, META:L]) for k in range(KC)]).then_inc(job_done, 1)

            channels(FJ["att_k"], unit_at["w_k"], xT)
            project_natural(FJ["att_v"], unit_at["w_v"], xT, (1, 2), KC)
            channels(FJ["att_q"], unit_at["w_q"], xT)
            pe.wait_ge(bias_loaded, 16)
            all_read_out(pe, FJ["att_heads"])

            def scores(n):
                b, h = n // HEADS, n % HEADS
                keys = P * (b + 1)
                j = AJ["scores", n]
                take_bank(j)
                rows = slice(HD * (h % 2), HD * (h % 2) + HD)
                for comp in range(2):
                    c = 4 * comp + h // 2
                    pe.matmul(bank(j)[:, comp * SEQ:comp * SEQ + keys], flip[:, :], bias[:, h, SEQ - keys:SEQ],
                              start=True, stop=False)
                    last = pe.matmul(bank(j)[:, comp * SEQ:comp * SEQ + keys], qT[rows, c, b * P:b * P + P],
                                     kT[rows, c, 0:keys], start=False, stop=True)
                last.then_inc(job_done, 1)

            def turn(n):
                b = n // HEADS
                j = AJ["turn", n]
                take_bank(j)
                pe.wait_ge(mixed_ready, n + 1)
                for kb in range(b + 1):
                    last = pe.transpose(bank(j)[:, kb * P:kb * P + P], mixed[:, n % 2, kb * P:kb * P + P], ident[:, :])
                last.then_inc(job_done, 1)

            def values(n):
                b, h = n // HEADS, n % HEADS
                j = AJ["values", n]
                take_bank(j)
                pe.wait_ge(mixedT_ready, n + 1)
                products(bank(j)[:, 0:P], [(mixedT[:, n % 2, kb * P:kb * P + P], v_nat[:, kb, h * P:h * P + P])
                                           for kb in range(b + 1)]).then_inc(job_done, 1)

            for n in range(PAIRS + 2):
                if n < PAIRS:
                    scores(n)
                if 1 <= n <= PAIRS:
                    turn(n - 1)
                if n >= 2:
                    values(n - 2)
            pe.wait_ge(o_normed, 1)
            transposes_pe(FJ["att_T"], (1, 2), lambda t: o_nat[:, t - 1, :])
            all_read_out(pe, FJ["att_o"])
            project_natural(FJ["att_o"], unit_at["w_o"], oT, (1, 2), KC)

        @block.scalar
        def _(act):
            act.wait_ge(rel_written, 16)
            skewed = bass.AP(rel_scratch.tensor, 0, [[1, P], [3 * P, HEADS], [1, SEQ]])
            act.dma_start(bias, skewed).then_inc(bias_loaded, 16)
            for first, dst, scale in ((FJ["att_k"], kT, 1.0), (FJ["att_q"], qT, HD ** -0.5)):
                for c in range(KC):
                    j = first + c
                    job_ready(act, j)
                    act.activation(dst[:, c, :], bank(j)[:, 0:SEQ], ACT.Copy, scale=scale).then_inc(
                        bank_free[j % BANKS], 1)
            act.wait_ge(lam_summed, 1)
            act.activation(small[:, 10:12], small[:, 10:12], ACT.Exp).then_inc(lam_exp, 1)

            def exponentials(n):
                keys = P * (n // HEADS + 1)
                j = AJ["scores", n]
                act.wait_ge(max_ready, n + 1)
                if n >= 2:
                    act.wait_ge(mixed_ready, n - 1)
                for comp in range(2):
                    m = 16 + 4 * (n % 2) + comp
                    last = act.activation(probs[:, n % 2, comp, 0:keys], bank(j)[:, comp * SEQ:comp * SEQ + keys],
                                          ACT.Exp, bias=small[:, m:m + 1], accum_out=small[:, m + 2:m + 3])
                last.then_inc(probs_ready, 1)
                act.wait_ge(probs_ready, n + 1)
                act.nop().then_inc(bank_free[j % BANKS], 1)

            def turned(n):
                keys = P * (n // HEADS + 1)
                j = AJ["turn", n]
                job_ready(act, j)
                if n >= 2:
                    job_ready(act, AJ["values", n - 2])
                act.activation(mixedT[:, n % 2, 0:keys], bank(j)[:, 0:keys], ACT.Copy).then_inc(mixedT_ready, 1)
                act.wait_ge(mixedT_ready, n + 1)
                act.nop().then_inc(bank_free[j % BANKS], 1)

            for n in range(PAIRS + 1):
                if n < PAIRS:
                    exponentials(n)
                if n >= 1:
                    turned(n - 1)
            act.wait_ge(o_ready, PAIRS)
            act.activation(oT_flat, o_nat_flat, ACT.Square).then_inc(o_squared, 1)
            sqrt_of(act, small[:, 32:48], 1.0 / (2 * HD), LN_EPS, root)
            transposes_out(FJ["att_T"], (1, 2), oT)

        @block.vector
        def _(dve):
            pairs = lam_rows[:, :, :].rearrange("p (a b) d -> p a b d", b=2)
            dve_step(dve.tensor_tensor(lam_rows[:, 0:2, :], pairs[:, :, 0, :], pairs[:, :, 1, :], ALU.mult))
            dve.tensor_reduce(small[:, 10:12], lam_rows[:, 0:2, :], AX_X, ALU.add).then_inc(lam_summed, 1)
            for half in range(2):
                for t in range(2):
                    j = FJ["att_v"] + 2 * half + t
                    job_ready(dve, j)
                    dve.tensor_copy(v_nat[:, t, half * 512:half * 512 + 512], bank(j)).then_inc(
                        bank_free[j % BANKS], 1)
            dve.wait_ge(lam_exp, 1)
            dve_step(dve.tensor_tensor(neg_lam, small[:, 11:12], small[:, 10:11], ALU.subtract))
            dve_step(dve.tensor_scalar(neg_lam, neg_lam, -LAMBDA_INIT, None, ALU.add))

            def row_max(n):
                keys = P * (n // HEADS + 1)
                j = AJ["scores", n]
                job_ready(dve, j)
                m = 16 + 4 * (n % 2)
                src = bank(j).rearrange("p (c k) -> p c k", c=2)[:, :, 0:keys]
                dve_step(dve.tensor_reduce(small[:, m:m + 2], src, AX_X, ALU.max))
                dve.tensor_scalar(small[:, m:m + 2], small[:, m:m + 2], -1.0, None, ALU.mult).then_inc(max_ready, 1)

            def combine(n):
                keys = P * (n // HEADS + 1)
                m = 16 + 4 * (n % 2) + 2
                dve.wait_ge(probs_ready, n + 1)
                dve_step(dve.reciprocal(small[:, m:m + 2], small[:, m:m + 2]))
                dve_step(dve.tensor_scalar(small[:, m + 1:m + 2], small[:, m + 1:m + 2], neg_lam, None, ALU.mult))
                if n >= 2:
                    job_ready(dve, AJ["turn", n - 2])
                dve_step(dve.tensor_scalar(mixed[:, n % 2, 0:keys], probs[:, n % 2, 0, 0:keys], small[:, m:m + 1],
                                           None, ALU.mult))
                dve.scalar_tensor_tensor(mixed[:, n % 2, 0:keys], probs[:, n % 2, 1, 0:keys],
                                         small[:, m + 1:m + 2], mixed[:, n % 2, 0:keys], ALU.mult,
                                         ALU.add).then_inc(mixed_ready, 1)

            def values_out(n):
                b, h = n // HEADS, n % HEADS
                j = AJ["values", n]
                job_ready(dve, j)
                dve.tensor_copy(o_nat[:, b, h * P:h * P + P], bank(j)[:, 0:P]).then_inc(o_ready, 1)
                dve.wait_ge(o_ready, n + 1)
                dve.nop().then_inc(bank_free[j % BANKS], 1)

            for n in range(PAIRS + 2):
                if n < PAIRS:
                    row_max(n)
                if 1 <= n <= PAIRS:
                    combine(n - 1)
                if n >= 2:
                    values_out(n - 2)
            dve.wait_ge(o_squared, 1)
            dve.tensor_reduce(small[:, 32:48], oT_flat.rearrange("p (h d) -> p h d", d=P), AX_X,
                              ALU.add).then_inc(var_ready, 1)
            reciprocal_of(dve, small[:, 32:48], root)
            heads_of = o_nat_flat.rearrange("p (h d) -> p h d", d=P)
            dve_step(dve.tensor_tensor(heads_of, heads_of, small[:, 32:48].unsqueeze(2).broadcast_to([P, 16, P]),
                                       ALU.mult))
            dve.scalar_tensor_tensor(heads_of, heads_of, 1.0 - LAMBDA_INIT,
                                     subln_rows[:, :].unsqueeze(1).broadcast_to([P, 16, P]), ALU.mult,
                                     ALU.mult).then_inc(o_normed, 1)
            add_residual(FJ["att_o"])

    o_nat_flat, oT_flat = arena[:, 8192:10240], arena[:, 10240:12288]

    @stage
    def mix_norm1():
        layer_norm(2, "mix1_xT", normed[2])

    @stage
    def moe1():
        moe_stage(1)

    @stage
    def ffn_norm1():
        layer_norm(3, "ffn1_xT", normed[3], last=True)

    ALL = (0, 1, 2)

    def rms(name, tiles, src, dst, scaled, root):
        lo, hi = 48 + tiles[0], 48 + tiles[-1] + 1
        cleared, summed = sem(f"{name}_cleared"), sem(f"{name}_summed")

        @block.scalar
        def _(act):
            act.wait_ge(cleared, 1)
            for t in tiles:
                n = TILE_N[t]
                act_last = act.activation(dst(t)[0:n], src(t)[0:n], ACT.Square,
                                          accum_out=small[0:n, 48 + t:49 + t])
            act_last.then_inc(summed, 1)
            act.wait_ge(summed, 1)
            act.activation(small[:, lo:hi], small[:, lo:hi], ACT.Sqrt, bias=eps_cols[:, 1:2],
                           scale=1.0 / D).then_inc(std_ready, 1)

        @block.vector
        def _(dve):
            dve.memset(small[:, lo:hi], 1.0).then_inc(cleared, 1)
            reciprocal_of(dve, small[:, lo:hi], root)
            for t in tiles:
                n = TILE_N[t]
                dve.tensor_scalar(dst(t)[0:n], src(t)[0:n], small[0:n, 48 + t:49 + t], None,
                                  ALU.mult).then_inc(scaled, 1)

    def rms_to_T(name, job_name, src, dst, dstT, gain):
        scaled = sem(f"{name}_scaled")
        tmp = dst
        rms(name, ALL, src, tmp, scaled, next_sqrt())
        block.tensor(lambda pe: transposes_pe(FJ[job_name], ALL, dst, lambda t: pe.wait_ge(scaled, t + 1)))
        block.scalar(lambda act: transposes_out(FJ[job_name], ALL, dstT, gain))

    xn = carve(0, 3, D)

    @stage
    def pre_norm():
        rms_to_T("pre", "pre_xT", lambda t: x_nat[:, t, :], lambda t: xn[:, t, :], xT, "mix_pre_g_2")

    zs = carve(0, 3, D)
    xbcT = carve(3072, XC, L)
    XPAD = SSD_TAPS - 1
    xraw = carve(6336, XC, XPAD + L)
    in_ready, xconv_step, dt_pos, dt_exp, dt_one, dt_ln, a_exp = (
        sem("xbc_in"), sem("xconv_step"), sem("dt_neg_abs"), sem("dt_exp"), sem("dt_one"), sem("dt_ln"), sem("a_exp"))
    xpad_ready = sem("xpad_ready")
    dt_v, dt_m, dt_e, dt_w, dt_l, dt_r, dt, adt = (dts[:, n, :] for n in range(8))
    dt_d = dts[:, 8, :]

    def by_tile(x):
        return x.rearrange("p (t h) -> p t h", t=3)

    @stage
    def inner():
        @block.tensor
        def _(pe):
            project_natural(FJ["z"], unit_at["w_z"], xT, ALL, KC)
            for c in range(XC):
                j, u = FJ["xbc"] + c, unit_at["w_xbc"] + c // 4
                unit_ready(u)
                take_bank(j)
                products(bank(j)[:, 0:L], [(slot_k(u)[:, k, (c % 4) * P:(c % 4) * P + P], xT[:, k, :])
                                           for k in range(KC)]).then_inc(job_done, 1)
            j = FJ["dt"]
            take_bank(j)
            for t in ALL:
                n, at = TILE_N[t], TILE_AT[t]
                last = products(bank(j)[0:n, t * SSD_HEADS:(t + 1) * SSD_HEADS],
                                [(xT[:, k, at:at + n], w_dt[:, k, :]) for k in range(KC)])
            last.then_inc(job_done, 1)

        @block.scalar
        def _(act):
            j = FJ["z"]
            for half in range(2):
                for t in ALL:
                    n = TILE_N[t]
                    job_ready(act, j)
                    act.activation(zs[0:n, t, half * 512:half * 512 + 512], bank(j)[0:n, :], ACT.Silu).then_inc(
                        bank_free[j % BANKS], 1)
                    j += 1
            act.wait_ge(xpad_ready, 1)
            for c in range(XC):
                j = FJ["xbc"] + c
                job_ready(act, j)
                act.activation(xraw[:, c, XPAD:XPAD + L], bank(j)[:, 0:L], ACT.Copy).then_inc(in_ready, 1)
                act.wait_ge(in_ready, c + 1)
                act.nop().then_inc(bank_free[j % BANKS], 1)
            for c in range(XC):
                act.wait_ge(xconv_step, (SSD_TAPS - 1) * 4 + c % 4 + 1 + (c // 4) * 4 * SSD_TAPS)
                act.activation(xbcT[:, c, :], xbcT[:, c, :], ACT.Silu, bias=column("ssd_conv_b_2", c))
            act.wait_ge(dt_pos, 1)
            act.activation(dt_e, dt_e, ACT.Exp).then_inc(dt_exp, 1)
            act.activation(ssd_rows[:, 1, :], ssd_rows[:, 1, :], ACT.Exp).then_inc(a_exp, 1)
            act.wait_ge(dt_one, 1)
            act.activation(dt_l, dt_w, ACT.Ln).then_inc(dt_ln, 1)

        @block.vector
        def _(dve):
            dve.memset(xraw[:, :, 0:XPAD], 0.0).then_inc(xpad_ready, 1)
            dve_step(dve.memset(dts[:, :, :], 0.0))
            n = 0
            for quad in range(XC // 4):
                for tap in range(SSD_TAPS):
                    for c in range(4 * quad, 4 * quad + 4):
                        src = xraw[:, c, tap:tap + L]
                        w = column("ssd_conv_w_2", tap * XC + c)
                        if tap == 0:
                            dve.wait_ge(in_ready, c + 1)
                            ins = dve.tensor_scalar(xbcT[:, c, :], src, w, None, ALU.mult)
                        else:
                            dve.wait_ge(xconv_step, n - 3)
                            ins = dve.scalar_tensor_tensor(xbcT[:, c, :], src, w, xbcT[:, c, :], ALU.mult, ALU.add)
                        ins.then_inc(xconv_step, 1)
                        n += 1
            j = FJ["dt"]
            job_ready(dve, j)
            dve.tensor_copy(by_tile(dt_v)[0:META, 0, :], bank(j)[0:META, 0:SSD_HEADS])
            dve_step(dve.tensor_copy(dt_v[:, SSD_HEADS:], bank(j)[:, SSD_HEADS:3 * SSD_HEADS]))
            dve.nop().then_inc(bank_free[j % BANKS], 1)
            dve_step(dve.tensor_tensor(by_tile(dt_v), by_tile(dt_v),
                                       ssd_rows[:, 0, :].unsqueeze(1).broadcast_to([P, 3, SSD_HEADS]), ALU.add))
            dve_step(dve.tensor_scalar(dt_m, dt_v, 0.0, None, ALU.max))
            dve.scalar_tensor_tensor(dt_e, dt_m, -2.0, dt_v, ALU.mult, ALU.add).then_inc(dt_pos, 1)
            dve.wait_ge(dt_exp, 1)
            dve.tensor_scalar(dt_w, dt_e, 1.0, None, ALU.add).then_inc(dt_one, 1)
            dve.wait_ge(dt_one, 1)
            dve_step(dve.tensor_scalar(dt_d, dt_w, -1.0, 1e-30, ALU.add, ALU.max))
            dve_step(dve.reciprocal(dt_d, dt_d))
            dve.wait_ge(dt_ln, 1)
            dve_step(dve.tensor_tensor(dt_r, dt_l, dt_d, ALU.mult))
            dve_step(dve.tensor_scalar(dt_w, dt_w, 1.0, None, ALU.is_equal))
            dve_step(dve.tensor_tensor(dt_r, dt_r, dt_w, ALU.add))
            dve_step(dve.tensor_tensor(dt_r, dt_r, dt_e, ALU.mult))
            dve_step(dve.tensor_tensor(dt, dt_m, dt_r, ALU.add))
            dve.wait_ge(a_exp, 1)
            dve_step(dve.tensor_scalar(dt_v, dt, -1.0, None, ALU.mult))
            dve_step(dve.tensor_tensor(by_tile(adt), by_tile(dt_v),
                                       ssd_rows[:, 1, :].unsqueeze(1).broadcast_to([P, 3, SSD_HEADS]), ALU.mult))

    xs, xdt, xd = carve(6336, D), carve(6336 + D, D), carve(6336 + 2 * D, D)
    decay = carve(9636, SSD_HEADS, P)
    steps = carve(11684, 2, 4, P)
    cb = carve(12708, SSD_GROUPS, P)
    b_nat = carve(12964, SSD_GROUPS, STATE)
    state = carve(13220, D)
    y_tmp = carve(14244, D)
    yT = carve(14440, KC, L)
    cums = carve(9408, 4, SSD_HEADS)
    PD = SSD_HEADS // SSD_GROUPS
    HG = D // SSD_GROUPS

    def ssd_jobs():
        order = {}
        for c in ALL:
            kinds = ["sums", "cb", "xs0", "xs1", "b", "row0", "row1", "row2", "row3", "diag0", "diag1"]
            kinds += ["off0", "off1"] if c > 0 else []
            kinds += ["state0", "state1"] if c < 2 else []
            for kind in kinds:
                order[kind, c] = FJ["ssd"] + len(order)
        return order

    SJ = ssd_jobs()
    cums_ready, cums_exp, cb_out, cb_masked, xs_ready, b_ready, step_ready, seg_ready, seg_exp, decay_ready = (
        sem("cums_ready"), sem("cums_exp"), sem("cb_out"), sem("cb_masked"), sem("xs_ready"), sem("b_ready"),
        sem("step_ready"), sem("seg_ready"), sem("seg_exp"), sem("decay_ready"))
    xdt_ready, xd_ready, state_ready, y_done = sem("xdt_ready"), sem("xd_ready"), sem("state_ready"), sem("y_done")

    def per_head(x, n, h0=0, nh=SSD_HEADS, width=SSD_HEADS and 64):
        return x.unsqueeze(2).broadcast_to([n, nh, width])

    def heads_of_row(x, n):
        return x[0:n].rearrange("p (h d) -> p h d", d=64)

    @stage
    def ssd():
        @block.tensor
        def _(pe):
            for c in ALL:
                n, at = TILE_N[c], TILE_AT[c]
                a_c = by_tile(adt)[0:n, c, :]
                j = SJ["sums", c]
                take_bank(j)
                products(bank(j)[:, 0:SSD_HEADS], [(ones[0:n, :], a_c)])
                products(bank(j)[0:n, SSD_HEADS:2 * SSD_HEADS], [(upto[0:n, 0:n], a_c)]).then_inc(job_done, 1)
                j = SJ["cb", c]
                take_bank(j)
                for g in range(SSD_GROUPS):
                    last = products(bank(j)[0:n, g * P:g * P + n],
                                    [(xbcT[:, KC + g, at:at + n], xbcT[:, KC + SSD_GROUPS + g, at:at + n])])
                last.then_inc(job_done, 1)
                for half in range(2):
                    j = SJ[f"xs{half}", c]
                    take_bank(j)
                    for k in range(4):
                        last = pe.transpose(bank(j)[0:n, k * P:k * P + P], xbcT[:, 4 * half + k, at:at + n],
                                            ident[:, :])
                    last.then_inc(job_done, 1)
                j = SJ["b", c]
                take_bank(j)
                for g in range(SSD_GROUPS):
                    last = pe.transpose(bank(j)[0:n, g * P:g * P + P], xbcT[:, KC + g, at:at + n], ident[:, :])
                last.then_inc(job_done, 1)
                for q in range(4):
                    j = SJ[f"row{q}", c]
                    take_bank(j)
                    pe.wait_ge(step_ready, 4 * c + q + 1)
                    products(bank(j)[:, 0:4 * n].rearrange("p (h l) -> p h l", h=4),
                             [(ones[0:n, :], steps[0:n, q % 2, :, 0:n])]).then_inc(job_done, 1)
                pe.wait_ge(decay_ready, 4 * c + 4)
                pe.wait_ge(xdt_ready, c + 1)
                for g in range(SSD_GROUPS):
                    j = SJ[f"diag{g}", c]
                    take_bank(j)
                    for h in range(PD):
                        last = products(bank(j)[0:n, h * 64:h * 64 + 64],
                                        [(decay[0:n, PD * g + h, 0:n],
                                          xdt[0:n, g * HG + h * 64:g * HG + h * 64 + 64])])
                    last.then_inc(job_done, 1)
                if c > 0:
                    pe.wait_ge(state_ready, c)
                    for g in range(SSD_GROUPS):
                        j = SJ[f"off{g}", c]
                        take_bank(j)
                        products(bank(j)[0:n, :], [(xbcT[:, KC + SSD_GROUPS + g, at:at + n],
                                                    state[:, g * HG:g * HG + HG])]).then_inc(job_done, 1)
                if c < 2:
                    pe.wait_ge(xd_ready, c + 1)
                    pe.wait_ge(b_ready, c + 1)
                    for g in range(SSD_GROUPS):
                        j = SJ[f"state{g}", c]
                        take_bank(j)
                        products(bank(j), [(b_nat[0:n, g, :], xd[0:n, g * HG:g * HG + HG])]).then_inc(job_done, 1)

        @block.scalar
        def _(act):
            for c in ALL:
                n = TILE_N[c]
                if c:
                    act.wait_ge(y_done, c)
                j = SJ["cb", c]
                job_ready(act, j)
                act.activation(cb[0:n, :, 0:n], bank(j)[0:n, 0:2 * P].rearrange("p (g l) -> p g l", g=2)[:, :, 0:n],
                               ACT.Copy).then_inc(cb_out, 1)
                act.wait_ge(cb_out, c + 1)
                act.nop().then_inc(bank_free[j % BANKS], 1)
                for half in range(2):
                    j = SJ[f"xs{half}", c]
                    job_ready(act, j)
                    act.activation(xs[0:n, half * 512:half * 512 + 512], bank(j)[0:n, :], ACT.Copy).then_inc(
                        bank_free[j % BANKS], 1)
                act.nop().then_inc(xs_ready, 1)
                j = SJ["b", c]
                job_ready(act, j)
                act.activation(b_nat[0:n, :, :], bank(j)[0:n, 0:2 * P].rearrange("p (g l) -> p g l", g=2),
                               ACT.Copy).then_inc(b_ready, 1)
                act.wait_ge(b_ready, c + 1)
                act.nop().then_inc(bank_free[j % BANKS], 1)
                act.wait_ge(cums_ready, c + 1)
                act.activation(cums[:, 0:3, :], cums[:, 0:3, :], ACT.Exp).then_inc(cums_exp, 1)
                for q in range(4):
                    act.wait_ge(seg_ready, 4 * c + q + 1)
                    m = decay[0:n, 4 * q:4 * q + 4, 0:n]
                    act.activation(m, m, ACT.Exp).then_inc(seg_exp, 1)

        @block.gpsimd
        def _(pool):
            for c in ALL:
                n = TILE_N[c]
                pool.wait_ge(cb_out, c + 1)
                pool.affine_select(out=cb[0:n, :, 0:n], in_=cb[0:n, :, 0:n], compare_op=ALU.is_ge, fill=0.0, base=0,
                                   pattern=[[0, 2], [1, n]], channel_multiplier=-1).then_inc(cb_masked, 1)

        @block.vector
        def _(dve):
            dve_step(dve.memset(cums, 0.0))
            for c in ALL:
                n = TILE_N[c]
                for q in range(4):
                    k = 4 * c + q
                    if k >= 2:
                        job_ready(dve, SJ[f"row{(k - 2) % 4}", (k - 2) // 4])
                    dve.tensor_tensor(steps[0:n, q % 2, :, 0:n],
                                      by_tile(adt)[0:n, c, 4 * q:4 * q + 4].unsqueeze(2).broadcast_to([n, 4, n]),
                                      upto[0:n, 0:n].unsqueeze(1).broadcast_to([n, 4, n]), ALU.mult).then_inc(
                                          step_ready, 1)
                    if q == 1:
                        j = SJ["sums", c]
                        job_ready(dve, j)
                        dve.tensor_copy(cums[:, 2, :], bank(j)[:, 0:SSD_HEADS])
                        dve.tensor_copy(cums[0:n, 3, :], bank(j)[0:n, SSD_HEADS:2 * SSD_HEADS])
                        dve_step(dve.tensor_copy(cums[0:n, 0, :], bank(j)[0:n, SSD_HEADS:2 * SSD_HEADS]))
                        dve.nop().then_inc(bank_free[j % BANKS], 1)
                        dve.tensor_tensor(cums[0:n, 1, :], cums[0:n, 2, :], cums[0:n, 3, :],
                                          ALU.subtract).then_inc(cums_ready, 1)
                    if q >= 1:
                        segment(dve, c, q - 1)
                segment(dve, c, 3)
                dve.wait_ge(xs_ready, c + 1)
                dve.wait_ge(bank_free[SJ["xs1", c] % BANKS], SJ["xs1", c] // BANKS + 1)
                dve.tensor_tensor(heads_of_row(xdt, n), heads_of_row(xs, n),
                                  per_head(by_tile(dt)[0:n, c, :], n), ALU.mult).then_inc(xdt_ready, 1)
                for q in range(4):
                    dve.wait_ge(seg_exp, 4 * c + q + 1)
                    dve.wait_ge(cb_masked, c + 1)
                    m = decay[0:n, 4 * q:4 * q + 4, 0:n]
                    dve.tensor_tensor(m, m, cb[0:n, q // 2, 0:n].unsqueeze(1).broadcast_to([n, 4, n]),
                                      ALU.mult).then_inc(decay_ready, 1)
                dve.wait_ge(cums_exp, c + 1)
                dve.wait_ge(xdt_ready, c + 1)
                dve.tensor_tensor(heads_of_row(xd, n), heads_of_row(xdt, n), per_head(cums[0:n, 1, :], n),
                                  ALU.mult).then_inc(xd_ready, 1)
                y = y_tmp[0:n]
                dve_step(dve.tensor_tensor(heads_of_row(xs, n), heads_of_row(xs, n),
                                           per_head(ssd_rows[0:n, 2, :], n), ALU.mult))
                for g in range(SSD_GROUPS):
                    j = SJ[f"diag{g}", c]
                    job_ready(dve, j)
                    cols = slice(g * HG, g * HG + HG)
                    dve_step(dve.tensor_tensor(y[:, cols], xs[0:n, cols], bank(j)[0:n, :], ALU.add))
                    dve.nop().then_inc(bank_free[j % BANKS], 1)
                if c > 0:
                    for g in range(SSD_GROUPS):
                        j = SJ[f"off{g}", c]
                        job_ready(dve, j)
                        cols = slice(g * HG, g * HG + HG)
                        part = xs[0:n, cols].rearrange("p (h d) -> p h d", d=64)
                        dve_step(dve.tensor_tensor(part, bank(j)[0:n, :].rearrange("p (h d) -> p h d", d=64),
                                                   per_head(cums[0:n, 0, PD * g:PD * g + PD], n, nh=PD), ALU.mult))
                        dve.nop().then_inc(bank_free[j % BANKS], 1)
                        dve_step(dve.tensor_tensor(y[:, cols], y[:, cols], xs[0:n, cols], ALU.add))
                dve_step(dve.tensor_tensor(zs[0:n, c, :], zs[0:n, c, :], y, ALU.mult))
                if c < 2:
                    for g in range(SSD_GROUPS):
                        j = SJ[f"state{g}", c]
                        job_ready(dve, j)
                        cols = slice(g * HG, g * HG + HG)
                        if c == 0:
                            dve_step(dve.tensor_copy(state[:, cols], bank(j)))
                        else:
                            part = state[:, cols].rearrange("p (h d) -> p h d", d=64)
                            dve_step(dve.tensor_tensor(part, part,
                                                       per_head(cums[:, 2, PD * g:PD * g + PD], P, nh=PD), ALU.mult))
                            dve_step(dve.tensor_tensor(state[:, cols], state[:, cols], bank(j), ALU.add))
                        dve.nop().then_inc(bank_free[j % BANKS], 1)
                    dve.nop().then_inc(state_ready, 1)
                dve.nop().then_inc(y_done, 1)

    def segment(dve, c, q):
        n = TILE_N[c]
        j = SJ[f"row{q}", c]
        job_ready(dve, j)
        if q == 0:
            dve.wait_ge(cums_ready, c + 1)
        m = decay[0:n, 4 * q:4 * q + 4, 0:n]
        dve_step(dve.tensor_tensor(m, bank(j)[0:n, 0:4 * n].rearrange("p (h l) -> p h l", h=4),
                                   cums[0:n, 3, 4 * q:4 * q + 4].unsqueeze(2).broadcast_to([n, 4, n]), ALU.subtract))
        dve.nop().then_inc(bank_free[j % BANKS], 1)
        dve.tensor_scalar(m, m, 0.0, None, ALU.min).then_inc(seg_ready, 1)

    @stage
    def ssd_norm():
        rms_to_T("ssd_norm", "y_T", lambda t: zs[:, t, :], lambda t: xn2[:, t, :], yT, "ssd_norm_g_2")

    xn2 = carve(3072, 3, D)

    sqT, skT = carve(0, KC, L), carve(2176, KC, L)
    sv = carve(4352, 3, D)
    so = carve(7424, 3, D)
    W1 = 384
    pos, soft, wts = carve(10496, 2, W1 + L), carve(11808, 2, W1 + L), carve(13120, 2, W1 + L)
    z_ready, neg_abs, soft_exp, soft_ln, soft_sum, soft_ready, expo_ready, w_exp, w_ready, so_ready = (
        sem(f"sb_{x}") for x in ("z_ready", "neg_abs", "exp", "ln", "sum", "soft_ready", "expo", "w_exp",
                                 "w_ready", "o_ready"))

    def sb_bank(h):
        return psum[:, BANKS + 2 * (h % 2), 0:W1], psum[0:META, BANKS + 2 * (h % 2) + 1, 0:L]

    def sb_parts(x, h):
        return x[:, h % 2, 0:W1], x[0:META, h % 2, W1:W1 + L]

    @stage
    def stick_breaking():
        @block.tensor
        def _(pe):
            for first, u0 in ((FJ["sb_q"], unit_at["w_sb_q"]), (FJ["sb_k"], unit_at["w_sb_k"])):
                for c in range(KC):
                    j = first + c
                    unit_ready(u0 + c // 4)
                    take_bank(j)
                    products(bank(j)[:, 0:L], [(slot_k(u0 + c // 4)[:, k, (c % 4) * P:(c % 4) * P + P], xT[:, k, :])
                                               for k in range(KC)]).then_inc(job_done, 1)
            project_natural(FJ["sb_v"], unit_at["w_sb_v"], xT, ALL, KC)
            all_read_out(pe, FJ["sb_heads"])

            def logits(h):
                rows = slice(64 * (h % 2), 64 * (h % 2) + 64)
                c = h // 2
                main, meta = sb_bank(h)
                if h >= 2:
                    pe.wait_ge(w_exp, 2 * (h - 1))
                pe.matmul(main[:, 0:SEQ], skT[rows, c, META:META + P], sqT[rows, c, META:L], start=True, stop=True)
                pe.matmul(main[:, SEQ:W1], skT[rows, c, META + P:L], sqT[rows, c, META + P:L], start=False, stop=True,
                          skip_group_check=True)
                pe.matmul(meta, skT[rows, c, 0:META], sqT[rows, c, :], start=True, stop=True).then_inc(z_ready, 1)

            def exponents(h):
                main, meta = sb_bank(h)
                s1, s0 = sb_parts(soft, h)
                pe.wait_ge(soft_ready, h + 1)
                terms = [(main[:, SEQ:W1], neg_from[:, :], s1[:, SEQ:W1]),
                         (main[:, 0:SEQ], neg_from[:, :], s1[:, 0:SEQ]),
                         (main[:, P:SEQ], neg_ones[:, :], s1[:, SEQ:W1]),
                         (meta, neg_from[0:META, 0:META], s0),
                         (meta[:, META:L], neg_ones[:, 0:META], s1[:, 0:SEQ]),
                         (meta[:, META + P:L], neg_ones[:, 0:META], s1[:, SEQ:W1])]
                for dst, lhsT, rhs in terms:
                    last = pe.matmul(dst, lhsT, rhs, start=False, stop=True, skip_group_check=True)
                last.then_inc(expo_ready, 1)

            def values(h):
                j = FJ["sb_heads"] + h
                w1, w0 = sb_parts(wts, h)
                cols = slice(64 * h, 64 * h + 64)
                pe.wait_ge(w_ready, h + 1)
                take_bank(j)
                products(bank(j)[0:META, 0:64], [(w0[:, 0:META], sv[0:META, 0, cols])])
                products(bank(j)[:, 64:128], [(w0[:, META:META + P], sv[0:META, 0, cols]),
                                              (w1[:, 0:P], sv[:, 1, cols])])
                products(bank(j)[:, 128:192], [(w0[:, META + P:L], sv[0:META, 0, cols]),
                                               (w1[:, P:SEQ], sv[:, 1, cols]),
                                               (w1[:, SEQ:W1], sv[:, 2, cols])]).then_inc(job_done, 1)

            for n in range(SB_HEADS + 2):
                if n < SB_HEADS:
                    logits(n)
                if 1 <= n <= SB_HEADS:
                    exponents(n - 1)
                if n >= 2:
                    values(n - 2)

        @block.scalar
        def _(act):
            for first, dst, scale in ((FJ["sb_q"], sqT, 0.125), (FJ["sb_k"], skT, 1.0)):
                for c in range(KC):
                    j = first + c
                    job_ready(act, j)
                    act.activation(dst[:, c, :], bank(j)[:, 0:L], ACT.Copy, scale=scale).then_inc(
                        bank_free[j % BANKS], 1)

            def softplus(h):
                for part in sb_parts(soft, h):
                    act.wait_ge(neg_abs, h + 1)
                    act.activation(part, part, ACT.Exp).then_inc(soft_exp, 1)
                for n, part in enumerate(sb_parts(soft, h)):
                    act.wait_ge(soft_exp, 2 * h + n + 1)
                    act.activation(part, part, ACT.Ln, bias=1.0).then_inc(soft_ln, 1)

            def weights(h):
                act.wait_ge(expo_ready, h + 1)
                if h >= 2:
                    job_ready(act, FJ["sb_heads"] + h - 2)
                for dst, src in zip(sb_parts(wts, h), sb_bank(h)):
                    act.activation(dst, src, ACT.Exp).then_inc(w_exp, 1)

            for n in range(SB_HEADS + 1):
                if n < SB_HEADS:
                    softplus(n)
                if n >= 1:
                    weights(n - 1)

        @block.gpsimd
        def _(pool):
            def masked(x, h):
                main, meta = sb_parts(x, h)
                for part in (main[:, 0:P], main[:, SEQ:W1], meta[:, 0:META]):
                    n = part.shape[1]
                    ins = pool.affine_select(out=part, in_=part, compare_op=ALU.is_gt, fill=0.0, base=0,
                                             pattern=[[1, n]], channel_multiplier=-1)
                return ins

            for n in range(SB_HEADS + 1):
                if n < SB_HEADS:
                    pool.wait_ge(soft_ln, 2 * n + 2)
                    pool.wait_ge(neg_abs, n + 1)
                    for dst, more in zip(sb_parts(soft, n), sb_parts(pos, n)):
                        pool_step(pool.tensor_tensor(dst, dst, more, ALU.add))
                    masked(soft, n).then_inc(soft_ready, 1)
                if n >= 1:
                    pool.wait_ge(w_exp, 2 * n)
                    masked(wts, n - 1).then_inc(w_ready, 1)

        @block.vector
        def _(dve):
            j = FJ["sb_v"]
            for half in range(2):
                for t in ALL:
                    n = TILE_N[t]
                    job_ready(dve, j)
                    dve.tensor_copy(sv[0:n, t, half * 512:half * 512 + 512], bank(j)[0:n, :]).then_inc(
                        bank_free[j % BANKS], 1)
                    j += 1
            for n in range(SB_HEADS + 2):
                if n < SB_HEADS:
                    dve.wait_ge(z_ready, n + 1)
                    if n >= 2:
                        dve.wait_ge(expo_ready, n - 1)
                    for m, z in zip(sb_parts(pos, n), sb_bank(n)):
                        dve_step(dve.tensor_scalar(m, z, 0.0, None, ALU.max))
                    for s, m, z in zip(sb_parts(soft, n), sb_parts(pos, n), sb_bank(n)):
                        ins = dve.scalar_tensor_tensor(s, m, -2.0, z, ALU.mult, ALU.add)
                    ins.then_inc(neg_abs, 1)
                if n >= 2:
                    h = n - 2
                    j = FJ["sb_heads"] + h
                    job_ready(dve, j)
                    dve.tensor_copy(so[0:META, 0, 64 * h:64 * h + 64], bank(j)[0:META, 0:64])
                    dve_step(dve.tensor_copy(so[:, 1:3, 64 * h:64 * h + 64],
                                             bank(j)[:, 64:192].rearrange("p (t d) -> p t d", t=2)))
                    dve.nop().then_inc(bank_free[j % BANKS], 1)

    sbT = carve(0, KC, L)
    so_n = carve(10496, 3, D)

    @stage
    def sb_norm():
        rms_to_T("sb_norm", "sb_T", lambda t: so[:, t, :], lambda t: so_n[:, t, :], sbT, "sb_norm_g_2")

    mix = carve(4352, 3, D)
    mix_n = carve(7424, 3, D)
    mix_out, mix_scaled, w_out_done = sem("mix_out"), sem("mix_scaled"), sem("w_out_done")

    def post_norm(k, name, tiles, src, dst):
        scaled = sem(f"{name}_scaled")
        rms(name, tiles, src, dst, scaled, next_sqrt())

        @block.vector
        def _(dve):
            dve.wait_ge(norm_loaded[k % 2], norm_count[k % 2])
            for i, t in enumerate(tiles):
                n = TILE_N[t]
                dve.wait_ge(scaled, i + 1)
                dve_step(dve.tensor_tensor(dst(t)[0:n], dst(t)[0:n], norm_rows[0:n, k % 2, 0, :], ALU.mult))
                dve.tensor_tensor(x_nat[0:n, t, :], x_nat[0:n, t, :], dst(t)[0:n], ALU.add)

    @stage
    def project_out():
        @block.tensor
        def _(pe):
            j = FJ["w_out"]
            for half in range(2):
                for part in range(2):
                    unit_ready(unit_at["w_out"] + 2 * half + part)
                for t in ALL:
                    n, at = TILE_N[t], TILE_AT[t]
                    take_bank(j)
                    pairs = [(srcT[:, k, at:at + n], slot_k(unit_at["w_out"] + 2 * half + part)[:, k, :])
                             for part, srcT in enumerate((yT, sbT)) for k in range(KC)]
                    products(bank(j)[0:n, :], pairs).then_inc(job_done, 1)
                    j += 1

        @block.vector
        def _(dve):
            j = FJ["w_out"]
            for half in range(2):
                for t in ALL:
                    n = TILE_N[t]
                    job_ready(dve, j)
                    dve.tensor_copy(mix[0:n, t, half * 512:half * 512 + 512], bank(j)[0:n, :]).then_inc(
                        bank_free[j % BANKS], 1)
                    j += 1

    @stage
    def mix_post():
        post_norm(4, "mix_post", ALL, lambda t: mix[:, t, :], lambda t: mix_n[:, t, :])

    @stage
    def ffn_pre():
        rms_to_T("ffn_pre", "ffn_T", lambda t: x_nat[:, t, :], lambda t: xn[:, t, :], xT, "ffn_pre_g_2")

    fT = carve(3072, FC, SEQ)
    gate = carve(8800, 4, SEQ)
    act_g = carve(9900, 2, SEQ)
    G0 = META - (FFN_TAPS - 1)
    GW = SEQ + FFN_TAPS - 1
    gconv_step, gelu_ready, f_ready, down_ready = sem("gconv_step"), sem("gelu_ready"), sem("f_ready"), sem("down_ready")
    f_out = carve(10500, 2, D)
    f_n = carve(12600, 2, D)

    @stage
    def ffn():
        @block.tensor
        def _(pe):
            for c in range(FC):
                u = unit_at["w_up"] + c // 2
                unit_ready(u)
                for side, (at, width) in enumerate(((G0, GW), (META, SEQ))):
                    j = FJ["up"] + 2 * c + side
                    take_bank(j)
                    cols = side * 256 + (c % 2) * P
                    products(bank(j)[:, 0:width], [(slot_k(u)[:, k, cols:cols + P], xT[:, k, at:at + width])
                                                   for k in range(KC)]).then_inc(job_done, 1)
            for c in range(FC):
                u = unit_at["w_down"] + c // 4
                if c % 4 == 0:
                    unit_ready(u)
                pe.wait_ge(f_ready, c + 1)
                for t in range(2):
                    for half in range(2):
                        last = pe.matmul(psum[:, BANKS + 2 * t + half, :], fT[:, c, t * P:t * P + P],
                                         slot_k(u, D)[:, c % 4, half * 512:half * 512 + 512], start=(c == 0),
                                         stop=(c == FC - 1))
            last.then_inc(down_ready, 1)

        @block.scalar
        def _(act):
            for c in range(FC):
                act.wait_ge(gconv_step, 3 * c + 3)
                if c >= 2:
                    act.wait_ge(f_ready, c - 1)
                act.activation(act_g[:, c % 2, :], gate[:, c % 4, :], ACT.Gelu_apprx_tanh).then_inc(gelu_ready, 1)

        @block.vector
        def _(dve):
            for c in range(FC):
                j = FJ["up"] + 2 * c
                job_ready(dve, j)
                if c >= 4:
                    dve.wait_ge(gelu_ready, c - 3)
                for tap in range(FFN_TAPS):
                    src = bank(j)[:, tap:tap + SEQ]
                    w = column("ffn_conv_w_2", tap * FC + c)
                    g = gate[:, c % 4, :]
                    if tap == 0:
                        ins = dve.tensor_scalar(g, src, w, column("ffn_conv_b_2", c), ALU.mult, ALU.add)
                    else:
                        dve.wait_ge(gconv_step, 3 * c + tap)
                        ins = dve.scalar_tensor_tensor(g, src, w, g, ALU.mult, ALU.add)
                    ins.then_inc(gconv_step, 1)
                dve.wait_ge(gconv_step, 3 * c + 3)
                dve.nop().then_inc(bank_free[j % BANKS], 1)
                dve.wait_ge(gelu_ready, c + 1)
                job_ready(dve, j + 1)
                dve.tensor_tensor(fT[:, c, :], act_g[:, c % 2, :], bank(j + 1)[:, 0:SEQ], ALU.mult).then_inc(f_ready, 1)
                dve.wait_ge(f_ready, c + 1)
                dve.nop().then_inc(bank_free[(j + 1) % BANKS], 1)
            dve.wait_ge(down_ready, 1)
            for t in range(2):
                dve.tensor_copy(f_out[:, t, :], psum[:, BANKS + 2 * t:BANKS + 2 * t + 2, :].rearrange(
                    "p b n -> p (b n)"))

    @stage
    def ffn_post():
        post_norm(5, "ffn_post", (1, 2), lambda t: f_out[:, t - 1, :], lambda t: f_n[:, t - 1, :])

    order = ["constants", "conformer", "mix_norm0", "moe0", "ffn_norm0", "attention", "mix_norm1", "moe1", "ffn_norm1",
             "pre_norm", "inner", "ssd", "ssd_norm", "stick_breaking", "sb_norm", "project_out", "mix_post", "ffn_pre",
             "ffn", "ffn_post"]
    next_norm = {
        "constants": (1, a["ln_ffn_g"][0], a["ln_ffn_b"][0]), "mix_norm0": (2, a["ln_mix_g"][1], a["ln_mix_b"][1]),
        "ffn_norm0": (3, a["ln_ffn_g"][1], a["ln_ffn_b"][1]), "mix_norm1": (4, a["mix_post_g_2"][0]),
        "ffn_norm1": (5, a["ffn_post_g_2"][0]),
    }
    table = {f.__name__: f for f in stages}
    for name in order:
        table[name]()
        next_stage()
        if name in next_norm:
            block.scalar(lambda act, args=next_norm[name]: load_norm(*args))
        if stop == name:
            break

    @block.sync
    def _(sp):
        sp.wait_ge(stage_left, len(compute) * left[0])
        sp.dma_start(out[0].rearrange("(t p) n -> p t n", p=P), x_nat[:, 1:3, :]).then_inc(output_written, 16)
        sp.wait_ge(output_written, 16)
        for k in range(2):
            if norm_count[k]:
                sp.wait_ge(norm_loaded[k], norm_count[k])

    ctx.close()


_INS = ["x", "a_w_pw1", "a_b_pw1", "a_w_dw", "a_b_dw", "a_ln_g", "a_ln_b", "a_w_pw2", "a_b_pw2", "w_kv", "b_w_q",
        "b_lambda", "b_subln_g", "b_w_o", "rel_bias", "ln_mix_g", "ln_mix_b", "ln_ffn_g", "ln_ffn_b", "router_w",
        "router_bias", "moe_w_gate", "moe_w_up", "moe_w_down", "meta_tokens_2", "mix_pre_g_2", "w_in_2",
        "ssd_conv_w_2", "ssd_conv_b_2", "ssd_dt_bias_2", "ssd_a_log_2", "ssd_d_2", "ssd_norm_g_2", "sb_norm_g_2",
        "w_out_2", "mix_post_g_2", "ffn_pre_g_2", "w_up_2", "ffn_conv_w_2", "ffn_conv_b_2", "w_down_2",
        "ffn_post_g_2"]


def kernel(**inputs):
    import concourse.bacc as bacc
    from concourse.bass_utils import run_bass_kernel_spmd

    nc = bacc.Bacc("TRN2", target_bir_lowering=False, num_devices=1)
    arrays, aps = {}, {}
    for name in _INS:
        arrays[f"in_{name}"] = np.ascontiguousarray(inputs[name])
    arrays["in_buckets"] = bucket_table()
    for name, arr in arrays.items():
        aps[name[3:]] = nc.dram_tensor(name, arr.shape, mybir.dt.from_np(arr.dtype), kind="ExternalInput").ap()
    out = nc.dram_tensor("out_0", (1, SEQ, D), F32, kind="ExternalOutput").ap()
    program(nc, aps, out)
    r = run_bass_kernel_spmd(nc, [arrays], core_ids=[0])
    return r.results[0]["out_0"]
```

```python
import math
from contextlib import ExitStack

import numpy as np

import concourse.bass as bass
from concourse import mybir

ARENA = 16640
F32 = mybir.dt.float32
ALU = mybir.AluOpType
ACT = mybir.ActivationFunctionType
AX_X = mybir.AxisListType.X

P = 128
D = 1024
KC = D // P
SEQ = 256
META = 16
L = META + SEQ
DEPTH = 2
ALPHA = (2.0 * DEPTH) ** 0.25
LN_EPS = 1e-5
TAPS = 31
HEADS, HD = 8, 64
N_BUCKETS, MAX_DISTANCE = 32, 128
LAMBDA_INIT = 0.8 - 0.6 * math.exp(-0.3 * 1)
MASKED = -1e30
EXPERTS, GROUPS, PER_GROUP, DE = 16, 4, 4, 512
RING = 6
BANKS = 4
TILE_AT, TILE_N = (0, META, META + P), (META, P, P)

SSD_HEADS, SSD_GROUPS, STATE, SSD_TAPS = 16, 2, 128, 4
XBC = D + 2 * SSD_GROUPS * STATE
XC = XBC // P
SB_HEADS = 16
EPS = 1e-6
D_FF = 2816
FC = D_FF // P
FFN_TAPS = 3
OFF_XBC = D
OFF_DT = OFF_XBC + XBC
OFF_Q = OFF_DT + SSD_HEADS
OFF_K, OFF_V = OFF_Q + D, OFF_Q + 2 * D

VEC_ROWS = [
    [("a_w_dw", 0, 128)],
    [("a_w_dw", 128, 120), ("a_b_dw", 0, 8)],
    [("a_ln_g", 0, 8), ("a_ln_b", 0, 8), ("a_b_pw1", 0, 16), ("mix_pre_g_2", 0, 8), ("ssd_norm_g_2", 0, 8),
     ("sb_norm_g_2", 0, 8), ("ffn_pre_g_2", 0, 8), ("ssd_conv_w_2", 0, SSD_TAPS * XC), ("ssd_conv_b_2", 0, XC)],
    [("ffn_conv_w_2", 0, FFN_TAPS * FC), ("ffn_conv_b_2", 0, FC)],
]
VEC_COL = {}
for _tile, _rows in enumerate(VEC_ROWS):
    _at = 0
    for _name, _first, _n in _rows:
        VEC_COL.setdefault(_name, _tile * P + _at)
        _at += _n

JOBS = [
    ("vec", 1), ("conv_xT", 4), ("glu", 8), ("iota", 1), ("relb", 1), ("conv", 2), ("conv_mean", 1), ("conv_var", 1), ("pw2", 4), ("mix0_xT", 4),
    ("route0", 2), ("moe0", 68), ("ffn0_xT", 4),
    ("att_k", 8), ("att_v", 4), ("att_q", 8), ("att_heads", 3 * 16), ("att_T", 4), ("att_o", 4),
    ("mix1_xT", 4), ("route1", 2), ("moe1", 68), ("ffn1_xT", 0),
    ("pre_xT", 6), ("z", 14), ("xbc", XC), ("dt", 1), ("ssd", 3 * 11 + 2 * 2 + 2 * 2), ("y_T", 6),
    ("sb_q", 8), ("sb_k", 8), ("sb_v", 14), ("sb_heads", SB_HEADS), ("sb_T", 6), ("w_out", 14),
    ("ffn_T", 6), ("up", 2 * FC),
]


def first_jobs():
    at, out = 0, {}
    for name, n in JOBS:
        out[name] = at
        at += n
    return out


def t5_bucket(n):
    exact = N_BUCKETS // 2
    nf = np.maximum(n, 1).astype(np.float32)
    large = exact + (np.log(nf / np.float32(exact)) / np.float32(math.log(MAX_DISTANCE / exact))
                     * np.float32(N_BUCKETS - exact)).astype(np.int32)
    return np.where(n < exact, n, np.minimum(large, N_BUCKETS - 1))


def bucket_table():
    table = np.zeros((N_BUCKETS, 3 * P), np.float32)
    j = np.arange(SEQ)
    table[t5_bucket(SEQ - 1 - j), j] = 1.0
    return table


ORDER = ["constants", "conformer", "mix_norm0", "route0", "overflow0", "moe0", "ffn_norm0", "attention", "mix_norm1", "route1", "overflow1", "moe1", "ffn_norm1",
         "pre_norm", "inner", "ssd", "ssd_norm", "stick_breaking", "sb_norm", "project_out", "mix_post", "ffn_pre",
         "ffn", "ffn_post"]


class Chain:

    def __init__(self, eng, sem):
        self.eng, self.sem, self.n = eng, sem, 0

    def __call__(self, ins):
        self.n += 1
        ins.then_inc(self.sem, 1)
        self.eng.wait_ge(self.sem, self.n)


def program(nc, a, out, stop=None):
    ctx = ExitStack()

    def sb(name, *shape):
        return ctx.enter_context(nc.sbuf_tensor(name, list(shape), F32))

    def sem(name):
        return ctx.enter_context(nc.semaphore(name))

    FJ = first_jobs()
    ring = sb("ring", P, RING, 4096)
    x_nat = sb("x_nat", P, 3, D)
    xT = sb("xT", P, KC, L)
    norm_rows = sb("norm_rows", P, 2, 2, D)
    vec = sb("vec", P, 4 * P)
    ident = sb("ident", P, P)
    ones = sb("ones", P, P)
    router_w = sb("router_w", P, KC, EXPERTS)
    router_b = sb("router_b", P, EXPERTS)
    gates = sb("gates", P, 2, EXPERTS)
    eps_cols = sb("eps_cols", P, 2)
    counting = sb("counting", P, P)
    over_flag = ctx.enter_context(nc.sbuf_tensor("over_flag", [P, 1], mybir.dt.int32))
    rel_w = sb("rel_w", N_BUCKETS, HEADS)
    upto, neg_from, neg_ones = sb("upto", P, P), sb("neg_from", P, P), sb("neg_ones", P, P)
    ssd_rows = sb("ssd_rows", P, 3, SSD_HEADS)
    w_dt = sb("w_dt", P, KC, SSD_HEADS)
    dts = sb("dts", P, 10, 3 * SSD_HEADS)
    small = sb("small", P, 64)
    stats = sb("stats", P, 3, 2, 6)
    arena = sb("arena", P, ARENA)

    psum = ctx.enter_context(nc.psum_tensor("psum", [P, 8, 512], F32))
    rel_scratch = nc.dram_tensor("rel_scratch", (HEADS, 3 * P), F32).ap()

    slot_loaded = [sem(f"slot_loaded{i}") for i in range(RING)]
    job_done = sem("job_done")
    bank_free = [sem(f"bank_free{i}") for i in range(BANKS)]
    stage_left = sem("stage_left")
    consts_loaded = sem("consts_loaded")
    consts_made = sem("consts_made")
    x_loaded, rows_sent = sem("x_loaded"), sem("rows_sent")
    norm_loaded = [sem("norm_loaded0"), sem("norm_loaded1")]
    output_written = sem("output_written")
    var_ready, std_ready = sem("var_ready"), sem("std_ready")
    dve_step, act_step = Chain(nc.vector, sem("dve_step")), Chain(nc.scalar, sem("act_step"))
    pool_step = Chain(nc.gpsimd, sem("pool_step"))

    def carve(at, *shape):
        n = int(np.prod(shape))
        assert at + n <= ARENA, (at, n)
        flat = arena[:, at:at + n]
        if len(shape) == 1:
            return flat
        names = "abcd"[:len(shape)]
        return flat.rearrange(f"p ({' '.join(names)}) -> p {' '.join(names)}", **dict(zip(names, shape)))

    def column(name, i):
        at = VEC_COL[name] + i
        return vec[:, at:at + 1]

    def bank(j):
        return psum[:, j % BANKS, :]

    def take_bank(j):
        if j >= BANKS:
            nc.tensor.wait_ge(bank_free[j % BANKS], j // BANKS)

    def job_ready(eng, j):
        eng.wait_ge(job_done, j + 1)

    def all_read_out(eng, j):
        for b in range(BANKS):
            eng.wait_ge(bank_free[b], (j - b + BANKS - 1) // BANKS)

    def products(dst, pairs):
        for n, (lhsT, rhs) in enumerate(pairs):
            last = nc.tensor.matmul(dst, lhsT, rhs, start=(n == 0), stop=(n == len(pairs) - 1))
        return last

    def columns_of(w, at, n=512):
        return w[:, at:at + n].rearrange("(k p) n -> p k n", p=P)

    units = []

    def add_units(name, srcs, last_jobs):
        first = len(units)
        for s, j in zip(srcs, last_jobs):
            units.append((s, ("job", j)))
        unit_at[name] = first

    unit_at = {}
    w_pw1 = a["a_w_pw1"][0]
    add_units("pw1", [columns_of(w_pw1, c) for c in (0, D, 512, D + 512)],
              [FJ["glu"] + n for n in (3, 3, 7, 7)])
    add_units("pw2", [columns_of(a["a_w_pw2"][0], c) for c in (0, 512)], [FJ["pw2"] + n for n in (1, 3)])

    IN_GROUP = {("G", 0): 0, ("U", 0): 1, ("G", 1): 2, ("T", 0): 3, ("U", 1): 4, ("G", 2): 5, ("T", 1): 6,
                ("U", 2): 7, ("G", 3): 8, ("T", 2): 9, ("U", 3): 10, ("X", 0): 11, ("X", 1): 12, ("R", 0): 13,
                ("S", 0): 14, ("T", 3): 15}
    GROUP_JOBS = len(IN_GROUP)

    def group_first(layer, g):
        return FJ[f"moe{layer}"] + 4 + GROUP_JOBS * g

    def add_moe(layer):
        unit_at[f"moe{layer}"] = len(units)
        for e in range(EXPERTS):
            first = group_first(layer, e // PER_GROUP)
            units.append((("gate", layer, e), ("job", first + IN_GROUP["G", e % PER_GROUP])))
            units.append((("up", layer, e), ("job", first + IN_GROUP["U", e % PER_GROUP])))
            units.append((("down", layer, e), ("down", layer, e + 1)))

    add_moe(0)
    w_kv, w_q, w_o = a["w_kv"], a["b_w_q"][0], a["b_w_o"][0]
    add_units("w_k", [columns_of(w_kv, c) for c in (0, 512)], [FJ["att_k"] + n for n in (3, 7)])
    add_units("w_v", [columns_of(w_kv, c) for c in (D, D + 512)], [FJ["att_v"] + n for n in (1, 3)])
    add_units("w_q", [columns_of(w_q, c) for c in (0, 512)], [FJ["att_q"] + n for n in (3, 7)])
    add_units("w_o", [columns_of(w_o, c) for c in (0, 512)], [FJ["att_o"] + n for n in (1, 3)])
    add_moe(1)
    w_in, w_out, w_up, w_down = a["w_in_2"][0], a["w_out_2"][0], a["w_up_2"][0], a["w_down_2"][0]
    add_units("w_z", [columns_of(w_in, c) for c in (0, 512)], [FJ["z"] + n for n in (3, 7)])
    add_units("w_xbc", [columns_of(w_in, OFF_XBC + c) for c in (0, 512, 1024)], [FJ["xbc"] + n for n in (3, 7, 11)])
    add_units("w_sb_q", [columns_of(w_in, OFF_Q + c) for c in (0, 512)], [FJ["sb_q"] + n for n in (3, 7)])
    add_units("w_sb_k", [columns_of(w_in, OFF_K + c) for c in (0, 512)], [FJ["sb_k"] + n for n in (3, 7)])
    add_units("w_sb_v", [columns_of(w_in, OFF_V + c) for c in (0, 512)], [FJ["sb_v"] + n for n in (3, 7)])
    add_units("w_out", [columns_of(w_out[part * D:part * D + D], half * 512) for half in range(2) for part in range(2)],
              [FJ["w_out"] + n for n in (3, 3, 7, 7)])
    add_units("w_up", [(columns_of(w_up, 2 * P * n, 2 * P), columns_of(w_up, D_FF + 2 * P * n, 2 * P))
                       for n in range(FC // 2)], [FJ["up"] + 4 * n + 3 for n in range(FC // 2)])
    unit_at["w_down"] = len(units)
    for n in range((FC + 3) // 4):
        rows_n = min(4, FC - 4 * n)
        units.append((("rows", w_down[4 * n * P:(4 * n + rows_n) * P].rearrange("(k p) n -> p k n", p=P), rows_n),
                      ("last",)))

    def slot(u):
        return ring[:, u % RING, :]

    def slot_k(u, n=512):
        return slot(u).rearrange("p (k n) -> p k n", n=n)

    def loads_of(u):
        return 16 * sum(2 if isinstance(units[v][0], tuple) and not isinstance(units[v][0][0], str) else 1
                        for v in range(u % RING, u + 1, RING))

    def unit_ready(u):
        nc.tensor.wait_ge(slot_loaded[u % RING], loads_of(u))

    block = ctx.enter_context(nc.Block())

    down_done = [sem("down_done0"), sem("down_done1")]

    @block.sync
    def _(sp):
        def slot_freed(u, i=0):
            if u < RING:
                return
            free = units[u - RING][1]
            if free[0] == "job":
                sp.wait_ge(job_done, free[1] + 1 + GROUP_JOBS * i)
            else:
                sp.wait_ge(down_done[free[1]], free[2] + PER_GROUP * i)

        def load(u, src, dst=None):
            sp.dma_start(slot_k(u) if dst is None else dst, src).then_inc(slot_loaded[u % RING], 16)

        def load_expert(u, kind, layer, e):
            if kind == "down":
                src = a["moe_w_down"][layer, e if isinstance(e, int) else bass.ds(e, 1)]
                src = src.rearrange("(k p) n -> p k n" if isinstance(e, int) else "a (k p) n -> p (a k) n", p=P)
                load(u, src, slot_k(u, D))
            else:
                src = a[f"moe_w_{kind}"][layer, e if isinstance(e, int) else bass.ds(e, 1)]
                src = src.rearrange("(k p) n -> p k n" if isinstance(e, int) else "a (k p) n -> p (a k) n", p=P)
                load(u, src)

        sp.dma_start(x_nat[:, 1:3, :], a["x"][0].rearrange("(t p) n -> p t n", p=P)).then_inc(x_loaded, 16)
        sp.wait_ge(rows_sent, 1)
        u = 0
        until = len(units)
        if stop is not None:
            until = {'constants': 6, 'conformer': 6, 'mix_norm0': 6}.get(stop, until)
            if stop in ('moe0', 'ffn_norm0'):
                until = 54
            if stop in ('attention', 'mix_norm1'):
                until = unit_at['moe1']
            if stop in ('moe1', 'ffn_norm1', 'pre_norm', 'inner', 'ssd', 'ssd_norm'):
                until = unit_at['w_sb_q']
            if stop in ('stick_breaking', 'sb_norm'):
                until = unit_at['w_out']
            if stop in ('mix_post', 'ffn_pre'):
                until = unit_at['w_up']
        while u < until:
            src = units[u][0]
            if isinstance(src, tuple) and src[0] == "gate" and src[2] == 2:
                with sp.Fori(0, GROUPS - 1) as i:
                    for n in range(3 * PER_GROUP):
                        slot_freed(u + n, i)
                        load_expert(u + n, units[u + n][0][0], src[1], i * PER_GROUP + 2 + n // 3)
                u += 3 * PER_GROUP * (GROUPS - 1)
                continue
            slot_freed(u)
            if isinstance(src, tuple) and src[0] in ("gate", "up", "down"):
                load_expert(u, *src)
            elif isinstance(src, tuple) and src[0] == "rows":
                load(u, src[1], slot_k(u, D)[:, 0:src[2], :])
            elif isinstance(src, tuple):
                for side in range(2):
                    sp.dma_start(slot_k(u)[:, :, side * 256:side * 256 + 256], src[side]).then_inc(
                        slot_loaded[u % RING], 16)
            else:
                load(u, src)
            u += 1

    stages = []
    left = [0]
    norm_count = [0, 0]
    compute = (nc.tensor, nc.scalar, nc.vector, nc.gpsimd)

    def stage(f):
        stages.append(f)
        return f

    def next_stage():
        n = left[0] = left[0] + 1

        def meet(eng):
            eng.drain().then_inc(stage_left, 1)
            eng.wait_ge(stage_left, len(compute) * n)

        block.tensor(meet)
        block.scalar(meet)
        block.vector(meet)
        block.gpsimd(meet)

    def transposes_pe(first, tiles, src, ready=None):
        j = first
        for t in tiles:
            n = TILE_N[t]
            if ready is not None:
                ready(t)
            for half in range(2):
                take_bank(j)
                for c in range(4):
                    at = (4 * half + c) * P
                    last = nc.tensor.transpose(bank(j)[:, c * P:c * P + n], src(t)[0:n, at:at + P], ident[0:n, 0:n])
                last.then_inc(job_done, 1)
                j += 1

    def transposes_out(first, tiles, dst, gain=None):
        act = nc.scalar
        j = first
        for t in tiles:
            n, at = TILE_N[t], TILE_AT[t]
            for half in range(2):
                job_ready(act, j)
                src = bank(j).rearrange("p (c t) -> p c t", c=4)[:, :, 0:n]
                if gain is None:
                    act.activation(dst[:, 4 * half:4 * half + 4, at:at + n], src, ACT.Copy).then_inc(
                        bank_free[j % BANKS], 1)
                else:
                    for c in range(4):
                        last = act.activation(dst[:, 4 * half + c, at:at + n], src[:, c, :], ACT.Copy,
                                              scale=column(gain, 4 * half + c))
                    last.then_inc(bank_free[j % BANKS], 1)
                j += 1

    def load_norm(k, gain, bias=None):
        act = nc.scalar
        norm_count[k % 2] += 32
        act.dma_start(norm_rows[:, k % 2, 0, :], gain.partition_broadcast(P)).then_inc(norm_loaded[k % 2], 16)
        b = gain if bias is None else bias
        act.dma_start(norm_rows[:, k % 2, 1, :], b.partition_broadcast(P)).then_inc(norm_loaded[k % 2], 16)

    rsqrt_n = [0]

    def next_sqrt():
        rsqrt_n[0] += 1
        return rsqrt_n[0]

    def sqrt_of(act, values, scale, eps, n):
        act.wait_ge(var_ready, n)
        p = values.shape[0]
        bias = eps_cols[0:p, 0:1] if eps == LN_EPS else eps_cols[0:p, 1:2]
        act.activation(values, values, ACT.Sqrt, bias=bias, scale=scale).then_inc(std_ready, 1)

    def reciprocal_of(dve, values, n):
        dve.wait_ge(std_ready, n)
        dve_step(dve.reciprocal(values, values))

    def layer_norm(k, name, normed, last=False):
        mean_var = small[:, 2:6].rearrange("p (t s) -> p t s", s=2)
        root = next_sqrt()

        @block.vector
        def _(dve):
            dve.wait_ge(norm_loaded[k % 2], 32 * (k // 2 + 1))
            for t in (1, 2):
                for half in range(2):
                    dve_last = dve.bn_stats(stats[:, t, half, :], x_nat[:, t, half * 512:half * 512 + 512])
                dve_step(dve_last)
            for t in (1, 2):
                dve_last = dve.bn_aggr(small[:, 2 * t:2 * t + 2], stats[:, t, :, :])
            dve_last.then_inc(var_ready, 1)
            reciprocal_of(dve, mean_var[:, :, 1], root)
            for t in (1, 2):
                dve_step(dve.tensor_scalar(x_nat[:, t, :], x_nat[:, t, :], small[:, 2 * t:2 * t + 1],
                                           small[:, 2 * t + 1:2 * t + 2], ALU.subtract, ALU.mult))
                dve_step(dve.tensor_tensor(x_nat[:, t, :], x_nat[:, t, :], norm_rows[:, k % 2, 0, :], ALU.mult))
                dve.tensor_tensor(x_nat[:, t, :], x_nat[:, t, :], norm_rows[:, k % 2, 1, :], ALU.add).then_inc(
                    normed, 1)

        block.scalar(lambda act: sqrt_of(act, mean_var[:, :, 1], 1.0, LN_EPS, root))
        if last:
            return

        @block.tensor
        def _(pe):
            transposes_pe(FJ[name], (1, 2), lambda t: x_nat[:, t, :], lambda t: pe.wait_ge(normed, t))

        @block.scalar
        def _(act):
            transposes_out(FJ[name], (1, 2), xT)

    def project_natural(first, u0, lhs, tiles, k_chunks, bias=None):
        j = first
        for half in range(2):
            unit_ready(u0 + half)
            for t in tiles:
                n, at = TILE_N[t], TILE_AT[t]
                take_bank(j)
                pairs = [(lhs[:, k, at:at + n], slot_k(u0 + half)[:, k, :]) for k in range(k_chunks)]
                if bias is not None:
                    pairs.append((ones[0:1, 0:n], bias[:, half * 512:half * 512 + 512]))
                products(bank(j)[0:n, :], pairs).then_inc(job_done, 1)
                j += 1

    def project_turned(first, parts, turned, tiles=(0, 1, 2)):
        for c in range(KC):
            take_bank(first + c)
            for units_of_part in parts:
                unit_ready(units_of_part[c // 4])
            products(bank(first + c)[:, 0:L],
                     [(slot_k(part[c // 4])[:, k, (c % 4) * P:(c % 4) * P + P], part[2][:, k, :])
                      for part in parts for k in range(KC)]).then_inc(job_done, 1)
        j = first + KC
        for half in range(2):
            all_read_out(nc.tensor, first + 4 * half + 4)
            for t in tiles:
                n, at = TILE_N[t], TILE_AT[t]
                take_bank(j)
                for c in range(4):
                    last = nc.tensor.transpose(bank(j)[0:n, c * P:c * P + P], turned[:, 4 * half + c, at:at + n],
                                               ident[:, :])
                last.then_inc(job_done, 1)
                j += 1

    def turned_in(first, turned, function=ACT.Copy):
        for c in range(KC):
            job_ready(nc.scalar, first + c)
            nc.scalar.activation(turned[:, c, :], bank(first + c)[:, 0:L], function).then_inc(
                bank_free[(first + c) % BANKS], 1)

    def add_residual(first, tiles=(1, 2)):
        j = first
        for half in range(2):
            for t in tiles:
                job_ready(nc.vector, j)
                xs = x_nat[:, t, half * 512:half * 512 + 512]
                ins = nc.vector.scalar_tensor_tensor(xs, xs, ALPHA, bank(j), ALU.mult, ALU.add)
                ins.then_inc(bank_free[j % BANKS], 1)
                j += 1
        return ins

    rows = carve(0, 4, P)
    flip = carve(14500, P)
    lam_rows, subln_rows = carve(14628, 4, HD), carve(14884, 2 * HD)
    b_pw2 = arena[0:1, 8000:8000 + D]
    buckets = arena[0:N_BUCKETS, 9100:9100 + 3 * P]
    by_distance = arena[0:HEADS, 9500:9500 + 3 * P]
    inputs_loaded = sem("inputs_loaded")
    INPUT_DMAS = 12
    rel_written = sem("rel_written")
    rows_cleared = sem("rows_cleared")

    @stage
    def constants():
        @block.gpsimd
        def _(pool):
            pool.memset(rows[:, :, :], 0.0).then_inc(rows_cleared, 1)
            pool_step(pool.memset(ident[:, :], 0.0))
            pool_step(pool.affine_select(out=ident[:, :], in_=ident[:, :], compare_op=ALU.not_equal, fill=1.0, base=0,
                                         pattern=[[-1, P]], channel_multiplier=1))
            pool_step(pool.memset(ones[:, :], 1.0))
            pool_step(pool.memset(flip, 0.0))
            pool_step(pool.affine_select(out=flip, in_=flip, compare_op=ALU.not_equal, fill=1.0,
                                         base=1 - P, pattern=[[1, P]], channel_multiplier=1))
            pool_step(pool.memset(by_distance, MASKED))
            pool_step(pool.memset(upto[:, :], 1.0))
            pool_step(pool.affine_select(out=upto[:, :], in_=upto[:, :], compare_op=ALU.is_ge, fill=0.0,
                                         base=0, pattern=[[1, P]], channel_multiplier=-1))
            pool_step(pool.memset(neg_ones[:, :], -1.0))
            pool_step(pool.affine_select(out=neg_from[:, :], in_=neg_ones[:, :], compare_op=ALU.is_ge, fill=0.0,
                                         base=0, pattern=[[-1, P]], channel_multiplier=1))
            pool_step(pool.memset(eps_cols[:, 0:1], LN_EPS))
            pool_step(pool.memset(eps_cols[:, 1:2], EPS))
            pool.nop().then_inc(consts_made, 1)

        @block.scalar
        def _(act):
            act.wait_ge(rows_cleared, 1)
            for tile, parts in enumerate(VEC_ROWS):
                at = 0
                for name, first, n in parts:
                    src = a[name]
                    src = src.rearrange("a b (c p) -> (a b c) p" if len(src.shape) == 3 else "a (c p) -> (a c) p", p=P)
                    act.dma_start(rows[at:at + n, tile, :], src[first:first + n, :]).then_inc(consts_loaded, 16)
                    at += n
            act.nop().then_inc(rows_sent, 1)
            act.dma_start(router_w[:, :, :], a["router_w"].rearrange("(k p) n -> p k n", p=P)).then_inc(
                inputs_loaded, 16)
            act.dma_start(router_b[:, :], a["router_bias"].partition_broadcast(P)).then_inc(inputs_loaded, 16)
            act.dma_start(b_pw2, a["a_b_pw2"]).then_inc(inputs_loaded, 16)
            for n, name in enumerate(("ssd_dt_bias_2", "ssd_a_log_2", "ssd_d_2")):
                act.dma_start(ssd_rows[:, n, :], a[name][0].partition_broadcast(P)).then_inc(inputs_loaded, 16)
            act.dma_start(w_dt[:, :, :], a["w_in_2"][0][:, OFF_DT:OFF_Q].rearrange("(k p) n -> p k n", p=P),
                          ).then_inc(inputs_loaded, 16)
            act.dma_start(x_nat[0:META, 0, :], a["meta_tokens_2"]).then_inc(inputs_loaded, 16)
            act.dma_start(lam_rows[:, :, :], a["b_lambda"][0].partition_broadcast(P)).then_inc(inputs_loaded, 16)
            act.dma_start(subln_rows, a["b_subln_g"][0].partition_broadcast(P)).then_inc(inputs_loaded, 16)
            act.dma_start(rel_w[:, :], a["rel_bias"]).then_inc(inputs_loaded, 16)
            act.dma_start(buckets, a["buckets"]).then_inc(inputs_loaded, 16)
            load_norm(0, a["ln_mix_g"][0], a["ln_mix_b"][0])
            job_ready(act, FJ["vec"])
            act.activation(vec[:, :], bank(FJ["vec"]), ACT.Copy).then_inc(bank_free[FJ["vec"] % BANKS], 1)
            transposes_out(FJ["conv_xT"], (1, 2), xT)

        @block.tensor
        def _(pe):
            pe.wait_ge(consts_made, 1)
            pe.wait_ge(consts_loaded, 16 * sum(len(r) for r in VEC_ROWS))
            take_bank(FJ["vec"])
            for tile in range(4):
                last = pe.transpose(bank(FJ["vec"])[:, tile * P:tile * P + P], rows[:, tile, :], ident[:, :])
            last.then_inc(job_done, 1)
            pe.wait_ge(x_loaded, 16)
            transposes_pe(FJ["conv_xT"], (1, 2), lambda t: x_nat[:, t, :])

    PAD = TAPS - 1
    glu = carve(0, KC, PAD + SEQ)
    conv = carve(2400, KC, SEQ)
    squares = carve(4500, KC, SEQ)
    sig = carve(6600, 2, SEQ)
    mean_b, rstd_b = carve(7200, SEQ), carve(7500, SEQ)
    sig_ready, glu_ready, conv_step = sem("sig_ready"), sem("glu_ready"), sem("conv_step")
    DIAGS = 30
    diags = carve(9900, DIAGS, P)
    pool_term = carve(13900, 2, SEQ)
    POOL_CHUNK, DVE_CHUNKS, PE_CHUNKS = 0, (range(1, 3), range(3, 6)), range(6, KC)
    diag_made, taps_used, pool_tap = sem("diag_made"), sem("taps_used"), sem("pool_tap")
    term_ready = sem("pool_term_ready")

    def diagonal(eng, n):
        if n >= DIAGS:
            m = n - DIAGS
            if m % TAPS == TAPS - 1:
                job_ready(eng, FJ["conv"] + m // TAPS)
            else:
                eng.wait_ge(taps_used, m + 1 - m // TAPS)
        chunk = PE_CHUNKS[n // TAPS]
        eng.activation(diags[:, n % DIAGS, :], ident[:, :], ACT.Copy,
                       scale=column("a_w_dw", (n % TAPS) * KC + chunk)).then_inc(diag_made, 1)

    conv_ready, centred, squared, conv_normed, act_ready = (
        sem("conv_ready"), sem("centred"), sem("squared"), sem("conv_normed"), sem("conv_activated"))

    @stage
    def conformer():
        root = next_sqrt()

        @block.tensor
        def _(pe):
            for n in range(KC):
                j, pair = FJ["glu"] + n, n // 4
                take_bank(j)
                for side in range(2):
                    u = 2 * pair + side
                    unit_ready(u)
                    last = products(bank(j)[:, side * SEQ:side * SEQ + SEQ],
                                    [(slot_k(u)[:, k, (n % 4) * P:(n % 4) * P + P], xT[:, k, META:L])
                                     for k in range(KC)])
                last.then_inc(job_done, 1)
            pe.wait_ge(inputs_loaded, INPUT_DMAS * 16)
            take_bank(FJ["iota"])
            products(bank(FJ["iota"])[:, 0:P], [(ones[:, :], upto[:, :])]).then_inc(job_done, 1)
            take_bank(FJ["relb"])
            products(bank(FJ["relb"])[0:HEADS, 0:3 * P], [(rel_w[:, :], buckets)]).then_inc(job_done, 1)
            for i, c in enumerate(PE_CHUNKS):
                j = FJ["conv"] + i
                take_bank(j)
                pe.wait_ge(glu_ready, c + 1)
                for tap in range(TAPS):
                    n = i * TAPS + tap
                    pe.wait_ge(diag_made, n + 1)
                    last = pe.matmul(bank(j)[:, 0:SEQ], diags[:, n % DIAGS, :], glu[:, c, tap:tap + SEQ],
                                     start=(tap == 0), stop=(tap == TAPS - 1))
                    last.then_inc(taps_used if tap < TAPS - 1 else job_done, 1)
            j = FJ["conv_mean"]
            all_read_out(pe, j)
            pe.wait_ge(conv_ready, 1)
            pe.wait_ge(pool_tap, TAPS)
            products(bank(j)[:, 0:SEQ], [(ones[:, :], conv[:, c, :]) for c in range(KC)]).then_inc(job_done, 1)
            j = FJ["conv_var"]
            take_bank(j)
            pe.wait_ge(squared, 1)
            products(bank(j)[:, 0:SEQ], [(ones[:, :], squares[:, c, :]) for c in range(KC)]).then_inc(job_done, 1)
            pe.wait_ge(act_ready, KC)
            j = FJ["pw2"]
            for half in range(2):
                unit_ready(unit_at["pw2"] + half)
                for t in (0, 1):
                    take_bank(j)
                    pairs = [(conv[:, k, t * P:t * P + P], slot_k(unit_at["pw2"] + half)[:, k, :]) for k in range(KC)]
                    pairs.append((ones[0:1, :], b_pw2[:, half * 512:half * 512 + 512]))
                    products(bank(j), pairs).then_inc(job_done, 1)
                    j += 1

        @block.gpsimd
        def _(pool):
            c = POOL_CHUNK
            pool.wait_ge(glu_ready, c + 1)
            for tap in range(TAPS):
                src, w = glu[:, c, tap:tap + SEQ], column("a_w_dw", tap * KC + c)
                if tap == 0:
                    pool.tensor_scalar(conv[:, c, :], src, w, column("a_b_dw", c), ALU.mult, ALU.add).then_inc(
                        pool_tap, 1)
                    continue
                if tap >= 3:
                    pool.wait_ge(pool_tap, tap - 1)
                term = pool_term[:, tap % 2, :]
                pool.tensor_scalar(term, src, w, None, ALU.mult).then_inc(term_ready, 1)
                pool.wait_ge(term_ready, tap)
                pool.wait_ge(pool_tap, tap)
                pool.tensor_tensor(conv[:, c, :], conv[:, c, :], term, ALU.add).then_inc(pool_tap, 1)

        @block.scalar
        def _(act):
            for n in range(DIAGS):
                diagonal(act, n)
            for n in range(KC):
                j = FJ["glu"] + n
                job_ready(act, j)
                if n >= 2:
                    act.wait_ge(glu_ready, n - 1)
                act.activation(sig[:, n % 2, :], bank(j)[:, SEQ:2 * SEQ], ACT.Sigmoid,
                               bias=column("a_b_pw1", KC + n)).then_inc(sig_ready, 1)
            job_ready(act, FJ["iota"])
            act.activation(counting[:, :], bank(FJ["iota"])[:, 0:P], ACT.Copy).then_inc(
                bank_free[FJ["iota"] % BANKS], 1)
            job_ready(act, FJ["relb"])
            act.activation(by_distance[:, 0:SEQ], bank(FJ["relb"])[0:HEADS, 0:SEQ], ACT.Copy).then_inc(
                bank_free[FJ["relb"] % BANKS], 1)
            act.wait_ge(bank_free[FJ["relb"] % BANKS], FJ["relb"] // BANKS + 1)
            act.dma_start(rel_scratch, by_distance).then_inc(rel_written, 16)

            def taps_out(i):
                j, c = FJ["conv"] + i, PE_CHUNKS[i]
                job_ready(act, j)
                act.activation(conv[:, c, :], bank(j)[:, 0:SEQ], ACT.Identity, bias=column("a_b_dw", c)).then_inc(
                    bank_free[j % BANKS], 1)

            for n in range(DIAGS, len(PE_CHUNKS) * TAPS):
                if n >= TAPS and n % TAPS == 12:
                    taps_out(n // TAPS - 1)
                diagonal(act, n)
            taps_out(len(PE_CHUNKS) - 1)
            act.wait_ge(rel_written, 16)
            act.wait_ge(centred, 1)
            act.activation(squares[:, :, :], conv[:, :, :], ACT.Square).then_inc(squared, 1)
            sqrt_of(act, rstd_b, 1.0 / D, LN_EPS, root)
            act.wait_ge(conv_normed, 1)
            for c in range(KC):
                act.activation(conv[:, c, :], conv[:, c, :], ACT.Silu, bias=column("a_ln_b", c),
                               scale=column("a_ln_g", c)).then_inc(act_ready, 1)

        @block.vector
        def _(dve):
            dve_step(dve.memset(glu[:, :, 0:PAD], 0.0))

            def gated(n):
                j = FJ["glu"] + n
                dve.wait_ge(sig_ready, n + 1)
                dve.scalar_tensor_tensor(glu[:, n, PAD:PAD + SEQ], bank(j)[:, 0:SEQ], column("a_b_pw1", n),
                                         sig[:, n % 2, :], ALU.add, ALU.mult).then_inc(glu_ready, 1)
                dve.wait_ge(glu_ready, n + 1)
                dve.nop().then_inc(bank_free[j % BANKS], 1)

            for n in range(3):
                gated(n)
            n, next_gated = 0, 3
            for chunks in DVE_CHUNKS:
                while next_gated <= chunks[-1]:
                    gated(next_gated)
                    next_gated += 1
                for tap in range(TAPS):
                    if tap % 10 == 9 and next_gated < KC:
                        gated(next_gated)
                        next_gated += 1
                    for i, c in enumerate(chunks):
                        src = glu[:, c, tap:tap + SEQ]
                        w = column("a_w_dw", tap * KC + c)
                        if tap == 0:
                            ins = dve.tensor_scalar(conv[:, c, :], src, w, column("a_b_dw", c), ALU.mult, ALU.add)
                        else:
                            dve.wait_ge(conv_step, n - len(chunks) + 1)
                            ins = dve.scalar_tensor_tensor(conv[:, c, :], src, w, conv[:, c, :], ALU.mult, ALU.add)
                        ins.then_inc(conv_step, 1)
                        n += 1
            dve.wait_ge(conv_step, n)
            dve.nop().then_inc(conv_ready, 1)
            j = FJ["conv_mean"]
            job_ready(dve, j)
            ins = dve.tensor_scalar(mean_b, bank(j)[:, 0:SEQ], 1.0 / D, None, ALU.mult)
            dve_step(ins)
            dve.nop().then_inc(bank_free[j % BANKS], 1)
            dve.tensor_tensor(conv[:, :, :], conv[:, :, :], mean_b.unsqueeze(1).broadcast_to([P, KC, SEQ]),
                              ALU.subtract).then_inc(centred, 1)
            j = FJ["conv_var"]
            job_ready(dve, j)
            dve.tensor_copy(rstd_b, bank(j)[:, 0:SEQ]).then_inc(var_ready, 1)
            reciprocal_of(dve, rstd_b, root)
            dve.nop().then_inc(bank_free[j % BANKS], 1)
            dve.tensor_tensor(conv[:, :, :], conv[:, :, :], rstd_b.unsqueeze(1).broadcast_to([P, KC, SEQ]),
                              ALU.mult).then_inc(conv_normed, 1)
            add_residual(FJ["pw2"])

    normed = [sem(f"normed{k}") for k in range(4)]

    @stage
    def mix_norm0():
        layer_norm(0, "mix0_xT", normed[0])

    aff, sel = carve(0, 2, EXPERTS), carve(40, 2, EXPERTS)
    beats = carve(80, 2, EXPERTS)
    cmp = carve(120, 2, GROUPS)
    group_score, group_lost = carve(140, 2, GROUPS), carve(150, 2, GROUPS)
    total = carve(160, 2)
    pair = carve(190, 2, GROUPS)
    member_rank, slot_of = carve(175, 3, GROUPS), carve(4640 - 60, 2, GROUPS)
    silu_g, hid, hidT = carve(200, 2, DE), carve(1230, 2, DE), carve(2260, 2, DE)
    tokens = carve(3290, KC, P)
    seats = carve(4320, 2, P)
    slot_cell, gate_cell, seat_gate = carve(4590, 2), carve(4592, 2, PER_GROUP), carve(4600, PER_GROUP)
    base = carve(4640, 2, D)
    y_all = carve(6690, GROUPS, D)
    seatsT = carve(10790, GROUPS, 2 * P)
    over_w, over_y, over_count = carve(6690, 4096), carve(11820, D), carve(12850, P)
    over_slots = carve(12980, 2, EXPERTS)
    over_hi = carve(13020, P)

    def route(layer):
        aff_ready, won_ready, ranks_out = sem(f"aff_ready{layer}"), sem(f"won_ready{layer}"), sem(f"ranks_out{layer}")
        J = FJ[f"route{layer}"]

        @block.scalar
        def _(act):
            job_ready(act, J)
            act.activation(aff[:, :, :], bank(J)[:, 0:2 * EXPERTS].rearrange("p (t e) -> p t e", t=2),
                           ACT.Sigmoid).then_inc(aff_ready, 1)
            act.activation(base[:, :, :], x_nat[:, 1:3, :], ACT.Copy, scale=ALPHA)

        @block.vector
        def _(dve):
            if layer == 0:
                dve.wait_ge(inputs_loaded, INPUT_DMAS * 16)
            dve.wait_ge(aff_ready, 1)
            dve.tensor_tensor(sel, aff, router_b[:, :].unsqueeze(1).broadcast_to([P, 2, EXPERTS]),
                              ALU.add).then_inc(bank_free[J % BANKS], 1)
            dve.wait_ge(bank_free[J % BANKS], J // BANKS + 1)
            dve_step(dve.memset(beats, 0.0))
            sg = sel.rearrange("p t (g e) -> p t g e", g=GROUPS)
            bg = beats.rearrange("p t (g e) -> p t g e", g=GROUPS)
            first = True
            for hi in range(PER_GROUP):
                for lo in range(hi):
                    dve.tensor_tensor(pair, sg[:, :, :, lo], sg[:, :, :, hi], ALU.add)
                    dve_step(dve.tensor_tensor(cmp, sg[:, :, :, lo], sg[:, :, :, hi], ALU.is_ge))
                    if first:
                        dve.tensor_copy(group_score, pair)
                        first = False
                    else:
                        dve.tensor_tensor(group_score, group_score, pair, ALU.max)
                    dve.tensor_tensor(bg[:, :, :, hi], bg[:, :, :, hi], cmp, ALU.add)
                    dve_step(dve.scalar_tensor_tensor(bg[:, :, :, lo], bg[:, :, :, lo], 1.0, cmp, ALU.add,
                                                      ALU.subtract))
            dve_step(dve.memset(group_lost, 0.0))
            for hi in range(GROUPS):
                for lo in range(hi):
                    s_lo, s_hi = group_score[:, :, lo:lo + 1], group_score[:, :, hi:hi + 1]
                    c1 = cmp[:, :, 0:1]
                    dve_step(dve.tensor_tensor(c1, s_lo, s_hi, ALU.is_ge))
                    dve.tensor_tensor(group_lost[:, :, hi:hi + 1], group_lost[:, :, hi:hi + 1], c1, ALU.add)
                    dve_step(dve.scalar_tensor_tensor(group_lost[:, :, lo:lo + 1], group_lost[:, :, lo:lo + 1], 1.0,
                                                      c1, ALU.add, ALU.subtract))
            dve.tensor_scalar(group_lost, group_lost, 0.5, None, ALU.is_lt).then_inc(won_ready, 1)
            dve.wait_ge(won_ready, 1)
            won = group_lost
            dve_step(dve.tensor_scalar(beats, beats, 1.5, None, ALU.is_lt))
            dve_step(dve.tensor_tensor(bg, bg, won.unsqueeze(3).broadcast_to([P, 2, GROUPS, PER_GROUP]), ALU.mult))
            dve_step(dve.tensor_tensor(gates[:, :, :], beats, aff, ALU.mult))
            dve_step(dve.tensor_reduce(total, gates[:, :, :], AX_X, ALU.add))
            dve_step(dve.reciprocal(total, total))
            dve_step(dve.tensor_tensor(gates[:, :, :], gates[:, :, :],
                                       total.unsqueeze(2).broadcast_to([P, 2, EXPERTS]), ALU.mult))
            job_ready(dve, J + 1)
            dve.tensor_copy(member_rank, bank(J + 1)[:, 0:3 * GROUPS].rearrange(
                "p (t g) -> p t g", t=3)).then_inc(bank_free[(J + 1) % BANKS], 1)
            dve.wait_ge(bank_free[(J + 1) % BANKS], (J + 1) // BANKS + 1)
            dve_step(dve.tensor_tensor(slot_of, won, member_rank[:, 0:2, :], ALU.mult))
            dve_step(dve.tensor_reduce(total[:, 0:1], member_rank[:, 2, :], AX_X, ALU.max))
            dve_step(dve.tensor_copy(over_flag[:, :], total[:, 0:1]))

        @block.tensor
        def _(pe):
            take_bank(J)
            for t in (1, 2):
                at = TILE_AT[t]
                last = products(bank(J)[:, (t - 1) * EXPERTS:t * EXPERTS],
                                [(xT[:, k, at:at + P], router_w[:, k, :]) for k in range(KC)])
            last.then_inc(job_done, 1)
            take_bank(J + 1)
            pe.wait_ge(won_ready, 1)
            won = group_lost
            products(bank(J + 1)[:, 0:GROUPS], [(upto[:, :], won[:, 0, :])])
            products(bank(J + 1)[:, GROUPS:2 * GROUPS], [(ones[:, :], won[:, 0, :]), (upto[:, :], won[:, 1, :])])
            products(bank(J + 1)[:, 2 * GROUPS:3 * GROUPS],
                     [(ones[:, :], won[:, 0, :]), (ones[:, :], won[:, 1, :])]).then_inc(job_done, 1)

    def gather(dst_at, tokens_dst, sources=seats):
        for c in range(4):
            k = dst_at * 4 + c
            last = products(tokens_dst[:, c * P:c * P + P],
                            [(x_nat[:, t + 1, k * P:k * P + P], sources[:, t, :]) for t in range(2)])
        return last

    def overflow(layer):
        names = ("w_free", "w_loaded", "cell", "seated", "gathered", "tokens", "silu", "hid", "turned", "hidT", "y",
                 "scattered", "added")
        (w_free, w_loaded, cell_ready, seated, gathered, tokens_out, silu_out, hid_out, turned, hidT_out, y_out,
         scattered, added) = (sem(f"over_{x}{layer}") for x in names)

        def where_over(eng, body):
            count = eng.value_load(over_flag[0:1, 0:1], min_val=0, max_val=SEQ)
            with eng.If(count > P):
                body()

        @block.tensor
        def _(pe):
            def body():
                pe.nop().then_inc(w_free, 1)
                with pe.Fori(0, EXPERTS) as i:
                    pe.wait_ge(seated, i + 1)
                    for half in range(2):
                        gather(half, psum[:, half, :])
                    products(psum[:, 2, 0:1], [(seats[:, t, :], gate_cell[:, t, 0:1]) for t in range(2)])
                    for t in range(2):
                        last = pe.transpose(psum[:, 3, t * P:t * P + P], seats[:, t, :], ident[:, :])
                    last.then_inc(gathered, 1)
                    pe.wait_ge(tokens_out, i + 1)
                    for n in range(2):
                        pe.wait_ge(w_loaded, i * 48 + 16 * (n + 1))
                        w = over_w.rearrange("p (k n) -> p k n", n=512)
                        products(psum[:, n, :], [(tokens[:, k, :], w[:, k, :]) for k in range(KC)]).then_inc(w_free, 1)
                    pe.wait_ge(hid_out, i + 1)
                    for k in range(DE // P):
                        last = pe.transpose(psum[:, 2, k * P:k * P + P], hid[:, 0, k * P:k * P + P], ident[:, :])
                    last.then_inc(turned, 1)
                    pe.wait_ge(hidT_out, i + 1)
                    pe.wait_ge(w_loaded, i * 48 + 48)
                    w = over_w.rearrange("p (k n) -> p k n", n=D)
                    for half in range(2):
                        last = products(psum[:, 4 + half, :],
                                        [(hidT[:, 0, k * P:k * P + P], w[:, k, half * 512:half * 512 + 512])
                                         for k in range(DE // P)])
                    last.then_inc(w_free, 1)
                    pe.wait_ge(y_out, i + 1)
                    for t in range(2):
                        for half in range(2):
                            last = products(psum[:, 4 + 2 * t + half, :],
                                            [(seatsT[:, 0, t * P:t * P + P], over_y[:, half * 512:half * 512 + 512])])
                    last.then_inc(scattered, 1)

            where_over(pe, body)

        @block.scalar
        def _(act):
            def body():
                with act.Fori(0, EXPERTS) as i:
                    def load(n, name, width):
                        act.wait_ge(w_free, i * 3 + n + 1)
                        src = a[name][layer, bass.ds(i, 1)].rearrange("a (k p) n -> p (a k) n", p=P)
                        act.dma_start(over_w.rearrange("p (k n) -> p k n", n=width), src).then_inc(w_loaded, 16)

                    load(0, "moe_w_gate", DE)
                    act.wait_ge(gathered, i + 1)
                    for half in range(2):
                        act.activation(tokens[:, 4 * half:4 * half + 4, :],
                                       psum[:, half, :].rearrange("p (c s) -> p c s", c=4), ACT.Copy)
                    act.activation(seat_gate[:, 0:1], psum[:, 2, 0:1], ACT.Copy)
                    act.activation(seatsT[:, 0, :], psum[:, 3, 0:2 * P], ACT.Copy).then_inc(tokens_out, 1)
                    load(1, "moe_w_up", DE)
                    act.activation(silu_g[:, 0, :], psum[:, 0, :], ACT.Silu).then_inc(silu_out, 1)
                    load(2, "moe_w_down", D)
                    act.wait_ge(turned, i + 1)
                    act.activation(hidT[:, 0, :], psum[:, 2, :], ACT.Copy).then_inc(hidT_out, 1)
                    act.wait_ge(w_free, i * 3 + 4)
                    act.activation(over_y.rearrange("p (b n) -> p b n", b=2), psum[:, 4:6, :], ACT.Copy).then_inc(
                        y_out, 1)

            where_over(act, body)

        @block.vector
        def _(dve):
            def body():
                dve.tensor_copy(over_slots.rearrange("p t (g e) -> p t g e", g=GROUPS),
                                slot_of.unsqueeze(3).broadcast_to([P, 2, GROUPS, PER_GROUP]))
                dve.tensor_scalar(over_hi, counting[:, :], float(P), None, ALU.add).then_inc(added, 1)
                dve.wait_ge(added, 1)
                with dve.Fori(0, EXPERTS) as i:
                    dve.tensor_copy(slot_cell.unsqueeze(2), over_slots[:, :, bass.ds(i, 1)])
                    dve.tensor_copy(gate_cell[:, :, 0:1], gates[:, :, bass.ds(i, 1)]).then_inc(cell_ready, 1)
                    dve.wait_ge(cell_ready, i + 1)
                    for t in range(2):
                        ins = dve.tensor_scalar(seats[:, t, :], over_hi, slot_cell[:, t:t + 1], None, ALU.is_equal)
                    ins.then_inc(seated, 1)
                    dve.wait_ge(w_free, i * 3 + 3)
                    dve.wait_ge(silu_out, i + 1)
                    dve.scalar_tensor_tensor(hid[:, 0, :], psum[:, 1, :], seat_gate[:, 0:1], silu_g[:, 0, :],
                                             ALU.mult, ALU.mult).then_inc(hid_out, 1)
                    dve.wait_ge(scattered, i + 1)
                    for t in range(2):
                        for half in range(2):
                            part = base[:, t, half * 512:half * 512 + 512]
                            ins = dve.tensor_tensor(part, part, psum[:, 4 + 2 * t + half, :], ALU.add)
                    ins.then_inc(added, 1)
                    dve.wait_ge(added, i + 2)

            where_over(dve, body)

    def experts(layer):
        B = FJ[f"moe{layer}"]
        U = unit_at[f"moe{layer}"]
        cell_ready, seats_ready, sum_free = (sem(f"cell_ready{layer}"), sem(f"seats_ready{layer}"),
                                             sem(f"sum_free{layer}"))
        SUM = (BANKS, BANKS + 1)
        TS = FJ[f"moe{layer}"] + 64

        def job(kind, e=0, g=0):
            return group_first(layer, g) + IN_GROUP[kind, e]

        def last_turn():
            return group_first(layer, GROUPS - 1) + IN_GROUP["X", 0]

        def done(eng, j, i=0):
            eng.wait_ge(job_done, j + 1 + i * GROUP_JOBS)

        def read_out(eng, j, i=0):
            eng.wait_ge(bank_free[j % BANKS], j // BANKS + 1 + i * (GROUP_JOBS // BANKS))

        def next_group_jobs(g):
            if g == 0:
                return B, B + 1, B + 2, B + 3
            first = group_first(layer, g - 1)
            return tuple(first + IN_GROUP[x] for x in (("X", 0), ("X", 1), ("R", 0), ("S", 0)))

        @block.vector
        def _(dve):
            def seat(i, jobs):
                one = slice(i, i + 1) if isinstance(i, int) else bass.ds(i, 1)
                four = slice(PER_GROUP * i, PER_GROUP * i + PER_GROUP) if isinstance(i, int) else bass.ds(
                    i * PER_GROUP, PER_GROUP)
                dve.tensor_copy(slot_cell.unsqueeze(2), slot_of[:, :, one])
                dve.tensor_copy(gate_cell[:, :, :], gates[:, :, four]).then_inc(cell_ready, 1)
                dve.wait_ge(cell_ready, i + 1)
                for t in range(2):
                    ins = dve.tensor_scalar(seats[:, t, :], counting[:, :], slot_cell[:, t:t + 1], None, ALU.is_equal)
                ins.then_inc(seats_ready, 1)

            def hidden(e, i, g=0):
                jg, ju = job("G", e, g), job("U", e, g)
                read_out(dve, jg, i)
                done(dve, ju, i)
                dve.scalar_tensor_tensor(hid[:, e % 2, :], bank(ju), seat_gate[:, e:e + 1], silu_g[:, e % 2, :],
                                         ALU.mult, ALU.mult).then_inc(bank_free[ju % BANKS], 1)

            def gates_out(jr, i=0):
                done(dve, jr, i)
                dve.tensor_copy(seat_gate, bank(jr)[:, 0:PER_GROUP]).then_inc(bank_free[jr % BANKS], 1)
                read_out(dve, jr, i)

            seat(0, None)
            gates_out(B + 2)
            with dve.Fori(0, GROUPS - 1) as i:
                dve.wait_ge(job_done, group_first(layer, 0) + i * GROUP_JOBS)
                seat(i + 1, None)
                for e in range(PER_GROUP):
                    hidden(e, i)
                read_out(dve, job("U", 3), i)
                gates_out(job("R"), i)
            for e in range(PER_GROUP):
                hidden(e, 0, GROUPS - 1)
            j = TS
            for t in range(2):
                for half in range(2):
                    job_ready(dve, j)
                    dve.tensor_tensor(x_nat[:, t + 1, half * 512:half * 512 + 512],
                                      base[:, t, half * 512:half * 512 + 512], bank(j), ALU.add).then_inc(
                                          bank_free[j % BANKS], 1)
                    j += 1

        @block.scalar
        def _(act):
            def silu(e, i, g=0):
                j = job("G", e, g)
                done(act, j, i)
                act.activation(silu_g[:, e % 2, :], bank(j), ACT.Silu).then_inc(bank_free[j % BANKS], 1)

            def turned(j, e, i):
                done(act, j, i)
                act.activation(hidT[:, e % 2, :], bank(j), ACT.Copy).then_inc(bank_free[j % BANKS], 1)

            def gathered(jobs, g, i=0):
                for half in range(2):
                    j = jobs[half]
                    done(act, j, i)
                    act.activation(tokens[:, 4 * half:4 * half + 4, :], bank(j).rearrange("p (c s) -> p c s", c=4),
                                   ACT.Copy).then_inc(bank_free[j % BANKS], 1)
                j = jobs[3]
                done(act, j, i)
                dst = seatsT[:, g, :] if isinstance(g, int) else seatsT[:, bass.ds(g, 1), :]
                src = bank(j)[:, 0:2 * P] if isinstance(g, int) else bank(j)[:, 0:2 * P].unsqueeze(1)
                act.activation(dst, src, ACT.Copy).then_inc(bank_free[j % BANKS], 1)

            def summed(g):
                act.wait_ge(down_done[layer], g * PER_GROUP + PER_GROUP)
                dst = y_all[:, g, :] if isinstance(g, int) else y_all[:, bass.ds(g, 1), :]
                src = psum[:, SUM[0]:SUM[1] + 1, :].rearrange("p b n -> p (b n)")
                act.activation(dst, src if isinstance(g, int) else src.unsqueeze(1), ACT.Copy).then_inc(sum_free, 1)

            act.nop().then_inc(sum_free, 1)
            gathered(next_group_jobs(0), 0)
            with act.Fori(0, GROUPS - 1) as i:
                silu(0, i)
                for e in range(1, PER_GROUP):
                    silu(e, i)
                    turned(job("T", e - 1), e - 1, i)
                gathered(next_group_jobs(1), i + 1, i)
                turned(job("T", 3), 3, i)
                summed(i)
            g = GROUPS - 1
            silu(0, 0, g)
            for e in range(1, PER_GROUP):
                silu(e, 0, g)
                turned(job("T", e - 1, g), e - 1, 0)
            turned(last_turn(), 3, 0)
            summed(g)

        @block.tensor
        def _(pe):
            def free(j, i=0):
                pe.wait_ge(bank_free[j % BANKS], j // BANKS + i * (GROUP_JOBS // BANKS))

            def wait_unit(u, i):
                pe.wait_ge(slot_loaded[u % RING], loads_of(u) + i * (16 * 3 * PER_GROUP // RING))

            def fetch(jobs, n, i=0):
                pe.wait_ge(seats_ready, n)
                for half in range(2):
                    free(jobs[half], i)
                    gather(half, bank(jobs[half])).then_inc(job_done, 1)
                free(jobs[2], i)
                products(bank(jobs[2])[:, 0:PER_GROUP], [(seats[:, t, :], gate_cell[:, t, :]) for t in range(2)]
                         ).then_inc(job_done, 1)
                free(jobs[3], i)
                for t in range(2):
                    last = pe.transpose(bank(jobs[3])[:, t * P:t * P + P], seats[:, t, :], ident[:, :])
                last.then_inc(job_done, 1)

            def up_gate(kind, e, i, g=0):
                j = job(kind, e, g)
                u = U + 3 * (PER_GROUP * g + e) + (kind == "U")
                free(j, i)
                wait_unit(u, i)
                products(bank(j), [(tokens[:, k, :], slot_k(u)[:, k, :]) for k in range(KC)]).then_inc(job_done, 1)

            def turn(j, e, i, g=0):
                free(j, i)
                read_out(pe, job("U", e, g), i)
                for k in range(DE // P):
                    last = pe.transpose(bank(j)[:, k * P:k * P + P], hid[:, e % 2, k * P:k * P + P], ident[:, :])
                last.then_inc(job_done, 1)

            def down(jt, e, i, g=0):
                u = U + 3 * (PER_GROUP * g + e) + 2
                wait_unit(u, i)
                read_out(pe, jt, i)
                if e == 0:
                    pe.wait_ge(sum_free, g + 1 + i)
                for half in range(2):
                    for k in range(DE // P):
                        last = pe.matmul(psum[:, SUM[half], :], hidT[:, e % 2, k * P:k * P + P],
                                         slot_k(u, D)[:, k, half * 512:half * 512 + 512],
                                         start=(e == 0 and k == 0), stop=(e == PER_GROUP - 1 and k == DE // P - 1))
                last.then_inc(down_done[layer], 1)

            def group(i, g=0):
                first, second, _, _ = next_group_jobs(g)
                if isinstance(i, int):
                    read_out(pe, first), read_out(pe, second)
                up_gate("G", 0, i, g)
                up_gate("U", 0, i, g)
                for e in range(1, PER_GROUP):
                    up_gate("G", e, i, g)
                    turn(job("T", e - 1, g), e - 1, i, g)
                    up_gate("U", e, i, g)
                    down(job("T", e - 1, g), e - 1, i, g)

            fetch(next_group_jobs(0), 1)
            read_out(pe, B), read_out(pe, B + 1)
            with pe.Fori(0, GROUPS - 1) as i:
                group(i)
                fetch(next_group_jobs(1), i + 2, i)
                turn(job("T", 3), 3, i)
                down(job("T", 3), 3, i)
                read_out(pe, job("X", 0), i), read_out(pe, job("X", 1), i)
            g = GROUPS - 1
            group(0, g)
            turn(last_turn(), 3, 0, g)
            down(last_turn(), 3, 0, g)
            pe.wait_ge(sum_free, GROUPS + 1)
            j = TS
            for t in range(2):
                for half in range(2):
                    take_bank(j)
                    products(bank(j), [(seatsT[:, n, t * P:t * P + P], y_all[:, n, half * 512:half * 512 + 512])
                                       for n in range(GROUPS)]).then_inc(job_done, 1)
                    j += 1

    @stage
    def route0():
        route(0)

    @stage
    def overflow0():
        overflow(0)

    @stage
    def moe0():
        experts(0)

    @stage
    def route1():
        route(1)

    @stage
    def overflow1():
        overflow(1)

    @stage
    def moe1():
        experts(1)

    @stage
    def ffn_norm0():
        layer_norm(1, "ffn0_xT", normed[1])

    kT, qT = carve(0, KC, SEQ), carve(2048, KC, SEQ)
    v_nat = carve(4096, 2, D)
    bias = carve(6144, HEADS, SEQ)
    o_nat = carve(8192, 2, D)
    oT = carve(10240, KC, L)
    probs, mixed, mixedT = carve(12416, 2, 2, SEQ), carve(13440, 2, SEQ), carve(13952, 2, SEQ)
    neg_lam = small[:, 8:9]
    bias_loaded = sem("bias_loaded")
    lam_summed, lam_exp = sem("lam_summed"), sem("lam_exp")
    max_ready, probs_ready, mixed_ready, mixedT_ready, o_ready = (
        sem("max_ready"), sem("probs_ready"), sem("mixed_ready"), sem("mixedT_ready"), sem("o_ready"))
    o_squared, o_summed, o_normed = sem("o_squared"), sem("o_summed"), sem("o_normed")
    PAIRS = 2 * HEADS

    def att_jobs():
        order = {}
        for n in range(PAIRS + 2):
            for kind, m in (("scores", n), ("turn", n - 1), ("values", n - 2)):
                if 0 <= m < PAIRS:
                    order[kind, m] = FJ["att_heads"] + len(order)
        return order

    AJ = att_jobs()

    @stage
    def attention():
        root = next_sqrt()

        @block.tensor
        def _(pe):
            def channels(first, u0, src):
                for c in range(KC):
                    j = first + c
                    if c % 4 == 0:
                        unit_ready(u0 + c // 4)
                    take_bank(j)
                    products(bank(j)[:, 0:SEQ], [(slot_k(u0 + c // 4)[:, k, (c % 4) * P:(c % 4) * P + P],
                                                  src[:, k, META:L]) for k in range(KC)]).then_inc(job_done, 1)

            channels(FJ["att_k"], unit_at["w_k"], xT)
            project_natural(FJ["att_v"], unit_at["w_v"], xT, (1, 2), KC)
            channels(FJ["att_q"], unit_at["w_q"], xT)
            pe.wait_ge(bias_loaded, 16)
            all_read_out(pe, FJ["att_heads"])

            def scores(n):
                b, h = n // HEADS, n % HEADS
                keys = P * (b + 1)
                j = AJ["scores", n]
                take_bank(j)
                rows = slice(HD * (h % 2), HD * (h % 2) + HD)
                for comp in range(2):
                    c = 4 * comp + h // 2
                    pe.matmul(bank(j)[:, comp * SEQ:comp * SEQ + keys], flip, bias[:, h, SEQ - keys:SEQ],
                              start=True, stop=False)
                    last = pe.matmul(bank(j)[:, comp * SEQ:comp * SEQ + keys], qT[rows, c, b * P:b * P + P],
                                     kT[rows, c, 0:keys], start=False, stop=True)
                last.then_inc(job_done, 1)

            def turn(n):
                b = n // HEADS
                j = AJ["turn", n]
                take_bank(j)
                pe.wait_ge(mixed_ready, n + 1)
                for kb in range(b + 1):
                    last = pe.transpose(bank(j)[:, kb * P:kb * P + P], mixed[:, n % 2, kb * P:kb * P + P], ident[:, :])
                last.then_inc(job_done, 1)

            def values(n):
                b, h = n // HEADS, n % HEADS
                j = AJ["values", n]
                take_bank(j)
                pe.wait_ge(mixedT_ready, n + 1)
                products(bank(j)[:, 0:P], [(mixedT[:, n % 2, kb * P:kb * P + P], v_nat[:, kb, h * P:h * P + P])
                                           for kb in range(b + 1)]).then_inc(job_done, 1)

            for n in range(PAIRS + 2):
                if n < PAIRS:
                    scores(n)
                if 1 <= n <= PAIRS:
                    turn(n - 1)
                if n >= 2:
                    values(n - 2)
            pe.wait_ge(o_normed, 1)
            transposes_pe(FJ["att_T"], (1, 2), lambda t: o_nat[:, t - 1, :])
            all_read_out(pe, FJ["att_o"])
            project_natural(FJ["att_o"], unit_at["w_o"], oT, (1, 2), KC)

        @block.scalar
        def _(act):
            act.wait_ge(rel_written, 16)
            skewed = bass.AP(rel_scratch.tensor, 0, [[1, P], [3 * P, HEADS], [1, SEQ]])
            act.dma_start(bias, skewed).then_inc(bias_loaded, 16)
            for first, dst, scale in ((FJ["att_k"], kT, 1.0), (FJ["att_q"], qT, HD ** -0.5)):
                for c in range(KC):
                    j = first + c
                    job_ready(act, j)
                    act.activation(dst[:, c, :], bank(j)[:, 0:SEQ], ACT.Copy, scale=scale).then_inc(
                        bank_free[j % BANKS], 1)
            act.wait_ge(lam_summed, 1)
            act.activation(small[:, 10:12], small[:, 10:12], ACT.Exp).then_inc(lam_exp, 1)

            def exponentials(n):
                keys = P * (n // HEADS + 1)
                j = AJ["scores", n]
                act.wait_ge(max_ready, n + 1)
                if n >= 2:
                    act.wait_ge(mixed_ready, n - 1)
                for comp in range(2):
                    m = 16 + 4 * (n % 2) + comp
                    last = act.activation(probs[:, n % 2, comp, 0:keys], bank(j)[:, comp * SEQ:comp * SEQ + keys],
                                          ACT.Exp, bias=small[:, m:m + 1], accum_out=small[:, m + 2:m + 3])
                last.then_inc(probs_ready, 1)
                act.wait_ge(probs_ready, n + 1)
                act.nop().then_inc(bank_free[j % BANKS], 1)

            def turned(n):
                keys = P * (n // HEADS + 1)
                j = AJ["turn", n]
                job_ready(act, j)
                if n >= 2:
                    job_ready(act, AJ["values", n - 2])
                act.activation(mixedT[:, n % 2, 0:keys], bank(j)[:, 0:keys], ACT.Copy).then_inc(mixedT_ready, 1)
                act.wait_ge(mixedT_ready, n + 1)
                act.nop().then_inc(bank_free[j % BANKS], 1)

            for n in range(PAIRS + 1):
                if n < PAIRS:
                    exponentials(n)
                if n >= 1:
                    turned(n - 1)
            act.wait_ge(o_ready, PAIRS)
            act.activation(oT_flat, o_nat_flat, ACT.Square).then_inc(o_squared, 1)
            sqrt_of(act, small[:, 32:48], 1.0 / (2 * HD), LN_EPS, root)
            transposes_out(FJ["att_T"], (1, 2), oT)

        @block.vector
        def _(dve):
            pairs = lam_rows[:, :, :].rearrange("p (a b) d -> p a b d", b=2)
            dve_step(dve.tensor_tensor(lam_rows[:, 0:2, :], pairs[:, :, 0, :], pairs[:, :, 1, :], ALU.mult))
            dve.tensor_reduce(small[:, 10:12], lam_rows[:, 0:2, :], AX_X, ALU.add).then_inc(lam_summed, 1)
            for half in range(2):
                for t in range(2):
                    j = FJ["att_v"] + 2 * half + t
                    job_ready(dve, j)
                    dve.tensor_copy(v_nat[:, t, half * 512:half * 512 + 512], bank(j)).then_inc(
                        bank_free[j % BANKS], 1)
            dve.wait_ge(lam_exp, 1)
            dve_step(dve.tensor_tensor(neg_lam, small[:, 11:12], small[:, 10:11], ALU.subtract))
            dve_step(dve.tensor_scalar(neg_lam, neg_lam, -LAMBDA_INIT, None, ALU.add))

            def row_max(n):
                keys = P * (n // HEADS + 1)
                j = AJ["scores", n]
                job_ready(dve, j)
                m = 16 + 4 * (n % 2)
                src = bank(j).rearrange("p (c k) -> p c k", c=2)[:, :, 0:keys]
                dve_step(dve.tensor_reduce(small[:, m:m + 2], src, AX_X, ALU.max))
                dve.tensor_scalar(small[:, m:m + 2], small[:, m:m + 2], -1.0, None, ALU.mult).then_inc(max_ready, 1)

            def combine(n):
                keys = P * (n // HEADS + 1)
                m = 16 + 4 * (n % 2) + 2
                dve.wait_ge(probs_ready, n + 1)
                dve_step(dve.reciprocal(small[:, m:m + 2], small[:, m:m + 2]))
                dve_step(dve.tensor_scalar(small[:, m + 1:m + 2], small[:, m + 1:m + 2], neg_lam, None, ALU.mult))
                if n >= 2:
                    job_ready(dve, AJ["turn", n - 2])
                dve_step(dve.tensor_scalar(mixed[:, n % 2, 0:keys], probs[:, n % 2, 0, 0:keys], small[:, m:m + 1],
                                           None, ALU.mult))
                dve.scalar_tensor_tensor(mixed[:, n % 2, 0:keys], probs[:, n % 2, 1, 0:keys],
                                         small[:, m + 1:m + 2], mixed[:, n % 2, 0:keys], ALU.mult,
                                         ALU.add).then_inc(mixed_ready, 1)

            def values_out(n):
                b, h = n // HEADS, n % HEADS
                j = AJ["values", n]
                job_ready(dve, j)
                dve.tensor_copy(o_nat[:, b, h * P:h * P + P], bank(j)[:, 0:P]).then_inc(o_ready, 1)
                dve.wait_ge(o_ready, n + 1)
                dve.nop().then_inc(bank_free[j % BANKS], 1)

            for n in range(PAIRS + 2):
                if n < PAIRS:
                    row_max(n)
                if 1 <= n <= PAIRS:
                    combine(n - 1)
                if n >= 2:
                    values_out(n - 2)
            dve.wait_ge(o_squared, 1)
            dve.tensor_reduce(small[:, 32:48], oT_flat.rearrange("p (h d) -> p h d", d=P), AX_X,
                              ALU.add).then_inc(var_ready, 1)
            reciprocal_of(dve, small[:, 32:48], root)
            heads_of = o_nat_flat.rearrange("p (h d) -> p h d", d=P)
            dve_step(dve.tensor_tensor(heads_of, heads_of, small[:, 32:48].unsqueeze(2).broadcast_to([P, 16, P]),
                                       ALU.mult))
            dve.scalar_tensor_tensor(heads_of, heads_of, 1.0 - LAMBDA_INIT,
                                     subln_rows.unsqueeze(1).broadcast_to([P, 16, P]), ALU.mult,
                                     ALU.mult).then_inc(o_normed, 1)
            add_residual(FJ["att_o"])

    o_nat_flat, oT_flat = arena[:, 8192:10240], arena[:, 10240:12288]

    @stage
    def mix_norm1():
        layer_norm(2, "mix1_xT", normed[2])

    @stage
    def ffn_norm1():
        layer_norm(3, "ffn1_xT", normed[3], last=True)

    ALL = (0, 1, 2)

    def rms(name, tiles, src, dst, scaled, root):
        lo, hi = 48 + tiles[0], 48 + tiles[-1] + 1
        cleared, summed = sem(f"{name}_cleared"), sem(f"{name}_summed")

        @block.scalar
        def _(act):
            act.wait_ge(cleared, 1)
            for t in tiles:
                n = TILE_N[t]
                act_last = act.activation(dst(t)[0:n], src(t)[0:n], ACT.Square,
                                          accum_out=small[0:n, 48 + t:49 + t])
            act_last.then_inc(summed, 1)
            act.wait_ge(summed, 1)
            act.activation(small[:, lo:hi], small[:, lo:hi], ACT.Sqrt, bias=eps_cols[:, 1:2],
                           scale=1.0 / D).then_inc(std_ready, 1)

        @block.vector
        def _(dve):
            dve.memset(small[:, lo:hi], 1.0).then_inc(cleared, 1)
            reciprocal_of(dve, small[:, lo:hi], root)
            for t in tiles:
                n = TILE_N[t]
                dve.tensor_scalar(dst(t)[0:n], src(t)[0:n], small[0:n, 48 + t:49 + t], None,
                                  ALU.mult).then_inc(scaled, 1)

    def rms_to_T(name, job_name, src, dst, dstT, gain):
        scaled = sem(f"{name}_scaled")
        tmp = dst
        rms(name, ALL, src, tmp, scaled, next_sqrt())
        block.tensor(lambda pe: transposes_pe(FJ[job_name], ALL, dst, lambda t: pe.wait_ge(scaled, t + 1)))
        block.scalar(lambda act: transposes_out(FJ[job_name], ALL, dstT, gain))

    xn = carve(0, 3, D)

    @stage
    def pre_norm():
        rms_to_T("pre", "pre_xT", lambda t: x_nat[:, t, :], lambda t: xn[:, t, :], xT, "mix_pre_g_2")

    zs = carve(0, 3, D)
    zT = carve(9700, KC, L)
    xbcT = carve(3072, XC, L)
    XPAD = SSD_TAPS - 1
    xraw = carve(6336, XC, XPAD + L)
    in_ready, xconv_step, dt_pos, dt_exp, dt_one, dt_ln, a_exp = (
        sem("xbc_in"), sem("xconv_step"), sem("dt_neg_abs"), sem("dt_exp"), sem("dt_one"), sem("dt_ln"), sem("a_exp"))
    xpad_ready = sem("xpad_ready")
    dt_v, dt_m, dt_e, dt_w, dt_l, dt_r, dt, adt = (dts[:, n, :] for n in range(8))
    dt_d = dts[:, 8, :]

    def by_tile(x):
        return x.rearrange("p (t h) -> p t h", t=3)

    @stage
    def inner():
        @block.tensor
        def _(pe):
            project_turned(FJ["z"], [(unit_at["w_z"], unit_at["w_z"] + 1, xT)], zT)
            for c in range(XC):
                j, u = FJ["xbc"] + c, unit_at["w_xbc"] + c // 4
                unit_ready(u)
                take_bank(j)
                products(bank(j)[:, 0:L], [(slot_k(u)[:, k, (c % 4) * P:(c % 4) * P + P], xT[:, k, :])
                                           for k in range(KC)]).then_inc(job_done, 1)
            j = FJ["dt"]
            take_bank(j)
            for t in ALL:
                n, at = TILE_N[t], TILE_AT[t]
                last = products(bank(j)[0:n, t * SSD_HEADS:(t + 1) * SSD_HEADS],
                                [(xT[:, k, at:at + n], w_dt[:, k, :]) for k in range(KC)])
            last.then_inc(job_done, 1)

        @block.scalar
        def _(act):
            turned_in(FJ["z"], zT, ACT.Silu)
            j = FJ["z"] + KC
            for half in range(2):
                for t in ALL:
                    n = TILE_N[t]
                    job_ready(act, j)
                    act.activation(zs[0:n, t, half * 512:half * 512 + 512], bank(j)[0:n, :], ACT.Copy).then_inc(
                        bank_free[j % BANKS], 1)
                    j += 1
            act.wait_ge(xpad_ready, 1)
            for c in range(XC):
                j = FJ["xbc"] + c
                job_ready(act, j)
                act.activation(xraw[:, c, XPAD:XPAD + L], bank(j)[:, 0:L], ACT.Copy).then_inc(in_ready, 1)
                act.wait_ge(in_ready, c + 1)
                act.nop().then_inc(bank_free[j % BANKS], 1)
            for c in range(XC):
                act.wait_ge(xconv_step, (SSD_TAPS - 1) * 4 + c % 4 + 1 + (c // 4) * 4 * SSD_TAPS)
                act.activation(xbcT[:, c, :], xbcT[:, c, :], ACT.Silu, bias=column("ssd_conv_b_2", c))
            act.wait_ge(dt_pos, 1)
            act.activation(dt_e, dt_e, ACT.Exp).then_inc(dt_exp, 1)
            act.activation(ssd_rows[:, 1, :], ssd_rows[:, 1, :], ACT.Exp).then_inc(a_exp, 1)
            act.wait_ge(dt_one, 1)
            act.activation(dt_l, dt_w, ACT.Ln).then_inc(dt_ln, 1)

        @block.vector
        def _(dve):
            dve.memset(xraw[:, :, 0:XPAD], 0.0).then_inc(xpad_ready, 1)
            dve_step(dve.memset(dts[:, :, :], 0.0))
            n = 0
            for quad in range(XC // 4):
                for tap in range(SSD_TAPS):
                    for c in range(4 * quad, 4 * quad + 4):
                        src = xraw[:, c, tap:tap + L]
                        w = column("ssd_conv_w_2", tap * XC + c)
                        if tap == 0:
                            dve.wait_ge(in_ready, c + 1)
                            ins = dve.tensor_scalar(xbcT[:, c, :], src, w, None, ALU.mult)
                        else:
                            dve.wait_ge(xconv_step, n - 3)
                            ins = dve.scalar_tensor_tensor(xbcT[:, c, :], src, w, xbcT[:, c, :], ALU.mult, ALU.add)
                        ins.then_inc(xconv_step, 1)
                        n += 1
            j = FJ["dt"]
            job_ready(dve, j)
            dve.tensor_copy(by_tile(dt_v)[0:META, 0, :], bank(j)[0:META, 0:SSD_HEADS])
            dve_step(dve.tensor_copy(dt_v[:, SSD_HEADS:], bank(j)[:, SSD_HEADS:3 * SSD_HEADS]))
            dve.nop().then_inc(bank_free[j % BANKS], 1)
            dve_step(dve.tensor_tensor(by_tile(dt_v), by_tile(dt_v),
                                       ssd_rows[:, 0, :].unsqueeze(1).broadcast_to([P, 3, SSD_HEADS]), ALU.add))
            dve_step(dve.tensor_scalar(dt_m, dt_v, 0.0, None, ALU.max))
            dve.scalar_tensor_tensor(dt_e, dt_m, -2.0, dt_v, ALU.mult, ALU.add).then_inc(dt_pos, 1)
            dve.wait_ge(dt_exp, 1)
            dve.tensor_scalar(dt_w, dt_e, 1.0, None, ALU.add).then_inc(dt_one, 1)
            dve.wait_ge(dt_one, 1)
            dve_step(dve.tensor_scalar(dt_d, dt_w, -1.0, 1e-30, ALU.add, ALU.max))
            dve_step(dve.reciprocal(dt_d, dt_d))
            dve.wait_ge(dt_ln, 1)
            dve_step(dve.tensor_tensor(dt_r, dt_l, dt_d, ALU.mult))
            dve_step(dve.tensor_scalar(dt_w, dt_w, 1.0, None, ALU.is_equal))
            dve_step(dve.tensor_tensor(dt_r, dt_r, dt_w, ALU.add))
            dve_step(dve.tensor_tensor(dt_r, dt_r, dt_e, ALU.mult))
            dve_step(dve.tensor_tensor(dt, dt_m, dt_r, ALU.add))
            dve.wait_ge(a_exp, 1)
            dve_step(dve.tensor_scalar(dt_v, dt, -1.0, None, ALU.mult))
            dve_step(dve.tensor_tensor(by_tile(adt), by_tile(dt_v),
                                       ssd_rows[:, 1, :].unsqueeze(1).broadcast_to([P, 3, SSD_HEADS]), ALU.mult))

    xs, xdt, xd = carve(6336, D), carve(6336 + D, D), carve(6336 + 2 * D, D)
    decay = carve(9636, SSD_HEADS, P)
    steps = carve(11684, 2, 4, P)
    cb = carve(12708, SSD_GROUPS, P)
    b_nat = carve(12964, SSD_GROUPS, STATE)
    state = carve(13220, D)
    y_tmp = carve(14244, D)
    yT = carve(14440, KC, L)
    cums = carve(9408, 4, SSD_HEADS)
    PD = SSD_HEADS // SSD_GROUPS
    HG = D // SSD_GROUPS

    def ssd_jobs():
        order = {}
        for c in ALL:
            kinds = ["sums", "cb", "xs0", "xs1", "b", "row0", "row1", "row2", "row3", "diag0", "diag1"]
            kinds += ["off0", "off1"] if c > 0 else []
            kinds += ["state0", "state1"] if c < 2 else []
            for kind in kinds:
                order[kind, c] = FJ["ssd"] + len(order)
        return order

    SJ = ssd_jobs()
    cums_ready, cums_exp, cb_out, cb_masked, xs_ready, b_ready, step_ready, seg_ready, seg_exp, decay_ready = (
        sem("cums_ready"), sem("cums_exp"), sem("cb_out"), sem("cb_masked"), sem("xs_ready"), sem("b_ready"),
        sem("step_ready"), sem("seg_ready"), sem("seg_exp"), sem("decay_ready"))
    xdt_ready, xd_ready, state_ready, y_done = sem("xdt_ready"), sem("xd_ready"), sem("state_ready"), sem("y_done")

    def per_head(x, n, h0=0, nh=SSD_HEADS, width=SSD_HEADS and 64):
        return x.unsqueeze(2).broadcast_to([n, nh, width])

    def heads_of_row(x, n):
        return x[0:n].rearrange("p (h d) -> p h d", d=64)

    @stage
    def ssd():
        @block.tensor
        def _(pe):
            for c in ALL:
                n, at = TILE_N[c], TILE_AT[c]
                a_c = by_tile(adt)[0:n, c, :]
                j = SJ["sums", c]
                take_bank(j)
                products(bank(j)[:, 0:SSD_HEADS], [(ones[0:n, :], a_c)])
                products(bank(j)[0:n, SSD_HEADS:2 * SSD_HEADS], [(upto[0:n, 0:n], a_c)]).then_inc(job_done, 1)
                j = SJ["cb", c]
                take_bank(j)
                for g in range(SSD_GROUPS):
                    last = products(bank(j)[0:n, g * P:g * P + n],
                                    [(xbcT[:, KC + g, at:at + n], xbcT[:, KC + SSD_GROUPS + g, at:at + n])])
                last.then_inc(job_done, 1)
                for half in range(2):
                    j = SJ[f"xs{half}", c]
                    take_bank(j)
                    for k in range(4):
                        last = pe.transpose(bank(j)[0:n, k * P:k * P + P], xbcT[:, 4 * half + k, at:at + n],
                                            ident[:, :])
                    last.then_inc(job_done, 1)
                j = SJ["b", c]
                take_bank(j)
                for g in range(SSD_GROUPS):
                    last = pe.transpose(bank(j)[0:n, g * P:g * P + P], xbcT[:, KC + g, at:at + n], ident[:, :])
                last.then_inc(job_done, 1)
                for q in range(4):
                    j = SJ[f"row{q}", c]
                    take_bank(j)
                    pe.wait_ge(step_ready, 4 * c + q + 1)
                    products(bank(j)[:, 0:4 * n].rearrange("p (h l) -> p h l", h=4),
                             [(ones[0:n, :], steps[0:n, q % 2, :, 0:n])]).then_inc(job_done, 1)
                pe.wait_ge(decay_ready, 4 * c + 4)
                pe.wait_ge(xdt_ready, c + 1)
                for g in range(SSD_GROUPS):
                    j = SJ[f"diag{g}", c]
                    take_bank(j)
                    for h in range(PD):
                        last = products(bank(j)[0:n, h * 64:h * 64 + 64],
                                        [(decay[0:n, PD * g + h, 0:n],
                                          xdt[0:n, g * HG + h * 64:g * HG + h * 64 + 64])])
                    last.then_inc(job_done, 1)
                if c > 0:
                    pe.wait_ge(state_ready, c)
                    for g in range(SSD_GROUPS):
                        j = SJ[f"off{g}", c]
                        take_bank(j)
                        products(bank(j)[0:n, :], [(xbcT[:, KC + SSD_GROUPS + g, at:at + n],
                                                    state[:, g * HG:g * HG + HG])]).then_inc(job_done, 1)
                if c < 2:
                    pe.wait_ge(xd_ready, c + 1)
                    pe.wait_ge(b_ready, c + 1)
                    for g in range(SSD_GROUPS):
                        j = SJ[f"state{g}", c]
                        take_bank(j)
                        products(bank(j), [(b_nat[0:n, g, :], xd[0:n, g * HG:g * HG + HG])]).then_inc(job_done, 1)

        @block.scalar
        def _(act):
            for c in ALL:
                n = TILE_N[c]
                if c:
                    act.wait_ge(y_done, c)
                j = SJ["cb", c]
                job_ready(act, j)
                act.activation(cb[0:n, :, 0:n], bank(j)[0:n, 0:2 * P].rearrange("p (g l) -> p g l", g=2)[:, :, 0:n],
                               ACT.Copy).then_inc(cb_out, 1)
                act.wait_ge(cb_out, c + 1)
                act.nop().then_inc(bank_free[j % BANKS], 1)
                for half in range(2):
                    j = SJ[f"xs{half}", c]
                    job_ready(act, j)
                    act.activation(xs[0:n, half * 512:half * 512 + 512], bank(j)[0:n, :], ACT.Copy).then_inc(
                        bank_free[j % BANKS], 1)
                act.nop().then_inc(xs_ready, 1)
                j = SJ["b", c]
                job_ready(act, j)
                act.activation(b_nat[0:n, :, :], bank(j)[0:n, 0:2 * P].rearrange("p (g l) -> p g l", g=2),
                               ACT.Copy).then_inc(b_ready, 1)
                act.wait_ge(b_ready, c + 1)
                act.nop().then_inc(bank_free[j % BANKS], 1)
                act.wait_ge(cums_ready, c + 1)
                act.activation(cums[:, 0:3, :], cums[:, 0:3, :], ACT.Exp).then_inc(cums_exp, 1)
                for q in range(4):
                    act.wait_ge(seg_ready, 4 * c + q + 1)
                    m = decay[0:n, 4 * q:4 * q + 4, 0:n]
                    act.activation(m, m, ACT.Exp).then_inc(seg_exp, 1)

        @block.gpsimd
        def _(pool):
            for c in ALL:
                n = TILE_N[c]
                pool.wait_ge(cb_out, c + 1)
                pool.affine_select(out=cb[0:n, :, 0:n], in_=cb[0:n, :, 0:n], compare_op=ALU.is_ge, fill=0.0, base=0,
                                   pattern=[[0, 2], [1, n]], channel_multiplier=-1).then_inc(cb_masked, 1)

        @block.vector
        def _(dve):
            dve_step(dve.memset(cums, 0.0))
            for c in ALL:
                n = TILE_N[c]
                for q in range(4):
                    k = 4 * c + q
                    if k >= 2:
                        job_ready(dve, SJ[f"row{(k - 2) % 4}", (k - 2) // 4])
                    dve.tensor_tensor(steps[0:n, q % 2, :, 0:n],
                                      by_tile(adt)[0:n, c, 4 * q:4 * q + 4].unsqueeze(2).broadcast_to([n, 4, n]),
                                      upto[0:n, 0:n].unsqueeze(1).broadcast_to([n, 4, n]), ALU.mult).then_inc(
                                          step_ready, 1)
                    if q == 1:
                        j = SJ["sums", c]
                        job_ready(dve, j)
                        dve.tensor_copy(cums[:, 2, :], bank(j)[:, 0:SSD_HEADS])
                        dve.tensor_copy(cums[0:n, 3, :], bank(j)[0:n, SSD_HEADS:2 * SSD_HEADS])
                        dve_step(dve.tensor_copy(cums[0:n, 0, :], bank(j)[0:n, SSD_HEADS:2 * SSD_HEADS]))
                        dve.nop().then_inc(bank_free[j % BANKS], 1)
                        dve.tensor_tensor(cums[0:n, 1, :], cums[0:n, 2, :], cums[0:n, 3, :],
                                          ALU.subtract).then_inc(cums_ready, 1)
                    if q >= 1:
                        segment(dve, c, q - 1)
                segment(dve, c, 3)
                dve.wait_ge(xs_ready, c + 1)
                dve.wait_ge(bank_free[SJ["xs1", c] % BANKS], SJ["xs1", c] // BANKS + 1)
                dve.tensor_tensor(heads_of_row(xdt, n), heads_of_row(xs, n),
                                  per_head(by_tile(dt)[0:n, c, :], n), ALU.mult).then_inc(xdt_ready, 1)
                for q in range(4):
                    dve.wait_ge(seg_exp, 4 * c + q + 1)
                    dve.wait_ge(cb_masked, c + 1)
                    m = decay[0:n, 4 * q:4 * q + 4, 0:n]
                    dve.tensor_tensor(m, m, cb[0:n, q // 2, 0:n].unsqueeze(1).broadcast_to([n, 4, n]),
                                      ALU.mult).then_inc(decay_ready, 1)
                dve.wait_ge(cums_exp, c + 1)
                dve.wait_ge(xdt_ready, c + 1)
                dve.tensor_tensor(heads_of_row(xd, n), heads_of_row(xdt, n), per_head(cums[0:n, 1, :], n),
                                  ALU.mult).then_inc(xd_ready, 1)
                y = y_tmp[0:n]
                dve_step(dve.tensor_tensor(heads_of_row(xs, n), heads_of_row(xs, n),
                                           per_head(ssd_rows[0:n, 2, :], n), ALU.mult))
                for g in range(SSD_GROUPS):
                    j = SJ[f"diag{g}", c]
                    job_ready(dve, j)
                    cols = slice(g * HG, g * HG + HG)
                    dve_step(dve.tensor_tensor(y[:, cols], xs[0:n, cols], bank(j)[0:n, :], ALU.add))
                    dve.nop().then_inc(bank_free[j % BANKS], 1)
                if c > 0:
                    for g in range(SSD_GROUPS):
                        j = SJ[f"off{g}", c]
                        job_ready(dve, j)
                        cols = slice(g * HG, g * HG + HG)
                        part = xs[0:n, cols].rearrange("p (h d) -> p h d", d=64)
                        dve_step(dve.tensor_tensor(part, bank(j)[0:n, :].rearrange("p (h d) -> p h d", d=64),
                                                   per_head(cums[0:n, 0, PD * g:PD * g + PD], n, nh=PD), ALU.mult))
                        dve.nop().then_inc(bank_free[j % BANKS], 1)
                        dve_step(dve.tensor_tensor(y[:, cols], y[:, cols], xs[0:n, cols], ALU.add))
                dve_step(dve.tensor_tensor(zs[0:n, c, :], zs[0:n, c, :], y, ALU.mult))
                if c < 2:
                    for g in range(SSD_GROUPS):
                        j = SJ[f"state{g}", c]
                        job_ready(dve, j)
                        cols = slice(g * HG, g * HG + HG)
                        if c == 0:
                            dve_step(dve.tensor_copy(state[:, cols], bank(j)))
                        else:
                            part = state[:, cols].rearrange("p (h d) -> p h d", d=64)
                            dve_step(dve.tensor_tensor(part, part,
                                                       per_head(cums[:, 2, PD * g:PD * g + PD], P, nh=PD), ALU.mult))
                            dve_step(dve.tensor_tensor(state[:, cols], state[:, cols], bank(j), ALU.add))
                        dve.nop().then_inc(bank_free[j % BANKS], 1)
                    dve.nop().then_inc(state_ready, 1)
                dve.nop().then_inc(y_done, 1)

    def segment(dve, c, q):
        n = TILE_N[c]
        j = SJ[f"row{q}", c]
        job_ready(dve, j)
        if q == 0:
            dve.wait_ge(cums_ready, c + 1)
        m = decay[0:n, 4 * q:4 * q + 4, 0:n]
        dve_step(dve.tensor_tensor(m, bank(j)[0:n, 0:4 * n].rearrange("p (h l) -> p h l", h=4),
                                   cums[0:n, 3, 4 * q:4 * q + 4].unsqueeze(2).broadcast_to([n, 4, n]), ALU.subtract))
        dve.nop().then_inc(bank_free[j % BANKS], 1)
        dve.tensor_scalar(m, m, 0.0, None, ALU.min).then_inc(seg_ready, 1)

    @stage
    def ssd_norm():
        rms_to_T("ssd_norm", "y_T", lambda t: zs[:, t, :], lambda t: xn2[:, t, :], yT, "ssd_norm_g_2")

    xn2 = carve(3072, 3, D)

    sqT, skT = carve(0, KC, L), carve(2176, KC, L)
    sv = carve(4352, 3, D)
    svT = carve(10496, KC, L)
    so = carve(7424, 3, D)
    W1 = 384
    pos, soft, wts = carve(10496, 2, W1 + L), carve(11808, 2, W1 + L), carve(13120, 2, W1 + L)
    z_ready, neg_abs, soft_exp, soft_ln, soft_sum, soft_ready, expo_ready, w_exp, w_ready, so_ready = (
        sem(f"sb_{x}") for x in ("z_ready", "neg_abs", "exp", "ln", "sum", "soft_ready", "expo", "w_exp",
                                 "w_ready", "o_ready"))

    def sb_bank(h):
        return psum[:, BANKS + 2 * (h % 2), 0:W1], psum[0:META, BANKS + 2 * (h % 2) + 1, 0:L]

    def sb_parts(x, h):
        return x[:, h % 2, 0:W1], x[0:META, h % 2, W1:W1 + L]

    @stage
    def stick_breaking():
        @block.tensor
        def _(pe):
            for first, u0 in ((FJ["sb_q"], unit_at["w_sb_q"]), (FJ["sb_k"], unit_at["w_sb_k"])):
                for c in range(KC):
                    j = first + c
                    unit_ready(u0 + c // 4)
                    take_bank(j)
                    products(bank(j)[:, 0:L], [(slot_k(u0 + c // 4)[:, k, (c % 4) * P:(c % 4) * P + P], xT[:, k, :])
                                               for k in range(KC)]).then_inc(job_done, 1)
            project_turned(FJ["sb_v"], [(unit_at["w_sb_v"], unit_at["w_sb_v"] + 1, xT)], svT)
            all_read_out(pe, FJ["sb_heads"])

            def logits(h):
                rows = slice(64 * (h % 2), 64 * (h % 2) + 64)
                c = h // 2
                main, meta = sb_bank(h)
                if h >= 2:
                    pe.wait_ge(w_exp, 2 * (h - 1))
                pe.matmul(main[:, 0:SEQ], skT[rows, c, META:META + P], sqT[rows, c, META:L], start=True, stop=True)
                pe.matmul(main[:, SEQ:W1], skT[rows, c, META + P:L], sqT[rows, c, META + P:L], start=False, stop=True,
                          skip_group_check=True)
                pe.matmul(meta, skT[rows, c, 0:META], sqT[rows, c, :], start=True, stop=True).then_inc(z_ready, 1)

            def exponents(h):
                main, meta = sb_bank(h)
                s1, s0 = sb_parts(soft, h)
                pe.wait_ge(soft_ready, h + 1)
                terms = [(main[:, SEQ:W1], neg_from[:, :], s1[:, SEQ:W1]),
                         (main[:, 0:SEQ], neg_from[:, :], s1[:, 0:SEQ]),
                         (main[:, P:SEQ], neg_ones[:, :], s1[:, SEQ:W1]),
                         (meta, neg_from[0:META, 0:META], s0),
                         (meta[:, META:L], neg_ones[:, 0:META], s1[:, 0:SEQ]),
                         (meta[:, META + P:L], neg_ones[:, 0:META], s1[:, SEQ:W1])]
                for dst, lhsT, rhs in terms:
                    last = pe.matmul(dst, lhsT, rhs, start=False, stop=True, skip_group_check=True)
                last.then_inc(expo_ready, 1)

            def values(h):
                j = FJ["sb_heads"] + h
                w1, w0 = sb_parts(wts, h)
                cols = slice(64 * h, 64 * h + 64)
                pe.wait_ge(w_ready, h + 1)
                take_bank(j)
                products(bank(j)[0:META, 0:64], [(w0[:, 0:META], sv[0:META, 0, cols])])
                products(bank(j)[:, 64:128], [(w0[:, META:META + P], sv[0:META, 0, cols]),
                                              (w1[:, 0:P], sv[:, 1, cols])])
                products(bank(j)[:, 128:192], [(w0[:, META + P:L], sv[0:META, 0, cols]),
                                               (w1[:, P:SEQ], sv[:, 1, cols]),
                                               (w1[:, SEQ:W1], sv[:, 2, cols])]).then_inc(job_done, 1)

            for n in range(SB_HEADS + 2):
                if n < SB_HEADS:
                    logits(n)
                if 1 <= n <= SB_HEADS:
                    exponents(n - 1)
                if n >= 2:
                    values(n - 2)

        @block.scalar
        def _(act):
            for first, dst, scale in ((FJ["sb_q"], sqT, 0.125), (FJ["sb_k"], skT, 1.0)):
                for c in range(KC):
                    j = first + c
                    job_ready(act, j)
                    act.activation(dst[:, c, :], bank(j)[:, 0:L], ACT.Copy, scale=scale).then_inc(
                        bank_free[j % BANKS], 1)
            turned_in(FJ["sb_v"], svT)

            def softplus(h):
                for part in sb_parts(soft, h):
                    act.wait_ge(neg_abs, h + 1)
                    act.activation(part, part, ACT.Exp).then_inc(soft_exp, 1)
                for n, part in enumerate(sb_parts(soft, h)):
                    act.wait_ge(soft_exp, 2 * h + n + 1)
                    act.activation(part, part, ACT.Ln, bias=1.0).then_inc(soft_ln, 1)

            def weights(h):
                act.wait_ge(expo_ready, h + 1)
                if h >= 2:
                    job_ready(act, FJ["sb_heads"] + h - 2)
                for dst, src in zip(sb_parts(wts, h), sb_bank(h)):
                    act.activation(dst, src, ACT.Exp).then_inc(w_exp, 1)

            for n in range(SB_HEADS + 1):
                if n < SB_HEADS:
                    softplus(n)
                if n >= 1:
                    weights(n - 1)

        @block.gpsimd
        def _(pool):
            def masked(x, h):
                main, meta = sb_parts(x, h)
                for part in (main[:, 0:P], main[:, SEQ:W1], meta[:, 0:META]):
                    n = part.shape[1]
                    ins = pool.affine_select(out=part, in_=part, compare_op=ALU.is_gt, fill=0.0, base=0,
                                             pattern=[[1, n]], channel_multiplier=-1)
                return ins

            for n in range(SB_HEADS + 1):
                if n < SB_HEADS:
                    pool.wait_ge(soft_ln, 2 * n + 2)
                    pool.wait_ge(neg_abs, n + 1)
                    for dst, more in zip(sb_parts(soft, n), sb_parts(pos, n)):
                        pool_step(pool.tensor_tensor(dst, dst, more, ALU.add))
                    masked(soft, n).then_inc(soft_ready, 1)
                if n >= 1:
                    pool.wait_ge(w_exp, 2 * n)
                    masked(wts, n - 1).then_inc(w_ready, 1)

        @block.vector
        def _(dve):
            j = FJ["sb_v"] + KC
            for half in range(2):
                for t in ALL:
                    n = TILE_N[t]
                    job_ready(dve, j)
                    dve.tensor_copy(sv[0:n, t, half * 512:half * 512 + 512], bank(j)[0:n, :]).then_inc(
                        bank_free[j % BANKS], 1)
                    j += 1
            for n in range(SB_HEADS + 2):
                if n < SB_HEADS:
                    dve.wait_ge(z_ready, n + 1)
                    if n >= 2:
                        dve.wait_ge(expo_ready, n - 1)
                    for m, z in zip(sb_parts(pos, n), sb_bank(n)):
                        dve_step(dve.tensor_scalar(m, z, 0.0, None, ALU.max))
                    for s, m, z in zip(sb_parts(soft, n), sb_parts(pos, n), sb_bank(n)):
                        ins = dve.scalar_tensor_tensor(s, m, -2.0, z, ALU.mult, ALU.add)
                    ins.then_inc(neg_abs, 1)
                if n >= 2:
                    h = n - 2
                    j = FJ["sb_heads"] + h
                    job_ready(dve, j)
                    dve.tensor_copy(so[0:META, 0, 64 * h:64 * h + 64], bank(j)[0:META, 0:64])
                    dve_step(dve.tensor_copy(so[:, 1:3, 64 * h:64 * h + 64],
                                             bank(j)[:, 64:192].rearrange("p (t d) -> p t d", t=2)))
                    dve.nop().then_inc(bank_free[j % BANKS], 1)

    sbT = carve(0, KC, L)
    so_n = carve(10496, 3, D)

    @stage
    def sb_norm():
        rms_to_T("sb_norm", "sb_T", lambda t: so[:, t, :], lambda t: so_n[:, t, :], sbT, "sb_norm_g_2")

    mix = carve(4352, 3, D)
    mix_n = carve(7424, 3, D)
    mixT = carve(10496, KC, L)
    mix_out, mix_scaled, w_out_done = sem("mix_out"), sem("mix_scaled"), sem("w_out_done")

    def post_norm(k, name, tiles, src, dst):
        scaled = sem(f"{name}_scaled")
        rms(name, tiles, src, dst, scaled, next_sqrt())

        @block.vector
        def _(dve):
            dve.wait_ge(norm_loaded[k % 2], norm_count[k % 2])
            for i, t in enumerate(tiles):
                n = TILE_N[t]
                dve.wait_ge(scaled, i + 1)
                dve_step(dve.tensor_tensor(dst(t)[0:n], dst(t)[0:n], norm_rows[0:n, k % 2, 0, :], ALU.mult))
                dve.tensor_tensor(x_nat[0:n, t, :], x_nat[0:n, t, :], dst(t)[0:n], ALU.add)

    @stage
    def project_out():
        @block.tensor
        def _(pe):
            w = unit_at["w_out"]
            project_turned(FJ["w_out"], [(w, w + 2, yT), (w + 1, w + 3, sbT)], mixT)

        block.scalar(lambda act: turned_in(FJ["w_out"], mixT))

        @block.vector
        def _(dve):
            j = FJ["w_out"] + KC
            for half in range(2):
                for t in ALL:
                    n = TILE_N[t]
                    job_ready(dve, j)
                    dve.tensor_copy(mix[0:n, t, half * 512:half * 512 + 512], bank(j)[0:n, :]).then_inc(
                        bank_free[j % BANKS], 1)
                    j += 1

    @stage
    def mix_post():
        post_norm(4, "mix_post", ALL, lambda t: mix[:, t, :], lambda t: mix_n[:, t, :])

    @stage
    def ffn_pre():
        rms_to_T("ffn_pre", "ffn_T", lambda t: x_nat[:, t, :], lambda t: xn[:, t, :], xT, "ffn_pre_g_2")

    fT = carve(3072, FC, SEQ)
    gate = carve(8800, 4, SEQ)
    act_g = carve(9900, 2, SEQ)
    G0 = META - (FFN_TAPS - 1)
    GW = SEQ + FFN_TAPS - 1
    gconv_step, gelu_ready, f_ready, down_ready = sem("gconv_step"), sem("gelu_ready"), sem("f_ready"), sem("down_ready")
    f_out = carve(10500, 2, D)
    f_n = carve(12600, 2, D)

    @stage
    def ffn():
        @block.tensor
        def _(pe):
            for c in range(FC):
                u = unit_at["w_up"] + c // 2
                unit_ready(u)
                for side, (at, width) in enumerate(((G0, GW), (META, SEQ))):
                    j = FJ["up"] + 2 * c + side
                    take_bank(j)
                    cols = side * 256 + (c % 2) * P
                    products(bank(j)[:, 0:width], [(slot_k(u)[:, k, cols:cols + P], xT[:, k, at:at + width])
                                                   for k in range(KC)]).then_inc(job_done, 1)
            for c in range(FC):
                u = unit_at["w_down"] + c // 4
                if c % 4 == 0:
                    unit_ready(u)
                pe.wait_ge(f_ready, c + 1)
                for t in range(2):
                    for half in range(2):
                        last = pe.matmul(psum[:, BANKS + 2 * t + half, :], fT[:, c, t * P:t * P + P],
                                         slot_k(u, D)[:, c % 4, half * 512:half * 512 + 512], start=(c == 0),
                                         stop=(c == FC - 1))
            last.then_inc(down_ready, 1)

        @block.scalar
        def _(act):
            for c in range(FC):
                act.wait_ge(gconv_step, 3 * c + 3)
                if c >= 2:
                    act.wait_ge(f_ready, c - 1)
                act.activation(act_g[:, c % 2, :], gate[:, c % 4, :], ACT.Gelu_apprx_tanh).then_inc(gelu_ready, 1)

        @block.vector
        def _(dve):
            for c in range(FC):
                j = FJ["up"] + 2 * c
                job_ready(dve, j)
                if c >= 4:
                    dve.wait_ge(gelu_ready, c - 3)
                for tap in range(FFN_TAPS):
                    src = bank(j)[:, tap:tap + SEQ]
                    w = column("ffn_conv_w_2", tap * FC + c)
                    g = gate[:, c % 4, :]
                    if tap == 0:
                        ins = dve.tensor_scalar(g, src, w, column("ffn_conv_b_2", c), ALU.mult, ALU.add)
                    else:
                        dve.wait_ge(gconv_step, 3 * c + tap)
                        ins = dve.scalar_tensor_tensor(g, src, w, g, ALU.mult, ALU.add)
                    ins.then_inc(gconv_step, 1)
                dve.wait_ge(gconv_step, 3 * c + 3)
                dve.nop().then_inc(bank_free[j % BANKS], 1)
                dve.wait_ge(gelu_ready, c + 1)
                job_ready(dve, j + 1)
                dve.tensor_tensor(fT[:, c, :], act_g[:, c % 2, :], bank(j + 1)[:, 0:SEQ], ALU.mult).then_inc(f_ready, 1)
                dve.wait_ge(f_ready, c + 1)
                dve.nop().then_inc(bank_free[(j + 1) % BANKS], 1)
            dve.wait_ge(down_ready, 1)
            for t in range(2):
                dve.tensor_copy(f_out[:, t, :], psum[:, BANKS + 2 * t:BANKS + 2 * t + 2, :].rearrange(
                    "p b n -> p (b n)"))

    @stage
    def ffn_post():
        post_norm(5, "ffn_post", (1, 2), lambda t: f_out[:, t - 1, :], lambda t: f_n[:, t - 1, :])

    next_norm = {
        "constants": (1, a["ln_ffn_g"][0], a["ln_ffn_b"][0]), "mix_norm0": (2, a["ln_mix_g"][1], a["ln_mix_b"][1]),
        "ffn_norm0": (3, a["ln_ffn_g"][1], a["ln_ffn_b"][1]), "mix_norm1": (4, a["mix_post_g_2"][0]),
        "ffn_norm1": (5, a["ffn_post_g_2"][0]),
    }
    table = {f.__name__: f for f in stages}
    for name in ORDER:
        table[name]()
        next_stage()
        if name in next_norm:
            block.scalar(lambda act, args=next_norm[name]: load_norm(*args))
        if stop == name:
            break

    @block.sync
    def _(sp):
        sp.wait_ge(stage_left, len(compute) * left[0])
        sp.dma_start(out[0].rearrange("(t p) n -> p t n", p=P), x_nat[:, 1:3, :]).then_inc(output_written, 16)
        sp.wait_ge(output_written, 16)
        for k in range(2):
            if norm_count[k]:
                sp.wait_ge(norm_loaded[k], norm_count[k])

    ctx.close()


_INS = ["x", "a_w_pw1", "a_b_pw1", "a_w_dw", "a_b_dw", "a_ln_g", "a_ln_b", "a_w_pw2", "a_b_pw2", "w_kv", "b_w_q",
        "b_lambda", "b_subln_g", "b_w_o", "rel_bias", "ln_mix_g", "ln_mix_b", "ln_ffn_g", "ln_ffn_b", "router_w",
        "router_bias", "moe_w_gate", "moe_w_up", "moe_w_down", "meta_tokens_2", "mix_pre_g_2", "w_in_2",
        "ssd_conv_w_2", "ssd_conv_b_2", "ssd_dt_bias_2", "ssd_a_log_2", "ssd_d_2", "ssd_norm_g_2", "sb_norm_g_2",
        "w_out_2", "mix_post_g_2", "ffn_pre_g_2", "w_up_2", "ffn_conv_w_2", "ffn_conv_b_2", "w_down_2",
        "ffn_post_g_2"]


def kernel(**inputs):
    import concourse.bacc as bacc
    from concourse.bass_utils import run_bass_kernel_spmd

    nc = bacc.Bacc("TRN2", target_bir_lowering=False, num_devices=1)
    arrays, aps = {}, {}
    for name in _INS:
        arrays[f"in_{name}"] = np.ascontiguousarray(inputs[name])
    arrays["in_buckets"] = bucket_table()
    for name, arr in arrays.items():
        aps[name[3:]] = nc.dram_tensor(name, arr.shape, mybir.dt.from_np(arr.dtype), kind="ExternalInput").ap()
    out = nc.dram_tensor("out_0", (1, SEQ, D), F32, kind="ExternalOutput").ap()
    program(nc, aps, out)
    r = run_bass_kernel_spmd(nc, [arrays], core_ids=[0])
    return r.results[0]["out_0"]
```

```python
import math
from contextlib import ExitStack

import numpy as np

import concourse.bass as bass
from concourse import mybir

ARENA = 16624
F32 = mybir.dt.float32
ALU = mybir.AluOpType
ACT = mybir.ActivationFunctionType
AX_X = mybir.AxisListType.X

P = 128
D = 1024
KC = D // P
SEQ = 256
META = 16
L = META + SEQ
DEPTH = 2
ALPHA = (2.0 * DEPTH) ** 0.25
LN_EPS = 1e-5
TAPS = 31
HEADS, HD = 8, 64
N_BUCKETS, MAX_DISTANCE = 32, 128
LAMBDA_INIT = 0.8 - 0.6 * math.exp(-0.3 * 1)
MASKED = -1e30
EXPERTS, GROUPS, PER_GROUP, DE = 16, 4, 4, 512
RING = 6
SEATS, PAIRS_E = 64, EXPERTS // 2
IN_PAIR = {x: n for n, x in enumerate(("GU0", "S", "GU1", "X0", "T", "X1", "Y0", "Y1"))}
IN_LAST = {x: n for n, x in enumerate(("GU0", "S", "GU1", "T", "Y0", "Y1"))}
PAIR_JOBS = len(IN_PAIR)
MOE_JOBS = 2 + PAIR_JOBS * (PAIRS_E - 1) + len(IN_LAST)
BANKS = 4
TILE_AT, TILE_N = (0, META, META + P), (META, P, P)

SSD_HEADS, SSD_GROUPS, STATE, SSD_TAPS = 16, 2, 128, 4
XBC = D + 2 * SSD_GROUPS * STATE
XC = XBC // P
SB_HEADS = 16
EPS = 1e-6
D_FF = 2816
FC = D_FF // P
FFN_TAPS = 3
OFF_XBC = D
OFF_DT = OFF_XBC + XBC
OFF_Q = OFF_DT + SSD_HEADS
OFF_K, OFF_V = OFF_Q + D, OFF_Q + 2 * D

VEC_ROWS = [
    [("a_w_dw", 0, 128)],
    [("a_w_dw", 128, 120), ("a_b_dw", 0, 8)],
    [("a_ln_g", 0, 8), ("a_ln_b", 0, 8), ("a_b_pw1", 0, 16), ("mix_pre_g_2", 0, 8), ("ssd_norm_g_2", 0, 8),
     ("sb_norm_g_2", 0, 8), ("ffn_pre_g_2", 0, 8), ("ssd_conv_w_2", 0, SSD_TAPS * XC), ("ssd_conv_b_2", 0, XC)],
    [("ffn_conv_w_2", 0, FFN_TAPS * FC), ("ffn_conv_b_2", 0, FC)],
]
VEC_COL = {}
for _tile, _rows in enumerate(VEC_ROWS):
    _at = 0
    for _name, _first, _n in _rows:
        VEC_COL.setdefault(_name, _tile * P + _at)
        _at += _n

JOBS = [
    ("conv_xT", 4), ("vec", 1), ("glu", 8), ("iota", 1), ("relb", 1), ("conv", 2), ("conv_mean", 1), ("conv_var", 1),
    ("pw2", 4), ("mix0_xT", 4),
    ("route0", 2), ("moe0", MOE_JOBS), ("ffn0_xT", 4),
    ("att_v", 4), ("att_heads", 3 * 16), ("att_T", 4), ("att_o", 4),
    ("mix1_xT", 4), ("route1", 2), ("moe1", MOE_JOBS), 
    ("pre_xT", 6), ("z", 14), ("xbc", XC), ("dt", 1), ("ssd", 3 * 11 + 2 * 2 + 2 * 2), ("y_T", 6),
    ("sb_v", 14), ("w_out", 14),
    ("ffn_T", 6), ("up", 2 * FC),
]


def first_jobs():
    at, out = 0, {}
    for name, n in JOBS:
        out[name] = at
        at += n
    return out


def t5_bucket(n):
    exact = N_BUCKETS // 2
    nf = np.maximum(n, 1).astype(np.float32)
    large = exact + (np.log(nf / np.float32(exact)) / np.float32(math.log(MAX_DISTANCE / exact))
                     * np.float32(N_BUCKETS - exact)).astype(np.int32)
    return np.where(n < exact, n, np.minimum(large, N_BUCKETS - 1))


def bucket_table():
    table = np.zeros((N_BUCKETS, 3 * P), np.float32)
    j = np.arange(SEQ)
    table[t5_bucket(SEQ - 1 - j), j] = 1.0
    return table


ORDER = ["constants", "conformer", "mix_norm0", "route0", "overflow0", "moe0", "ffn_norm0", "attention",
         "mix_norm1", "route1", "overflow1", "moe1", "ffn_norm1", "pre_norm", "inner", "ssd", "ssd_norm", "stick_breaking", "project_out", "mix_post", "ffn_pre",
         "ffn", "ffn_post"]


RUN_ON = {"conformer", "mix_norm0", "overflow0", "moe0", "ffn_norm0", "attention", "mix_norm1", "overflow1", "moe1",
          "ffn_norm1", "mix_post", "ffn"}


class Chain:

    def __init__(self, eng, sem):
        self.eng, self.sem, self.n = eng, sem, 0

    def __call__(self, ins):
        self.n += 1
        ins.then_inc(self.sem, 1)
        self.eng.wait_ge(self.sem, self.n)


def program(nc, a, out):
    ctx = ExitStack()

    def sb(name, *shape):
        return ctx.enter_context(nc.sbuf_tensor(name, list(shape), F32))

    def sem(name):
        return ctx.enter_context(nc.semaphore(name))

    FJ = first_jobs()
    ring = sb("ring", P, RING, 4096)
    x_nat = sb("x_nat", P, 3, D)
    xT = sb("xT", P, KC, L)
    norm_rows = sb("norm_rows", P, 2, 2, D)
    vec = sb("vec", P, 4 * P)
    ident = sb("ident", P, P)
    ones = sb("ones", P, P)
    router_w = sb("router_w", P, KC, EXPERTS)
    router_b = sb("router_b", P, EXPERTS)
    gates = sb("gates", P, 2, EXPERTS)
    eps_cols = sb("eps_cols", P, 2)
    counting = sb("counting", P, P)
    earlier = sb("earlier", P, 4, 4)
    over_flag = ctx.enter_context(nc.sbuf_tensor("over_flag", [P, 1], mybir.dt.int32))
    rel_w = sb("rel_w", N_BUCKETS, HEADS)
    upto, neg_from, neg_ones = sb("upto", P, P), sb("neg_from", P, P), sb("neg_ones", P, P)
    ssd_rows = sb("ssd_rows", P, 3, SSD_HEADS)
    w_dt = sb("w_dt", P, KC, SSD_HEADS)
    dts = sb("dts", P, 10, 3 * SSD_HEADS)
    small = sb("small", P, 64)
    stats = sb("stats", P, 3, 2, 6)
    arena = sb("arena", P, ARENA)

    psum = ctx.enter_context(nc.psum_tensor("psum", [P, 8, 512], F32))
    rel_scratch = nc.dram_tensor("rel_scratch", (HEADS, 3 * P), F32).ap()

    slot_loaded = [sem(f"slot_loaded{i}") for i in range(RING)]
    job_done = sem("job_done")
    bank_free = [sem(f"bank_free{i}") for i in range(BANKS)]
    stage_left = sem("stage_left")
    consts_loaded = sem("consts_loaded")
    consts_made = sem("consts_made")
    x_loaded, rows_sent = sem("x_loaded"), sem("rows_sent")
    norm_loaded = [sem("norm_loaded0"), sem("norm_loaded1")]
    output_written = sem("output_written")
    var_ready, std_ready, stats_ready = sem("var_ready"), sem("std_ready"), sem("stats_ready")
    dve_step, act_step = Chain(nc.vector, sem("dve_step")), Chain(nc.scalar, sem("act_step"))
    pool_step = Chain(nc.gpsimd, sem("pool_step"))

    def carve(at, *shape):
        n = int(np.prod(shape))
        assert at + n <= ARENA, (at, n)
        flat = arena[:, at:at + n]
        if len(shape) == 1:
            return flat
        names = "abcd"[:len(shape)]
        return flat.rearrange(f"p ({' '.join(names)}) -> p {' '.join(names)}", **dict(zip(names, shape)))

    def column(name, i):
        at = VEC_COL[name] + i
        return vec[:, at:at + 1]

    def bank(j):
        return psum[:, j % BANKS, :]

    def take_bank(j):
        if j >= BANKS:
            nc.tensor.wait_ge(bank_free[j % BANKS], j // BANKS)

    def job_ready(eng, j):
        eng.wait_ge(job_done, j + 1)

    def all_read_out(eng, j):
        for b in range(BANKS):
            eng.wait_ge(bank_free[b], (j - b + BANKS - 1) // BANKS)

    def products(dst, pairs):
        for n, (lhsT, rhs) in enumerate(pairs):
            last = nc.tensor.matmul(dst, lhsT, rhs, start=(n == 0), stop=(n == len(pairs) - 1))
        return last

    def columns_of(w, at, n=512):
        return w[:, at:at + n].rearrange("(k p) n -> p k n", p=P)

    units = []

    def add_units(name, srcs, last_jobs):
        first = len(units)
        for s, j in zip(srcs, last_jobs):
            units.append((s, ("job", j)))
        unit_at[name] = first

    unit_at = {}
    w_pw1 = a["a_w_pw1"][0]
    add_units("pw1", [columns_of(w_pw1, c) for c in (0, D, 512, D + 512)],
              [FJ["glu"] + n for n in (3, 3, 7, 7)])
    add_units("pw2", [columns_of(a["a_w_pw2"][0], c) for c in (0, 512)], [FJ["pw2"] + n for n in (1, 3)])

    def pair_job(layer, p, kind):
        return FJ[f"moe{layer}"] + 2 + PAIR_JOBS * p + (IN_LAST if p == PAIRS_E - 1 else IN_PAIR)[kind]

    def add_moe(layer):
        unit_at[f"moe{layer}"] = len(units)
        for p in range(PAIRS_E):
            for side in range(2):
                for kind in ("gate", "up"):
                    units.append(((kind, layer, 2 * p + side), ("job", pair_job(layer, p, f"GU{side}"))))
            for side in range(2):
                units.append((("down", layer, 2 * p + side), ("job", pair_job(layer, p, "Y1"))))

    add_moe(0)
    w_kv, w_q, w_o = a["w_kv"], a["b_w_q"][0], a["b_w_o"][0]
    add_units("w_v", [columns_of(w_kv, c) for c in (D, D + 512)], [FJ["att_v"] + n for n in (1, 3)])
    unit_at["w_kq"] = len(units)
    for n in range(4):
        units.append((columns_of((w_kv, w_q)[n // 2], 512 * (n % 2)), ("kq", 13 + n)))
    add_units("w_o", [columns_of(w_o, c) for c in (0, 512)], [FJ["att_o"] + n for n in (1, 3)])
    add_moe(1)
    w_in, w_out, w_up, w_down = a["w_in_2"][0], a["w_out_2"][0], a["w_up_2"][0], a["w_down_2"][0]
    add_units("w_z", [columns_of(w_in, c) for c in (0, 512)], [FJ["z"] + n for n in (3, 7)])
    add_units("w_xbc", [columns_of(w_in, OFF_XBC + c) for c in (0, 512, 1024)], [FJ["xbc"] + n for n in (3, 7, 11)])
    unit_at["w_sb_q"], unit_at["w_sb_k"] = len(units), len(units) + 2
    for n in range(4):
        units.append((columns_of(w_in, (OFF_Q, OFF_K)[n // 2] + 512 * (n % 2)), ("qk", 4 * n + 4)))
    add_units("w_sb_v", [columns_of(w_in, OFF_V + c) for c in (0, 512)], [FJ["sb_v"] + n for n in (3, 7)])
    add_units("w_out", [columns_of(w_out[part * D:part * D + D], half * 512) for half in range(2) for part in range(2)],
              [FJ["w_out"] + n for n in (3, 3, 7, 7)])
    add_units("w_up", [(columns_of(w_up, 2 * P * n, 2 * P), columns_of(w_up, D_FF + 2 * P * n, 2 * P))
                       for n in range(FC // 2)], [FJ["up"] + 4 * n + 3 for n in range(FC // 2)])
    unit_at["w_down"] = len(units)
    DOWN_UNITS = (FC + 3) // 4
    for n in range(DOWN_UNITS):
        rows_n = min(4, FC - 4 * n)
        units.append((("rows", w_down[4 * n * P:(4 * n + rows_n) * P].rearrange("(k p) n -> p k n", p=P), rows_n),
                      ("w_down", n + 1)))

    q_slot, k_slot = unit_at["w_z"] % RING, (unit_at["w_z"] + 1) % RING
    slots, before, landed = [], [], []
    for u in range(len(units)):
        if u < unit_at["w_sb_q"]:
            slots.append(u % RING)
        else:
            others = [s % RING for s in range(unit_at["w_sb_q"], unit_at["w_sb_q"] + RING)
                      if s % RING not in (q_slot, k_slot)]
            slots.append(others[(u - unit_at["w_sb_q"]) % len(others)])
        same = [v for v in range(u) if slots[v] == slots[u]]
        before.append(same[-1] if same else None)
        src = units[u][0]
        dmas = 2 if isinstance(src, tuple) and not isinstance(src[0], str) else 1
        landed.append((landed[same[-1]] if same else 0) + 16 * dmas)

    def slot(u):
        return ring[:, slots[u], :]

    def slot_k(u, n=512):
        return slot(u).rearrange("p (k n) -> p k n", n=n)

    def unit_ready(u):
        nc.tensor.wait_ge(slot_loaded[slots[u]], landed[u])

    block = ctx.enter_context(nc.Block())

    kq_done, kq_out = sem("kq_done"), sem("kq_out")
    qk_done, qk_out, down_ready = sem("qk_done"), sem("qk_out"), sem("down_ready")

    @block.sync
    def _(sp):
        def slot_freed(u, i=0):
            if before[u] is None:
                return
            free = units[before[u]][1]
            if free[0] == "job":
                sp.wait_ge(job_done, free[1] + 1 + PAIR_JOBS * i)
            elif free[0] == "kq":
                sp.wait_ge(kq_done, free[1])
            elif free[0] == "qk":
                sp.wait_ge(qk_done, free[1])
            elif free[0] == "w_down":
                sp.wait_ge(down_ready, free[1])

        def load(u, src, dst=None):
            sp.dma_start(slot_k(u) if dst is None else dst, src).then_inc(slot_loaded[slots[u]], 16)

        def load_expert(u, kind, layer, e):
            if kind == "down":
                src = a["moe_w_down"][layer, e if isinstance(e, int) else bass.ds(e, 1)]
                src = src.rearrange("(k p) n -> p k n" if isinstance(e, int) else "a (k p) n -> p (a k) n", p=P)
                load(u, src, slot_k(u, D))
            else:
                src = a[f"moe_w_{kind}"][layer, e if isinstance(e, int) else bass.ds(e, 1)]
                src = src.rearrange("(k p) n -> p k n" if isinstance(e, int) else "a (k p) n -> p (a k) n", p=P)
                load(u, src)

        sp.dma_start(x_nat[:, 1:3, :], a["x"][0].rearrange("(t p) n -> p t n", p=P)).then_inc(x_loaded, 16)
        u = 0
        while u < len(units):
            src = units[u][0]
            if isinstance(src, tuple) and src[0] == "gate" and src[2] == 2:
                with sp.Fori(0, PAIRS_E - 1) as i:
                    for n in range(RING):
                        slot_freed(u + n, i)
                        load_expert(u + n, units[u + n][0][0], src[1], i * 2 + units[u + n][0][2])
                u += RING * (PAIRS_E - 1)
                continue
            if u == 1:
                sp.wait_ge(rows_sent, 1)
            slot_freed(u)
            if isinstance(src, tuple) and src[0] in ("gate", "up", "down"):
                load_expert(u, *src)
            elif isinstance(src, tuple) and src[0] == "rows":
                load(u, src[1], slot_k(u, D)[:, 0:src[2], :])
            elif isinstance(src, tuple):
                for side in range(2):
                    sp.dma_start(slot_k(u)[:, :, side * 256:side * 256 + 256], src[side]).then_inc(
                        slot_loaded[slots[u]], 16)
            else:
                load(u, src)
            u += 1

    stages = []
    left = [0]
    norm_count = [0, 0]
    compute = (nc.tensor, nc.scalar, nc.vector, nc.gpsimd)

    def stage(f):
        stages.append(f)
        return f

    def next_stage():
        n = left[0] = left[0] + 1

        def meet(eng):
            eng.drain().then_inc(stage_left, 1)
            eng.wait_ge(stage_left, len(compute) * n)

        block.tensor(meet)
        block.scalar(meet)
        block.vector(meet)
        block.gpsimd(meet)

    def transposes_pe(first, tiles, src, ready=None):
        j = first
        for t in tiles:
            n = TILE_N[t]
            if ready is not None:
                ready(t)
            for half in range(2):
                take_bank(j)
                for c in range(4):
                    at = (4 * half + c) * P
                    last = nc.tensor.transpose(bank(j)[:, c * P:c * P + n], src(t)[0:n, at:at + P], ident[0:n, 0:n])
                last.then_inc(job_done, 1)
                j += 1

    def transposes_out(first, tiles, dst, gain=None):
        act = nc.scalar
        j = first
        for t in tiles:
            n, at = TILE_N[t], TILE_AT[t]
            for half in range(2):
                job_ready(act, j)
                src = bank(j).rearrange("p (c t) -> p c t", c=4)[:, :, 0:n]
                if gain is None:
                    act.activation(dst[:, 4 * half:4 * half + 4, at:at + n], src, ACT.Copy).then_inc(
                        bank_free[j % BANKS], 1)
                else:
                    for c in range(4):
                        last = act.activation(dst[:, 4 * half + c, at:at + n], src[:, c, :], ACT.Copy,
                                              scale=column(gain, 4 * half + c))
                    last.then_inc(bank_free[j % BANKS], 1)
                j += 1

    def load_norm(k, gain, bias=None):
        act = nc.scalar
        norm_count[k % 2] += 32
        act.dma_start(norm_rows[:, k % 2, 0, :], gain.partition_broadcast(P)).then_inc(norm_loaded[k % 2], 16)
        b = gain if bias is None else bias
        act.dma_start(norm_rows[:, k % 2, 1, :], b.partition_broadcast(P)).then_inc(norm_loaded[k % 2], 16)

    rsqrt_n = [0]

    def next_sqrt():
        rsqrt_n[0] += 1
        return rsqrt_n[0]

    variances = [0]

    def sqrt_of(act, values, scale, eps):
        act.preload_act_table(ACT.Sqrt)
        variances[0] += 1
        act.wait_ge(var_ready, variances[0])
        p = values.shape[0]
        bias = eps_cols[0:p, 0:1] if eps == LN_EPS else eps_cols[0:p, 1:2]
        act.activation(values, values, ACT.Sqrt, bias=bias, scale=scale).then_inc(std_ready, 1)

    def reciprocal_of(dve, values, n):
        dve.wait_ge(std_ready, n)
        dve_step(dve.reciprocal(values, values))

    def layer_norm(k, name, normed, last=False):
        mean_var = small[:, 2:6].rearrange("p (t s) -> p t s", s=2)
        root = next_sqrt()

        @block.vector
        def _(dve):
            dve.wait_ge(norm_loaded[k % 2], 32 * (k // 2 + 1))
            dve.wait_ge(stats_ready, 4 * (k + 1))
            for t in (1, 2):
                dve_last = dve.bn_aggr(small[:, 2 * t:2 * t + 2], stats[:, t, :, :])
            dve_last.then_inc(var_ready, 1)
            reciprocal_of(dve, mean_var[:, :, 1], root)
            for t in (1, 2):
                dve_step(dve.scalar_tensor_tensor(x_nat[:, t, :], x_nat[:, t, :], small[:, 2 * t:2 * t + 1],
                                                  norm_rows[:, k % 2, 0, :], ALU.subtract, ALU.mult))
                dve.scalar_tensor_tensor(x_nat[:, t, :], x_nat[:, t, :], small[:, 2 * t + 1:2 * t + 2],
                                         norm_rows[:, k % 2, 1, :], ALU.mult, ALU.add).then_inc(normed, 1)

        block.scalar(lambda act: sqrt_of(act, mean_var[:, :, 1], 1.0, LN_EPS))
        if last:
            return

        @block.tensor
        def _(pe):
            transposes_pe(FJ[name], (1, 2), lambda t: x_nat[:, t, :], lambda t: pe.wait_ge(normed, t))

        @block.scalar
        def _(act):
            transposes_out(FJ[name], (1, 2), xT)

    def project_natural(first, u0, lhs, tiles, k_chunks, bias=None, ready=None):
        j = first
        for half in range(2):
            unit_ready(u0 + half)
            for t in tiles:
                n, at = TILE_N[t], TILE_AT[t]
                take_bank(j)
                if ready is not None and half == 0:
                    ready(t)
                pairs = [(lhs[:, k, at:at + n], slot_k(u0 + half)[:, k, :]) for k in range(k_chunks)]
                if bias is not None:
                    pairs.append((ones[0:1, 0:n], bias[:, half * 512:half * 512 + 512]))
                products(bank(j)[0:n, :], pairs).then_inc(job_done, 1)
                j += 1

    def project_turned(first, parts, turned, tiles=(0, 1, 2)):
        for half in range(2):
            chunks = range(4 * half, 4 * half + 4)
            for i, (*part_units, src, ready) in enumerate(parts):
                if half == 0 and ready is not None:
                    ready()
                unit_ready(part_units[half])
                for c in chunks:
                    if i == 0:
                        take_bank(first + c)
                    for k in range(KC):
                        last = nc.tensor.matmul(bank(first + c)[:, 0:L],
                                                slot_k(part_units[half])[:, k, (c % 4) * P:(c % 4) * P + P],
                                                src[:, k, :], start=(i == 0 and k == 0),
                                                stop=(i == len(parts) - 1 and k == KC - 1))
                    if i == len(parts) - 1:
                        last.then_inc(job_done, 1)
        j = first + KC
        for half in range(2):
            all_read_out(nc.tensor, first + 4 * half + 4)
            for t in tiles:
                n, at = TILE_N[t], TILE_AT[t]
                take_bank(j)
                for c in range(4):
                    last = nc.tensor.transpose(bank(j)[0:n, c * P:c * P + P], turned[:, 4 * half + c, at:at + n],
                                               ident[:, :])
                last.then_inc(job_done, 1)
                j += 1

    def turned_in(first, turned, function=ACT.Copy):
        for c in range(KC):
            job_ready(nc.scalar, first + c)
            nc.scalar.activation(turned[:, c, :], bank(first + c)[:, 0:L], function).then_inc(
                bank_free[(first + c) % BANKS], 1)

    def add_residual(first, tiles=(1, 2)):
        j = first
        for half in range(2):
            for t in tiles:
                job_ready(nc.vector, j)
                xs = x_nat[:, t, half * 512:half * 512 + 512]
                ins = nc.vector.scalar_tensor_tensor(xs, xs, ALPHA, bank(j), ALU.mult, ALU.add)
                ins.then_inc(bank_free[j % BANKS], 1)
                residual_stats(j, t, half)
                j += 1

    def residual_stats(j, t, half):
        nc.vector.wait_ge(bank_free[j % BANKS], j // BANKS + 1)
        nc.vector.bn_stats(stats[:, t, half, :], x_nat[:, t, half * 512:half * 512 + 512]).then_inc(stats_ready, 1)

    rows = carve(0, 4, P)
    flip = carve(14500, P)
    lam_rows, subln_rows = carve(14628, 4, HD), carve(14884, 2 * HD)
    b_pw2 = arena[0:1, 8000:8000 + D]
    buckets = arena[0:N_BUCKETS, 9100:9100 + 3 * P]
    by_distance = arena[0:HEADS, 9500:9500 + 3 * P]
    inputs_loaded = sem("inputs_loaded")
    INPUT_DMAS = 12
    rel_written = sem("rel_written")
    rows_cleared = sem("rows_cleared")

    @stage
    def constants():
        @block.gpsimd
        def _(pool):
            pool.memset(rows[:, :, :], 0.0).then_inc(rows_cleared, 1)
            pool_step(pool.memset(ident[:, :], 0.0))
            pool_step(pool.affine_select(out=ident[:, :], in_=ident[:, :], compare_op=ALU.not_equal, fill=1.0, base=0,
                                         pattern=[[-1, P]], channel_multiplier=1))
            pool_step(pool.memset(ones[:, :], 1.0))
            pool_step(pool.memset(flip, 0.0))
            pool_step(pool.affine_select(out=flip, in_=flip, compare_op=ALU.not_equal, fill=1.0,
                                         base=1 - P, pattern=[[1, P]], channel_multiplier=1))
            pool_step(pool.memset(by_distance, MASKED))
            pool_step(pool.memset(upto[:, :], 1.0))
            pool_step(pool.affine_select(out=upto[:, :], in_=upto[:, :], compare_op=ALU.is_ge, fill=0.0,
                                         base=0, pattern=[[1, P]], channel_multiplier=-1))
            pool_step(pool.memset(neg_ones[:, :], -1.0))
            pool_step(pool.affine_select(out=neg_from[:, :], in_=neg_ones[:, :], compare_op=ALU.is_ge, fill=0.0,
                                         base=0, pattern=[[-1, P]], channel_multiplier=1))
            pool_step(pool.memset(earlier[:, :, :], 1.0))
            pool_step(pool.affine_select(out=earlier[:, :, :], in_=earlier[:, :, :], compare_op=ALU.is_gt, fill=0.0,
                                         base=0, pattern=[[1, 4], [-1, 4]], channel_multiplier=0))
            pool_step(pool.memset(eps_cols[:, 0:1], LN_EPS))
            pool_step(pool.memset(eps_cols[:, 1:2], EPS))
            pool.nop().then_inc(consts_made, 1)

        @block.scalar
        def _(act):
            act.wait_ge(rows_cleared, 1)
            for tile, parts in enumerate(VEC_ROWS):
                at = 0
                for name, first, n in parts:
                    src = a[name]
                    src = src.rearrange("a b (c p) -> (a b c) p" if len(src.shape) == 3 else "a (c p) -> (a c) p", p=P)
                    act.dma_start(rows[at:at + n, tile, :], src[first:first + n, :]).then_inc(consts_loaded, 16)
                    at += n
            act.nop().then_inc(rows_sent, 1)
            transposes_out(FJ["conv_xT"], (1, 2), xT)
            job_ready(act, FJ["vec"])
            act.activation(vec[:, :], bank(FJ["vec"]), ACT.Copy).then_inc(bank_free[FJ["vec"] % BANKS], 1)

        @block.tensor
        def _(pe):
            pe.wait_ge(consts_made, 1)
            pe.wait_ge(x_loaded, 16)
            transposes_pe(FJ["conv_xT"], (1, 2), lambda t: x_nat[:, t, :])
            pe.wait_ge(consts_loaded, 16 * sum(len(r) for r in VEC_ROWS))
            take_bank(FJ["vec"])
            for tile in range(4):
                last = pe.transpose(bank(FJ["vec"])[:, tile * P:tile * P + P], rows[:, tile, :], ident[:, :])
            last.then_inc(job_done, 1)

    PAD = TAPS - 1
    glu = carve(0, KC, PAD + SEQ)
    conv = carve(2400, KC, SEQ)
    squares = carve(4500, KC, SEQ)
    sig = carve(6600, 2, SEQ)
    mean_b, rstd_b = carve(7200, SEQ), carve(7500, SEQ)
    sig_ready, glu_ready, conv_step = sem("sig_ready"), sem("glu_ready"), sem("conv_step")
    DIAGS = 30
    diags = carve(9900, DIAGS, P)
    pool_term = carve(13900, 2, SEQ)
    POOL_CHUNK, DVE_CHUNKS, PE_CHUNKS = 0, (range(1, 3), range(3, 6)), range(6, KC)
    diag_made, taps_used, pool_tap = sem("diag_made"), sem("taps_used"), sem("pool_tap")
    term_ready = sem("pool_term_ready")

    def diagonal(eng, n):
        if n >= DIAGS:
            m = n - DIAGS
            if m % TAPS == TAPS - 1:
                job_ready(eng, FJ["conv"] + m // TAPS)
            else:
                eng.wait_ge(taps_used, m + 1 - m // TAPS)
        chunk = PE_CHUNKS[n // TAPS]
        eng.activation(diags[:, n % DIAGS, :], ident[:, :], ACT.Copy,
                       scale=column("a_w_dw", (n % TAPS) * KC + chunk)).then_inc(diag_made, 1)

    conv_ready, centred, squared, conv_normed, act_ready = (
        sem("conv_ready"), sem("centred"), sem("squared"), sem("conv_normed"), sem("conv_activated"))

    @stage
    def conformer():
        root = next_sqrt()

        @block.tensor
        def _(pe):
            for n in range(KC):
                j, pair = FJ["glu"] + n, n // 4
                take_bank(j)
                for side in range(2):
                    u = 2 * pair + side
                    unit_ready(u)
                    last = products(bank(j)[:, side * SEQ:side * SEQ + SEQ],
                                    [(slot_k(u)[:, k, (n % 4) * P:(n % 4) * P + P], xT[:, k, META:L])
                                     for k in range(KC)])
                last.then_inc(job_done, 1)
            pe.wait_ge(inputs_loaded, INPUT_DMAS * 16)
            take_bank(FJ["iota"])
            products(bank(FJ["iota"])[:, 0:P], [(ones[:, :], upto[:, :])]).then_inc(job_done, 1)
            take_bank(FJ["relb"])
            products(bank(FJ["relb"])[0:HEADS, 0:3 * P], [(rel_w[:, :], buckets)]).then_inc(job_done, 1)
            for i, c in enumerate(PE_CHUNKS):
                j = FJ["conv"] + i
                take_bank(j)
                pe.wait_ge(glu_ready, c + 1)
                for tap in range(TAPS):
                    n = i * TAPS + tap
                    pe.wait_ge(diag_made, n + 1)
                    last = pe.matmul(bank(j)[:, 0:SEQ], diags[:, n % DIAGS, :], glu[:, c, tap:tap + SEQ],
                                     start=(tap == 0), stop=(tap == TAPS - 1))
                    last.then_inc(taps_used if tap < TAPS - 1 else job_done, 1)
            j = FJ["conv_mean"]
            all_read_out(pe, j)
            pe.wait_ge(conv_ready, 1)
            pe.wait_ge(pool_tap, TAPS)
            products(bank(j)[:, 0:SEQ], [(ones[:, :], conv[:, c, :]) for c in range(KC)]).then_inc(job_done, 1)
            j = FJ["conv_var"]
            take_bank(j)
            for c in range(KC):
                if c % 4 == 0:
                    pe.wait_ge(squared, c // 4 + 1)
                last = pe.matmul(bank(j)[:, 0:SEQ], ones[:, :], squares[:, c, :], start=(c == 0), stop=(c == KC - 1))
            last.then_inc(job_done, 1)
            j = FJ["pw2"]
            for half in range(2):
                unit_ready(unit_at["pw2"] + half)
                for t in (0, 1):
                    take_bank(j)
                    pe.matmul(bank(j), ones[0:1, :], b_pw2[:, half * 512:half * 512 + 512], start=True, stop=False)
                    for k in range(KC):
                        if half == 0 and t == 0:
                            pe.wait_ge(act_ready, k + 1)
                        last = pe.matmul(bank(j), conv[:, k, t * P:t * P + P], slot_k(unit_at["pw2"] + half)[:, k, :],
                                         start=False, stop=(k == KC - 1))
                    last.then_inc(job_done, 1)
                    j += 1

        @block.gpsimd
        def _(pool):
            c = POOL_CHUNK
            pool.wait_ge(glu_ready, c + 1)
            for tap in range(TAPS):
                src, w = glu[:, c, tap:tap + SEQ], column("a_w_dw", tap * KC + c)
                if tap == 0:
                    pool.tensor_scalar(conv[:, c, :], src, w, column("a_b_dw", c), ALU.mult, ALU.add).then_inc(
                        pool_tap, 1)
                    continue
                if tap >= 3:
                    pool.wait_ge(pool_tap, tap - 1)
                term = pool_term[:, tap % 2, :]
                pool.tensor_scalar(term, src, w, None, ALU.mult).then_inc(term_ready, 1)
                pool.wait_ge(term_ready, tap)
                pool.wait_ge(pool_tap, tap)
                pool.tensor_tensor(conv[:, c, :], conv[:, c, :], term, ALU.add).then_inc(pool_tap, 1)

        @block.scalar
        def _(act):
            for n in range(DIAGS):
                diagonal(act, n)
            for n in range(KC):
                j = FJ["glu"] + n
                job_ready(act, j)
                if n >= 2:
                    act.wait_ge(glu_ready, n - 1)
                act.activation(sig[:, n % 2, :], bank(j)[:, SEQ:2 * SEQ], ACT.Sigmoid,
                               bias=column("a_b_pw1", KC + n)).then_inc(sig_ready, 1)
                if n == 3:
                    act.dma_start(router_w[:, :, :], a["router_w"].rearrange("(k p) n -> p k n", p=P)).then_inc(
                        inputs_loaded, 16)
                    act.dma_start(router_b[:, :], a["router_bias"].partition_broadcast(P)).then_inc(inputs_loaded, 16)
                    act.dma_start(b_pw2, a["a_b_pw2"]).then_inc(inputs_loaded, 16)
                    for row, name in enumerate(("ssd_dt_bias_2", "ssd_a_log_2", "ssd_d_2")):
                        act.dma_start(ssd_rows[:, row, :], a[name][0].partition_broadcast(P)).then_inc(inputs_loaded, 16)
                    act.dma_start(w_dt[:, :, :], a["w_in_2"][0][:, OFF_DT:OFF_Q].rearrange("(k p) n -> p k n", p=P),
                                  ).then_inc(inputs_loaded, 16)
                    act.dma_start(x_nat[0:META, 0, :], a["meta_tokens_2"]).then_inc(inputs_loaded, 16)
                    act.dma_start(lam_rows[:, :, :], a["b_lambda"][0].partition_broadcast(P)).then_inc(inputs_loaded, 16)
                    act.dma_start(subln_rows, a["b_subln_g"][0].partition_broadcast(P)).then_inc(inputs_loaded, 16)
                    act.dma_start(rel_w[:, :], a["rel_bias"]).then_inc(inputs_loaded, 16)
                    act.dma_start(buckets, a["buckets"]).then_inc(inputs_loaded, 16)
                    load_norm(0, a["ln_mix_g"][0], a["ln_mix_b"][0])
            job_ready(act, FJ["iota"])
            act.activation(counting[:, :], bank(FJ["iota"])[:, 0:P], ACT.Copy).then_inc(
                bank_free[FJ["iota"] % BANKS], 1)
            job_ready(act, FJ["relb"])
            act.activation(by_distance[:, 0:SEQ], bank(FJ["relb"])[0:HEADS, 0:SEQ], ACT.Copy).then_inc(
                bank_free[FJ["relb"] % BANKS], 1)
            act.wait_ge(bank_free[FJ["relb"] % BANKS], FJ["relb"] // BANKS + 1)
            act.dma_start(rel_scratch, by_distance).then_inc(rel_written, 16)

            def taps_out(i):
                j, c = FJ["conv"] + i, PE_CHUNKS[i]
                job_ready(act, j)
                act.activation(conv[:, c, :], bank(j)[:, 0:SEQ], ACT.Identity, bias=column("a_b_dw", c)).then_inc(
                    bank_free[j % BANKS], 1)

            for n in range(DIAGS, len(PE_CHUNKS) * TAPS):
                if n >= TAPS and n % TAPS == 12:
                    taps_out(n // TAPS - 1)
                diagonal(act, n)
            taps_out(len(PE_CHUNKS) - 1)
            act.wait_ge(rel_written, 16)
            for half in range(2):
                act.wait_ge(centred, half + 1)
                act.activation(squares[:, 4 * half:4 * half + 4, :], conv[:, 4 * half:4 * half + 4, :],
                               ACT.Square).then_inc(squared, 1)
            sqrt_of(act, rstd_b, 1.0 / D, LN_EPS)
            act.preload_act_table(ACT.Silu)
            for c in range(KC):
                act.wait_ge(conv_normed, c // 4 + 1)
                act.activation(conv[:, c, :], conv[:, c, :], ACT.Silu, bias=column("a_ln_b", c),
                               scale=column("a_ln_g", c)).then_inc(act_ready, 1)

        @block.vector
        def _(dve):
            dve_step(dve.memset(glu[:, :, 0:PAD], 0.0))

            def gated(n):
                j = FJ["glu"] + n
                dve.wait_ge(sig_ready, n + 1)
                dve.scalar_tensor_tensor(glu[:, n, PAD:PAD + SEQ], bank(j)[:, 0:SEQ], column("a_b_pw1", n),
                                         sig[:, n % 2, :], ALU.add, ALU.mult).then_inc(glu_ready, 1)
                dve.wait_ge(glu_ready, n + 1)
                dve.nop().then_inc(bank_free[j % BANKS], 1)

            for n in range(3):
                gated(n)
            n, next_gated = 0, 3
            for chunks in DVE_CHUNKS:
                while next_gated <= chunks[-1]:
                    gated(next_gated)
                    next_gated += 1
                for tap in range(TAPS):
                    if tap % 10 == 9 and next_gated < KC:
                        gated(next_gated)
                        next_gated += 1
                    for i, c in enumerate(chunks):
                        src = glu[:, c, tap:tap + SEQ]
                        w = column("a_w_dw", tap * KC + c)
                        if tap == 0:
                            ins = dve.tensor_scalar(conv[:, c, :], src, w, column("a_b_dw", c), ALU.mult, ALU.add)
                        else:
                            dve.wait_ge(conv_step, n - len(chunks) + 1)
                            ins = dve.scalar_tensor_tensor(conv[:, c, :], src, w, conv[:, c, :], ALU.mult, ALU.add)
                        ins.then_inc(conv_step, 1)
                        n += 1
            dve.wait_ge(conv_step, n)
            dve.nop().then_inc(conv_ready, 1)
            j = FJ["conv_mean"]
            job_ready(dve, j)
            ins = dve.tensor_scalar(mean_b, bank(j)[:, 0:SEQ], 1.0 / D, None, ALU.mult)
            dve_step(ins)
            dve.nop().then_inc(bank_free[j % BANKS], 1)
            for half in range(2):
                part = conv[:, 4 * half:4 * half + 4, :]
                dve.tensor_tensor(part, part, mean_b.unsqueeze(1).broadcast_to([P, 4, SEQ]),
                                  ALU.subtract).then_inc(centred, 1)
            j = FJ["conv_var"]
            job_ready(dve, j)
            dve.tensor_copy(rstd_b, bank(j)[:, 0:SEQ]).then_inc(var_ready, 1)
            reciprocal_of(dve, rstd_b, root)
            dve.nop().then_inc(bank_free[j % BANKS], 1)
            for half in range(2):
                part = conv[:, 4 * half:4 * half + 4, :]
                dve.tensor_tensor(part, part, rstd_b.unsqueeze(1).broadcast_to([P, 4, SEQ]),
                                  ALU.mult).then_inc(conv_normed, 1)
            add_residual(FJ["pw2"])

    normed = [sem(f"normed{k}") for k in range(4)]

    @stage
    def mix_norm0():
        layer_norm(0, "mix0_xT", normed[0])

    aff, sel = carve(0, 2, EXPERTS), carve(40, 2, EXPERTS)
    beats = carve(80, 2, EXPERTS)
    not_less, more, two_best = carve(10790, 8 * 16), carve(10920, 8 * 16), carve(11050, 2, EXPERTS)
    group_score, group_lost = carve(140, 2, GROUPS), carve(150, 2, GROUPS)
    total = carve(160, 2)
    member_rank, slot_of = carve(14330, 3, EXPERTS), carve(14380, 2, EXPERTS)
    silu_g, hid, hidT = carve(200, 2, DE), carve(1230, 2, DE), carve(2260, 2, 4 * SEATS)
    tokens = carve(3290, KC, P)
    seats = carve(4320, 2, P)
    gate_col = carve(14415, 1)
    slot_cell, gate_cell = carve(14420, 2, 2), carve(14430, 2, 2)
    base = carve(4640, 2, D)
    seatsT = carve(10790, 2 * P)
    y_pair = carve(13300, D)
    over_w, over_y, over_hi = carve(6690, 4096), carve(11820, D), carve(13000, 2, P)
    over_slot, over_gate = carve(14440, 2), carve(14445, 2, 1)
    over_hidT = carve(11050, DE)

    def route(layer):
        aff_ready, won_ready = sem(f"aff_ready{layer}"), sem(f"won_ready{layer}")
        J = FJ[f"route{layer}"]

        @block.scalar
        def _(act):
            job_ready(act, J)
            act.activation(aff[:, :, :], bank(J)[:, 0:2 * EXPERTS].rearrange("p (t e) -> p t e", t=2),
                           ACT.Sigmoid).then_inc(aff_ready, 1)
            act.activation(base[:, :, :], x_nat[:, 1:3, :], ACT.Copy, scale=ALPHA)

        @block.vector
        def _(dve):
            if layer == 0:
                dve.wait_ge(inputs_loaded, INPUT_DMAS * 16)
            dve.wait_ge(aff_ready, 1)
            dve.tensor_tensor(sel, aff, router_b[:, :].unsqueeze(1).broadcast_to([P, 2, EXPERTS]),
                              ALU.add).then_inc(bank_free[J % BANKS], 1)
            dve.wait_ge(bank_free[J % BANKS], J // BANKS + 1)
            def ranks(dst, score, n):
                shape = [P, n, 4, 4]
                own, other = score.unsqueeze(3).broadcast_to(shape), score.unsqueeze(2).broadcast_to(shape)
                ge, gt = (x[:, 0:16 * n].rearrange("p (s e f) -> p s e f", s=n, e=4) for x in (not_less, more))
                dve.tensor_tensor(gt, other, own, ALU.is_gt)
                dve_step(dve.tensor_tensor(ge, other, own, ALU.is_ge))
                dve_step(dve.tensor_tensor(ge, ge, gt, ALU.subtract))
                dve_step(dve.tensor_tensor(ge, ge, earlier[:, :, :].unsqueeze(1).broadcast_to(shape), ALU.mult))
                dve_step(dve.tensor_tensor(ge, ge, gt, ALU.add))
                dve_step(dve.tensor_reduce(dst, ge, AX_X, ALU.add))

            bg = beats.rearrange("p t (g e) -> p t g e", g=GROUPS)
            sets_of = lambda x: x.rearrange("p t (g e) -> p (t g) e", g=GROUPS)
            ranks(sets_of(beats), sets_of(sel), 2 * GROUPS)
            dve_step(dve.scalar_tensor_tensor(two_best, beats, 1.5, sel, ALU.is_lt, ALU.mult))
            dve_step(dve.tensor_reduce(group_score.rearrange("p t g -> p (t g)"), sets_of(two_best), AX_X, ALU.add))
            ranks(group_lost, group_score, 2)
            dve.tensor_scalar(beats, beats, 1.5, None, ALU.is_lt)
            dve_step(dve.tensor_scalar(group_lost, group_lost, 0.5, None, ALU.is_lt))
            won = group_lost
            dve.tensor_tensor(bg, bg, won.unsqueeze(3).broadcast_to([P, 2, GROUPS, PER_GROUP]),
                              ALU.mult).then_inc(won_ready, 1)
            dve.wait_ge(won_ready, 1)
            dve_step(dve.tensor_tensor(gates[:, :, :], beats, aff, ALU.mult))
            dve_step(dve.tensor_reduce(total, gates[:, :, :], AX_X, ALU.add))
            dve_step(dve.reciprocal(total, total))
            dve_step(dve.tensor_tensor(gates[:, :, :], gates[:, :, :],
                                       total.unsqueeze(2).broadcast_to([P, 2, EXPERTS]), ALU.mult))
            job_ready(dve, J + 1)
            dve.tensor_copy(member_rank, bank(J + 1)[:, 0:3 * EXPERTS].rearrange(
                "p (t e) -> p t e", t=3)).then_inc(bank_free[(J + 1) % BANKS], 1)
            dve.wait_ge(bank_free[(J + 1) % BANKS], (J + 1) // BANKS + 1)
            dve_step(dve.tensor_tensor(slot_of, beats, member_rank[:, 0:2, :], ALU.mult))
            dve_step(dve.tensor_reduce(total[:, 0:1], member_rank[:, 2, :], AX_X, ALU.max))
            dve_step(dve.tensor_copy(over_flag[:, :], total[:, 0:1]))

        @block.tensor
        def _(pe):
            take_bank(J)
            for t in (1, 2):
                at = TILE_AT[t]
                all_read_out(pe, FJ[f"mix{layer}_xT"] + 2 * t)
                last = products(bank(J)[:, (t - 1) * EXPERTS:t * EXPERTS],
                                [(xT[:, k, at:at + P], router_w[:, k, :]) for k in range(KC)])
            last.then_inc(job_done, 1)
            take_bank(J + 1)
            pe.wait_ge(won_ready, 1)
            n = EXPERTS
            products(bank(J + 1)[:, 0:n], [(upto[:, :], beats[:, 0, :])])
            products(bank(J + 1)[:, n:2 * n], [(ones[:, :], beats[:, 0, :]), (upto[:, :], beats[:, 1, :])])
            products(bank(J + 1)[:, 2 * n:3 * n],
                     [(ones[:, :], beats[:, 0, :]), (ones[:, :], beats[:, 1, :])]).then_inc(job_done, 1)

    def gather(dst_at, tokens_dst, sources=seats):
        for c in range(4):
            k = dst_at * 4 + c
            last = products(tokens_dst[:, c * P:c * P + P],
                            [(x_nat[:, t + 1, k * P:k * P + P], sources[:, t, :]) for t in range(2)])
        return last

    def overflow(layer):
        names = ("w_free", "w_loaded", "cell", "seated", "gathered", "tokens", "silu", "hid", "turned", "hidT", "y",
                 "scattered", "added")
        (w_free, w_loaded, cell_ready, seated, gathered, tokens_out, silu_out, hid_out, turned, hidT_out, y_out,
         scattered, added) = (sem(f"over_{x}{layer}") for x in names)

        over_left = sem(f"over_left{layer}")

        def where_over(eng, body):
            count = eng.value_load(over_flag[0:1, 0:1], min_val=0, max_val=SEQ)
            with eng.If(count > SEATS):
                body()
                eng.drain().then_inc(over_left, 1)
                eng.wait_ge(over_left, 3)

        @block.tensor
        def _(pe):
            def body():
                pe.nop().then_inc(w_free, 1)
                for r in range(2):
                    with pe.Fori(0, EXPERTS) as e:
                        i = e + r * EXPERTS
                        pe.wait_ge(seated, i + 1)
                        for half in range(2):
                            gather(half, psum[:, half, :])
                        products(psum[:, 2, 0:1], [(seats[:, t, :], over_gate[:, t, :]) for t in range(2)])
                        for t in range(2):
                            last = pe.transpose(psum[:, 3, t * P:t * P + P], seats[:, t, :], ident[:, :])
                        last.then_inc(gathered, 1)
                        pe.wait_ge(tokens_out, i + 1)
                        for n in range(2):
                            pe.wait_ge(w_loaded, i * 48 + 16 * (n + 1))
                            w = over_w.rearrange("p (k n) -> p k n", n=512)
                            products(psum[:, n, :], [(tokens[:, k, :], w[:, k, :]) for k in range(KC)]).then_inc(w_free, 1)
                        pe.wait_ge(hid_out, i + 1)
                        for k in range(DE // P):
                            last = pe.transpose(psum[:, 2, k * P:k * P + P], hid[:, 0, k * P:k * P + P], ident[:, :])
                        last.then_inc(turned, 1)
                        pe.wait_ge(hidT_out, i + 1)
                        pe.wait_ge(w_loaded, i * 48 + 48)
                        w = over_w.rearrange("p (k n) -> p k n", n=D)
                        for half in range(2):
                            last = products(psum[:, 4 + half, :],
                                            [(over_hidT[:, k * P:k * P + P], w[:, k, half * 512:half * 512 + 512])
                                             for k in range(DE // P)])
                        last.then_inc(w_free, 1)
                        pe.wait_ge(y_out, i + 1)
                        for t in range(2):
                            for half in range(2):
                                last = products(psum[:, 4 + 2 * t + half, :],
                                                [(seatsT[:, t * P:t * P + P], over_y[:, half * 512:half * 512 + 512])])
                        last.then_inc(scattered, 1)

            where_over(pe, body)

        @block.scalar
        def _(act):
            def body():
                for r in range(2):
                    with act.Fori(0, EXPERTS) as e:
                        i = e + r * EXPERTS
                        def load(n, name, width):
                            act.wait_ge(w_free, i * 3 + n + 1)
                            src = a[name][layer, bass.ds(e, 1)].rearrange("a (k p) n -> p (a k) n", p=P)
                            act.dma_start(over_w.rearrange("p (k n) -> p k n", n=width), src).then_inc(w_loaded, 16)

                        load(0, "moe_w_gate", DE)
                        act.wait_ge(gathered, i + 1)
                        for half in range(2):
                            act.activation(tokens[:, 4 * half:4 * half + 4, :],
                                           psum[:, half, :].rearrange("p (c s) -> p c s", c=4), ACT.Copy)
                        act.activation(gate_col, psum[:, 2, 0:1], ACT.Copy)
                        act.activation(seatsT, psum[:, 3, 0:2 * P], ACT.Copy).then_inc(tokens_out, 1)
                        load(1, "moe_w_up", DE)
                        act.activation(silu_g[:, 0, :], psum[:, 0, :], ACT.Silu).then_inc(silu_out, 1)
                        load(2, "moe_w_down", D)
                        act.wait_ge(turned, i + 1)
                        act.activation(over_hidT, psum[:, 2, :], ACT.Copy).then_inc(hidT_out, 1)
                        act.wait_ge(w_free, i * 3 + 4)
                        act.activation(over_y.rearrange("p (b n) -> p b n", b=2), psum[:, 4:6, :], ACT.Copy).then_inc(
                            y_out, 1)

            where_over(act, body)

        @block.vector
        def _(dve):
            def body():
                for r in range(2):
                    ins = dve.tensor_scalar(over_hi[:, r, :], counting[:, :], float(SEATS + P * r), None, ALU.add)
                ins.then_inc(added, 1)
                dve.wait_ge(added, 1)
                for r in range(2):
                    with dve.Fori(0, EXPERTS) as e:
                        i = e + r * EXPERTS
                        dve.tensor_copy(over_slot.unsqueeze(2), slot_of[:, :, bass.ds(e, 1)])
                        dve.tensor_copy(over_gate, gates[:, :, bass.ds(e, 1)]).then_inc(cell_ready, 1)
                        dve.wait_ge(cell_ready, i + 1)
                        for t in range(2):
                            ins = dve.tensor_scalar(seats[:, t, :], over_hi[:, r, :], over_slot[:, t:t + 1], None, ALU.is_equal)
                        ins.then_inc(seated, 1)
                        dve.wait_ge(w_free, i * 3 + 3)
                        dve.wait_ge(silu_out, i + 1)
                        dve.scalar_tensor_tensor(hid[:, 0, :], psum[:, 1, :], gate_col, silu_g[:, 0, :],
                                                 ALU.mult, ALU.mult).then_inc(hid_out, 1)
                        dve.wait_ge(scattered, i + 1)
                        for t in range(2):
                            for half in range(2):
                                part = base[:, t, half * 512:half * 512 + 512]
                                ins = dve.tensor_tensor(part, part, psum[:, 4 + 2 * t + half, :], ALU.add)
                        ins.then_inc(added, 1)
                        dve.wait_ge(added, i + 2)

            where_over(dve, body)

    def experts(layer):
        B, U = FJ[f"moe{layer}"], unit_at[f"moe{layer}"]
        LAST = PAIRS_E - 1
        cell_ready, seats_ready, silu_ready, scattered = (
            sem(f"cell_ready{layer}"), sem(f"seats_ready{layer}"), sem(f"silu_ready{layer}"), sem(f"scattered{layer}"))
        cleared = sem(f"sum_cleared{layer}")
        LOW, HIGH = slice(0, SEATS), slice(SEATS, 2 * SEATS)

        def job(kind, p):
            return pair_job(layer, p, kind)

        def done(eng, j, i=0):
            eng.wait_ge(job_done, j + 1 + i * PAIR_JOBS)

        def read_out(eng, j, i=0):
            eng.wait_ge(bank_free[j % BANKS], j // BANKS + 1 + i * (PAIR_JOBS // BANKS))

        def gathers(p):
            return (B, B + 1) if p == 0 else (job("X0", p - 1), job("X1", p - 1))

        @block.vector
        def _(dve):
            def seat(p, i=0):
                two = slice(2 * p, 2 * p + 2) if isinstance(i, int) else bass.ds(i * 2 + 2 * p, 2)
                dve.tensor_copy(slot_cell, slot_of[:, :, two])
                dve.tensor_copy(gate_cell, gates[:, :, two]).then_inc(cell_ready, 1)
                dve.wait_ge(cell_ready, i + p + 1)
                for t in range(2):
                    for side in range(2):
                        ins = dve.tensor_scalar(seats[:, t, side * SEATS:side * SEATS + SEATS], counting[:, 0:SEATS],
                                                slot_cell[:, t, side:side + 1], None, ALU.is_equal)
                ins.then_inc(seats_ready, 1)

            def hidden(side, p, i=0):
                j = job(f"GU{side}", p)
                dve.wait_ge(silu_ready, 2 * p + side + 1 + i * 2)
                dve.tensor_tensor(hid[HIGH, side, :], bank(j)[HIGH, :], silu_g[HIGH, side, :],
                                  ALU.mult).then_inc(bank_free[j % BANKS], 1)

            def turned_seats(p, i=0):
                j = job("S", p)
                done(dve, j, i)
                dve.tensor_copy(gate_col[LOW], bank(j)[LOW, 2 * P:2 * P + 1])
                dve.tensor_copy(gate_col[HIGH], bank(j)[HIGH, 2 * P + 1:2 * P + 2])
                dve.tensor_copy(seatsT, bank(j)[:, 0:2 * P]).then_inc(bank_free[j % BANKS], 1)
                read_out(dve, j, i)

            def gathered(j, i=0):
                done(dve, j, i)
                dve.tensor_copy(tokens[:, 4:8, :], bank(j).rearrange("p (c s) -> p c s", c=4)).then_inc(
                    bank_free[j % BANKS], 1)

            def summed(p, i=0):
                j = job("Y1", p)
                done(dve, j, i)
                dve.tensor_scalar(y_pair[:, 512:D], bank(j), gate_col, None, ALU.mult).then_inc(
                    bank_free[j % BANKS], 1)

            def pair(p, i=0):
                hidden(0, p, i)
                turned_seats(p, i)
                if p < LAST:
                    seat(p + 1, i)
                hidden(1, p, i)
                if p < LAST:
                    gathered(job("X1", p), i)
                summed(p, i)

            seat(0)
            gathered(B + 1)
            dve.memset(psum[:, BANKS:2 * BANKS, :], 0.0).then_inc(cleared, 1)
            pair(0)
            with dve.Fori(0, LAST - 1) as i:
                pair(1, i)
            pair(LAST)
            for t in range(2):
                for half in range(2):
                    dve.wait_ge(scattered, PAIRS_E + 2 * t + half)
                    cols = slice(half * 512, half * 512 + 512)
                    dve_step(dve.tensor_tensor(x_nat[:, t + 1, cols], base[:, t, cols],
                                               psum[:, BANKS + 2 * t + half, :], ALU.add))
                    dve.bn_stats(stats[:, t + 1, half, :], x_nat[:, t + 1, cols]).then_inc(stats_ready, 1)

        @block.scalar
        def _(act):
            def silu(side, p, i=0):
                j = job(f"GU{side}", p)
                done(act, j, i)
                act.activation(silu_g[HIGH, side, :], bank(j)[LOW, :], ACT.Silu).then_inc(silu_ready, 1)

            def gathered(j, i=0):
                done(act, j, i)
                act.activation(tokens[:, 0:4, :], bank(j).rearrange("p (c s) -> p c s", c=4), ACT.Copy).then_inc(
                    bank_free[j % BANKS], 1)

            def pair(p, i=0):
                silu(0, p, i)
                silu(1, p, i)
                if p < LAST:
                    gathered(job("X0", p), i)
                j = job("T", p)
                done(act, j, i)
                act.activation(hidT, bank(j).rearrange("p (e n) -> p e n", e=2), ACT.Copy).then_inc(
                    bank_free[j % BANKS], 1)
                read_out(act, job("S", p), i)
                j = job("Y0", p)
                done(act, j, i)
                act.activation(y_pair[:, 0:512], bank(j), ACT.Copy, scale=gate_col).then_inc(bank_free[j % BANKS], 1)

            gathered(B)
            pair(0)
            with act.Fori(0, LAST - 1) as i:
                pair(1, i)
            pair(LAST)

        @block.tensor
        def _(pe):
            def free(j, i=0):
                pe.wait_ge(bank_free[j % BANKS], j // BANKS + i * (PAIR_JOBS // BANKS))

            def wait_unit(u, i):
                pe.wait_ge(slot_loaded[slots[u]], landed[u] + i * 16)

            def fetch(half, p, i=0):
                j = gathers(p)[half]
                pe.wait_ge(seats_ready, p + 1 + i)
                free(j, i)
                gather(half, bank(j)).then_inc(job_done, 1)

            def gate_up(side, p, i=0):
                j = job(f"GU{side}", p)
                u = U + RING * p + 2 * side
                free(j, i)
                wait_unit(u, i)
                wait_unit(u + 1, i)
                for k in range(KC):
                    for n, part in enumerate((LOW, HIGH)):
                        last = pe.matmul(bank(j)[part, :], tokens[:, k, side * SEATS:side * SEATS + SEATS],
                                         slot_k(u + n)[:, k, :], start=(k == 0), stop=(k == KC - 1))
                last.then_inc(job_done, 1)

            def turn_seats(p, i=0):
                j = job("S", p)
                free(j, i)
                for t in range(2):
                    pe.transpose(bank(j)[:, t * P:t * P + P], seats[:, t, :], ident[:, :])
                products(bank(j)[:, 2 * P:2 * P + 2], [(seats[:, t, :], gate_cell[:, t, :]) for t in range(2)]
                         ).then_inc(job_done, 1)

            def turn(p, i=0):
                j = job("T", p)
                free(j, i)
                read_out(pe, job("GU0", p), i)
                read_out(pe, job("GU1", p), i)
                for side in range(2):
                    for k in range(DE // P):
                        at = (4 * side + k) * SEATS
                        last = pe.matmul(bank(j)[:, at:at + SEATS], hid[HIGH, side, k * P:k * P + P],
                                         ident[HIGH, HIGH], start=True, stop=True)
                last.then_inc(job_done, 1)

            def down(p, i=0):
                u = U + RING * p + 4
                wait_unit(u, i)
                wait_unit(u + 1, i)
                read_out(pe, job("T", p), i)
                for half in range(2):
                    j = job(f"Y{half}", p)
                    free(j, i)
                    for k in range(DE // P):
                        for side, part in enumerate((LOW, HIGH)):
                            last = pe.matmul(bank(j)[part, :], hidT[:, side, k * SEATS:k * SEATS + SEATS],
                                             slot_k(u + side, D)[:, k, half * 512:half * 512 + 512], start=(k == 0),
                                             stop=(k == DE // P - 1))
                    last.then_inc(job_done, 1)

            def scatter(p, i=0):
                read_out(pe, job("Y0", p), i)
                read_out(pe, job("Y1", p), i)
                for t in range(2):
                    for half in range(2):
                        last = pe.matmul(psum[:, BANKS + 2 * t + half, :], seatsT[:, t * P:t * P + P],
                                         y_pair[:, half * 512:half * 512 + 512], start=False, stop=(p == LAST),
                                         skip_group_check=True)
                        if p == LAST:
                            last.then_inc(scattered, 1)
                if p < LAST:
                    last.then_inc(scattered, 1)

            def pair(p, i=0):
                for j in gathers(p):
                    read_out(pe, j, i)
                gate_up(0, p, i)
                if p > 0:
                    scatter(p - 1, i)
                turn_seats(p, i)
                gate_up(1, p, i)
                if p < LAST:
                    fetch(0, p + 1, i)
                turn(p, i)
                if p < LAST:
                    fetch(1, p + 1, i)
                down(p, i)

            fetch(0, 0)
            fetch(1, 0)
            pair(0)
            pe.wait_ge(cleared, 1)
            with pe.Fori(0, LAST - 1) as i:
                pair(1, i)
            pair(LAST)
            scatter(LAST)

    @stage
    def route0():
        route(0)

    @stage
    def overflow0():
        overflow(0)

    @stage
    def moe0():
        experts(0)

    @stage
    def route1():
        route(1)

    @stage
    def overflow1():
        overflow(1)

    @stage
    def moe1():
        experts(1)

    @stage
    def ffn_norm0():
        layer_norm(1, "ffn0_xT", normed[1])

    kT, qT = carve(0, KC, SEQ), carve(2048, KC, SEQ)
    v_nat = carve(4096, 2, D)
    bias = carve(6144, HEADS, SEQ)
    o_nat = carve(8192, 2, D)
    oT = carve(10240, KC, L)
    probs, mixed, mixedT = carve(12416, 2, 2, SEQ), carve(13440, 2, SEQ), carve(13952, 2, SEQ)
    neg_lam = small[:, 8:9]
    bias_loaded = sem("bias_loaded")
    lam_summed, lam_exp = sem("lam_summed"), sem("lam_exp")
    max_ready, probs_ready, mixed_ready, mixedT_ready, o_ready = (
        sem("max_ready"), sem("probs_ready"), sem("mixed_ready"), sem("mixedT_ready"), sem("o_ready"))
    o_squared, o_normed = sem("o_squared"), sem("o_normed")
    squares_o = carve(10240, P)
    PAIRS = 2 * HEADS

    def block_head(n):
        return n % 2, n // 2

    def kq_products(p):
        m, i = p // 4, p % 4
        unit_ready(unit_at["w_kq"] + i)
        if p >= 4:
            nc.tensor.wait_ge(kq_out, p - 3)
        products(psum[:, BANKS + i, 0:SEQ], [(slot_k(unit_at["w_kq"] + i)[:, k, m * P:m * P + P], xT[:, k, META:L])
                                             for k in range(KC)]).then_inc(kq_done, 1)

    def kq_copy(p):
        m, i = p // 4, p % 4
        nc.scalar.wait_ge(kq_done, p + 1)
        dst, scale = (kT, 1.0) if i < 2 else (qT, HD ** -0.5)
        nc.scalar.activation(dst[:, m + 4 * (i % 2), :], psum[:, BANKS + i, 0:SEQ], ACT.Copy,
                             scale=scale).then_inc(kq_out, 1)

    def att_jobs():
        order = {}
        for n in range(PAIRS + 2):
            for kind, m in (("scores", n), ("turn", n - 1), ("values", n - 2)):
                if 0 <= m < PAIRS:
                    order[kind, m] = FJ["att_heads"] + len(order)
        return order

    AJ = att_jobs()

    @stage
    def attention():
        root = next_sqrt()

        @block.tensor
        def _(pe):
            project_natural(FJ["att_v"], unit_at["w_v"], xT, (1, 2), KC,
                            ready=lambda t: all_read_out(pe, FJ["ffn0_xT"] + 2 * t))
            for p in range(4):
                kq_products(p)
            pe.wait_ge(bias_loaded, 16)
            all_read_out(pe, FJ["att_heads"])

            def scores(n):
                b, h = block_head(n)
                keys = P * (b + 1)
                j = AJ["scores", n]
                take_bank(j)
                pe.wait_ge(kq_out, 4 * (n // 4) + 4)
                rows = slice(HD * (h % 2), HD * (h % 2) + HD)
                for comp in range(2):
                    c = 4 * comp + h // 2
                    pe.matmul(bank(j)[:, comp * SEQ:comp * SEQ + keys], flip, bias[:, h, SEQ - keys:SEQ],
                              start=True, stop=False)
                    last = pe.matmul(bank(j)[:, comp * SEQ:comp * SEQ + keys], qT[rows, c, b * P:b * P + P],
                                     kT[rows, c, 0:keys], start=False, stop=True)
                last.then_inc(job_done, 1)

            def turn(n):
                b, _ = block_head(n)
                j = AJ["turn", n]
                take_bank(j)
                pe.wait_ge(mixed_ready, n + 1)
                for kb in range(b + 1):
                    last = pe.transpose(bank(j)[:, kb * P:kb * P + P], mixed[:, n % 2, kb * P:kb * P + P], ident[:, :])
                last.then_inc(job_done, 1)

            def values(n):
                b, h = block_head(n)
                j = AJ["values", n]
                take_bank(j)
                pe.wait_ge(mixedT_ready, n + 1)
                products(bank(j)[:, 0:P], [(mixedT[:, n % 2, kb * P:kb * P + P], v_nat[:, kb, h * P:h * P + P])
                                           for kb in range(b + 1)]).then_inc(job_done, 1)

            for n in range(PAIRS + 2):
                if n < PAIRS:
                    scores(n)
                if n + 4 < PAIRS:
                    kq_products(n + 4)
                if 1 <= n <= PAIRS:
                    turn(n - 1)
                if n >= 2:
                    values(n - 2)
            transposes_pe(FJ["att_T"], (1, 2), lambda t: o_nat[:, t - 1, :], lambda t: pe.wait_ge(o_normed, t))
            all_read_out(pe, FJ["att_o"])
            project_natural(FJ["att_o"], unit_at["w_o"], oT, (1, 2), KC)

        @block.scalar
        def _(act):
            act.wait_ge(rel_written, 16)
            skewed = bass.AP(rel_scratch.tensor, 0, [[1, P], [3 * P, HEADS], [1, SEQ]])
            act.dma_start(bias, skewed).then_inc(bias_loaded, 16)
            for p in range(4):
                kq_copy(p)
            act.wait_ge(lam_summed, 1)
            act.activation(small[:, 10:12], small[:, 10:12], ACT.Exp).then_inc(lam_exp, 1)

            def exponentials(n):
                keys = P * (block_head(n)[0] + 1)
                j = AJ["scores", n]
                act.wait_ge(max_ready, n + 1)
                if n >= 2:
                    act.wait_ge(mixed_ready, n - 1)
                for comp in range(2):
                    m = 16 + 4 * (n % 2) + comp
                    last = act.activation(probs[:, n % 2, comp, 0:keys], bank(j)[:, comp * SEQ:comp * SEQ + keys],
                                          ACT.Exp, bias=small[:, m:m + 1], accum_out=small[:, m + 2:m + 3])
                last.then_inc(probs_ready, 1)
                act.wait_ge(probs_ready, n + 1)
                act.nop().then_inc(bank_free[j % BANKS], 1)

            def turned(n):
                keys = P * (block_head(n)[0] + 1)
                j = AJ["turn", n]
                job_ready(act, j)
                if n >= 2:
                    job_ready(act, AJ["values", n - 2])
                act.activation(mixedT[:, n % 2, 0:keys], bank(j)[:, 0:keys], ACT.Copy).then_inc(mixedT_ready, 1)
                act.wait_ge(mixedT_ready, n + 1)
                act.nop().then_inc(bank_free[j % BANKS], 1)

            def squares(n):
                b, h = block_head(n)
                job_ready(act, AJ["values", n])
                if n:
                    act.wait_ge(o_squared, n)
                col = 32 + HEADS * b + h
                act.activation(squares_o, bank(AJ["values", n])[:, 0:P], ACT.Square,
                               accum_out=small[:, col:col + 1]).then_inc(o_squared, 1)

            for n in range(PAIRS + 2):
                if n < PAIRS:
                    exponentials(n)
                if n + 4 < PAIRS:
                    kq_copy(n + 4)
                if 1 <= n <= PAIRS:
                    turned(n - 1)
                if n >= 2:
                    squares(n - 2)
            act.preload_act_table(ACT.Sqrt)
            act.wait_ge(o_squared, PAIRS)
            act.activation(small[:, 32:48], small[:, 32:48], ACT.Sqrt, bias=eps_cols[:, 0:1],
                           scale=1.0 / (2 * HD)).then_inc(std_ready, 1)
            transposes_out(FJ["att_T"], (1, 2), oT)

        @block.vector
        def _(dve):
            pairs = lam_rows[:, :, :].rearrange("p (a b) d -> p a b d", b=2)
            dve_step(dve.tensor_tensor(lam_rows[:, 0:2, :], pairs[:, :, 0, :], pairs[:, :, 1, :], ALU.mult))
            dve.tensor_reduce(small[:, 10:12], lam_rows[:, 0:2, :], AX_X, ALU.add).then_inc(lam_summed, 1)
            for half in range(2):
                for t in range(2):
                    j = FJ["att_v"] + 2 * half + t
                    job_ready(dve, j)
                    dve.tensor_copy(v_nat[:, t, half * 512:half * 512 + 512], bank(j)).then_inc(
                        bank_free[j % BANKS], 1)
            dve.wait_ge(lam_exp, 1)
            dve_step(dve.tensor_tensor(neg_lam, small[:, 11:12], small[:, 10:11], ALU.subtract))
            dve_step(dve.tensor_scalar(neg_lam, neg_lam, -LAMBDA_INIT, None, ALU.add))

            def row_max(n):
                keys = P * (block_head(n)[0] + 1)
                j = AJ["scores", n]
                job_ready(dve, j)
                m = 16 + 4 * (n % 2)
                src = bank(j).rearrange("p (c k) -> p c k", c=2)[:, :, 0:keys]
                dve_step(dve.tensor_reduce(small[:, m:m + 2], src, AX_X, ALU.max))
                dve.tensor_scalar(small[:, m:m + 2], small[:, m:m + 2], -1.0, None, ALU.mult).then_inc(max_ready, 1)

            def combine(n):
                keys = P * (block_head(n)[0] + 1)
                m = 16 + 4 * (n % 2) + 2
                dve.wait_ge(probs_ready, n + 1)
                dve_step(dve.reciprocal(small[:, m:m + 2], small[:, m:m + 2]))
                dve_step(dve.tensor_scalar(small[:, m + 1:m + 2], small[:, m + 1:m + 2], neg_lam, None, ALU.mult))
                if n >= 2:
                    job_ready(dve, AJ["turn", n - 2])
                dve_step(dve.tensor_scalar(mixed[:, n % 2, 0:keys], probs[:, n % 2, 0, 0:keys], small[:, m:m + 1],
                                           None, ALU.mult))
                dve.scalar_tensor_tensor(mixed[:, n % 2, 0:keys], probs[:, n % 2, 1, 0:keys],
                                         small[:, m + 1:m + 2], mixed[:, n % 2, 0:keys], ALU.mult,
                                         ALU.add).then_inc(mixed_ready, 1)

            def values_out(n):
                b, h = block_head(n)
                j = AJ["values", n]
                dve.wait_ge(o_squared, n + 1)
                dve.scalar_tensor_tensor(o_nat[:, b, h * P:h * P + P], bank(j)[:, 0:P], 1.0 - LAMBDA_INIT,
                                         subln_rows, ALU.mult, ALU.mult).then_inc(o_ready, 1)
                dve.wait_ge(o_ready, n + 1)
                dve.nop().then_inc(bank_free[j % BANKS], 1)

            for n in range(PAIRS + 2):
                if n < PAIRS:
                    row_max(n)
                if 1 <= n <= PAIRS:
                    combine(n - 1)
                if n >= 2:
                    values_out(n - 2)
            reciprocal_of(dve, small[:, 32:48], root)
            for b in range(2):
                heads_of = o_nat[:, b, :].rearrange("p (h d) -> p h d", d=P)
                rms = small[:, 32 + HEADS * b:32 + HEADS * b + HEADS]
                dve.tensor_tensor(heads_of, heads_of, rms.unsqueeze(2).broadcast_to([P, HEADS, P]),
                                  ALU.mult).then_inc(o_normed, 1)
            add_residual(FJ["att_o"])

    @stage
    def mix_norm1():
        layer_norm(2, "mix1_xT", normed[2])

    @stage
    def ffn_norm1():
        layer_norm(3, "ffn1_xT", normed[3], last=True)

    ALL = (0, 1, 2)

    def rms(name, tiles, src, dst, scaled, gain_rows=None, ready=None):
        summed = sem(f"{name}_summed")
        roots = [next_sqrt() for _ in tiles]

        @block.scalar
        def _(act):
            if name in ("ssd_norm", "ffn_post"):
                act.preload_act_table(ACT.Sqrt)
            for i, t in enumerate(tiles):
                n, total = TILE_N[t], small[0:TILE_N[t], 48 + t:49 + t]
                if ready is not None:
                    ready(t)
                act.activation(dst(t)[0:n], src(t)[0:n], ACT.Square, accum_out=total).then_inc(summed, 1)
                act.wait_ge(summed, i + 1)
                act.activation(total, total, ACT.Sqrt, bias=eps_cols[0:n, 1:2], scale=1.0 / D).then_inc(std_ready, 1)

        @block.vector
        def _(dve):
            if gain_rows is not None:
                dve.wait_ge(norm_loaded[gain_rows % 2], norm_count[gain_rows % 2])
            for i, t in enumerate(tiles):
                n, inverse = TILE_N[t], small[0:TILE_N[t], 48 + t:49 + t]
                reciprocal_of(dve, inverse, roots[i])
                if gain_rows is None:
                    dve.tensor_scalar(dst(t)[0:n], src(t)[0:n], inverse, None, ALU.mult).then_inc(scaled, 1)
                else:
                    dve.scalar_tensor_tensor(dst(t)[0:n], src(t)[0:n], inverse, norm_rows[0:n, gain_rows % 2, 0, :],
                                             ALU.mult, ALU.mult).then_inc(scaled, 1)

    def rms_to_T(name, job_name, src, dst, dstT, gain, pe_first=None, act_between=None, ready=None):
        scaled = sem(f"{name}_scaled")
        rms(name, ALL, src, dst, scaled, ready=ready)
        if pe_first is not None:
            block.tensor(pe_first)
            block.scalar(act_between)
        block.tensor(lambda pe: transposes_pe(FJ[job_name], ALL, dst, lambda t: pe.wait_ge(scaled, t + 1)))

        @block.scalar
        def _(act):
            for t in ALL:
                n, at, j = TILE_N[t], TILE_AT[t], FJ[job_name] + 2 * t
                job_ready(act, j)
                for c in range(4):
                    last = act.activation(dstT[:, c, at:at + n], bank(j)[:, c * P:c * P + n], ACT.Copy,
                                          scale=column(gain, c))
                last.then_inc(bank_free[j % BANKS], 1)

        @block.vector
        def _(dve):
            gains = vec[:, VEC_COL[gain] + 4:VEC_COL[gain] + 8]
            for t in ALL:
                n, at, j = TILE_N[t], TILE_AT[t], FJ[job_name] + 2 * t + 1
                job_ready(dve, j)
                dve.tensor_tensor(dstT[:, 4:8, at:at + n], bank(j).rearrange("p (c t) -> p c t", c=4)[:, :, 0:n],
                                  gains.unsqueeze(2).broadcast_to([P, 4, n]), ALU.mult).then_inc(
                                      bank_free[j % BANKS], 1)

    xn = carve(0, 3, D)

    @stage
    def pre_norm():
        rms_to_T("pre", "pre_xT", lambda t: x_nat[:, t, :], lambda t: xn[:, t, :], xT, "mix_pre_g_2",
                 ready=lambda t: nc.scalar.wait_ge(normed[3], t) if t else None)

    zs = carve(0, 3, D)
    zT = carve(9700, KC, L)
    xbcT = carve(3072, XC, L)
    XPAD = SSD_TAPS - 1
    xraw = carve(6336, XC, XPAD + L)
    in_ready, xconv_step, dt_pos, dt_exp, dt_one, dt_ln, a_exp = (
        sem("xbc_in"), sem("xconv_step"), sem("dt_neg_abs"), sem("dt_exp"), sem("dt_one"), sem("dt_ln"), sem("a_exp"))
    xpad_ready = sem("xpad_ready")
    dt_v, dt_m, dt_e, dt_w, dt_l, dt_r, dt, adt = (dts[:, n, :] for n in range(8))
    dt_d = dts[:, 8, :]

    def by_tile(x):
        return x.rearrange("p (t h) -> p t h", t=3)

    sqT, skT = (ring[:, s, 0:KC * L].rearrange("p (c t) -> p c t", c=KC) for s in (q_slot, k_slot))

    def qk_products(n):
        u = unit_at["w_sb_q"] + n // 4
        unit_ready(u)
        if n >= 4:
            nc.tensor.wait_ge(qk_out, n - 3)
        products(psum[:, BANKS + n % 4, 0:L], [(slot_k(u)[:, k, (n % 4) * P:(n % 4) * P + P], xT[:, k, :])
                                               for k in range(KC)]).then_inc(qk_done, 1)

    def qk_copy(n):
        nc.scalar.wait_ge(qk_done, n + 1)
        dst, scale = (sqT, 0.125) if n < KC else (skT, 1.0)
        nc.scalar.activation(dst[:, n % KC, :], psum[:, BANKS + n % 4, 0:L], ACT.Copy, scale=scale).then_inc(qk_out, 1)

    QK_AT = {"inner": 3, ("rows", 0): 1, ("diag", 0): 1, ("rows", 1): 2, ("diag", 1): 2, ("rows", 2): 2,
             ("diag", 2): 2, "norm": 3}
    assert sum(QK_AT.values()) == 2 * KC
    qk_pe, qk_act = iter(range(2 * KC)), iter(range(2 * KC))

    @stage
    def inner():
        @block.tensor
        def _(pe):
            project_turned(FJ["z"], [(unit_at["w_z"], unit_at["w_z"] + 1, xT, None)], zT)
            for c in range(XC):
                j, u = FJ["xbc"] + c, unit_at["w_xbc"] + c // 4
                unit_ready(u)
                take_bank(j)
                products(bank(j)[:, 0:L], [(slot_k(u)[:, k, (c % 4) * P:(c % 4) * P + P], xT[:, k, :])
                                           for k in range(KC)]).then_inc(job_done, 1)
            j = FJ["dt"]
            take_bank(j)
            for t in ALL:
                n, at = TILE_N[t], TILE_AT[t]
                last = products(bank(j)[0:n, t * SSD_HEADS:(t + 1) * SSD_HEADS],
                                [(xT[:, k, at:at + n], w_dt[:, k, :]) for k in range(KC)])
            last.then_inc(job_done, 1)
            for _ in range(QK_AT["inner"]):
                qk_products(next(qk_pe))

        @block.scalar
        def _(act):
            turned_in(FJ["z"], zT, ACT.Silu)
            j = FJ["z"] + KC
            for half in range(2):
                for t in ALL:
                    n = TILE_N[t]
                    job_ready(act, j)
                    act.activation(zs[0:n, t, half * 512:half * 512 + 512], bank(j)[0:n, :], ACT.Copy).then_inc(
                        bank_free[j % BANKS], 1)
                    j += 1
            act.wait_ge(xpad_ready, 1)
            for c in range(XC):
                j = FJ["xbc"] + c
                job_ready(act, j)
                act.activation(xraw[:, c, XPAD:XPAD + L], bank(j)[:, 0:L], ACT.Copy).then_inc(in_ready, 1)
                act.wait_ge(in_ready, c + 1)
                act.nop().then_inc(bank_free[j % BANKS], 1)
            for c in range(XC):
                act.wait_ge(xconv_step, (SSD_TAPS - 1) * 4 + c % 4 + 1 + (c // 4) * 4 * SSD_TAPS)
                act.activation(xbcT[:, c, :], xbcT[:, c, :], ACT.Silu, bias=column("ssd_conv_b_2", c))
            act.wait_ge(dt_pos, 1)
            act.activation(dt_e, dt_e, ACT.Exp).then_inc(dt_exp, 1)
            act.activation(ssd_rows[:, 1, :], ssd_rows[:, 1, :], ACT.Exp).then_inc(a_exp, 1)
            act.wait_ge(dt_one, 1)
            act.activation(dt_l, dt_w, ACT.Ln).then_inc(dt_ln, 1)
            for _ in range(QK_AT["inner"]):
                qk_copy(next(qk_act))

        @block.vector
        def _(dve):
            dve.memset(xraw[:, :, 0:XPAD], 0.0).then_inc(xpad_ready, 1)
            dve_step(dve.memset(dts[:, :, :], 0.0))
            n = 0
            for quad in range(XC // 4):
                for tap in range(SSD_TAPS):
                    for c in range(4 * quad, 4 * quad + 4):
                        src = xraw[:, c, tap:tap + L]
                        w = column("ssd_conv_w_2", tap * XC + c)
                        if tap == 0:
                            dve.wait_ge(in_ready, c + 1)
                            ins = dve.tensor_scalar(xbcT[:, c, :], src, w, None, ALU.mult)
                        else:
                            dve.wait_ge(xconv_step, n - 3)
                            ins = dve.scalar_tensor_tensor(xbcT[:, c, :], src, w, xbcT[:, c, :], ALU.mult, ALU.add)
                        ins.then_inc(xconv_step, 1)
                        n += 1
            j = FJ["dt"]
            job_ready(dve, j)
            dve.tensor_copy(by_tile(dt_v)[0:META, 0, :], bank(j)[0:META, 0:SSD_HEADS])
            dve_step(dve.tensor_copy(dt_v[:, SSD_HEADS:], bank(j)[:, SSD_HEADS:3 * SSD_HEADS]))
            dve.nop().then_inc(bank_free[j % BANKS], 1)
            dve_step(dve.tensor_tensor(by_tile(dt_v), by_tile(dt_v),
                                       ssd_rows[:, 0, :].unsqueeze(1).broadcast_to([P, 3, SSD_HEADS]), ALU.add))
            dve_step(dve.tensor_scalar(dt_m, dt_v, 0.0, None, ALU.max))
            dve.scalar_tensor_tensor(dt_e, dt_m, -2.0, dt_v, ALU.mult, ALU.add).then_inc(dt_pos, 1)
            dve.wait_ge(dt_exp, 1)
            dve.tensor_scalar(dt_w, dt_e, 1.0, None, ALU.add).then_inc(dt_one, 1)
            dve.wait_ge(dt_one, 1)
            dve_step(dve.tensor_scalar(dt_d, dt_w, -1.0, 1e-30, ALU.add, ALU.max))
            dve_step(dve.reciprocal(dt_d, dt_d))
            dve.wait_ge(dt_ln, 1)
            dve_step(dve.tensor_tensor(dt_r, dt_l, dt_d, ALU.mult))
            dve_step(dve.tensor_scalar(dt_w, dt_w, 1.0, None, ALU.is_equal))
            dve_step(dve.tensor_tensor(dt_r, dt_r, dt_w, ALU.add))
            dve_step(dve.tensor_tensor(dt_r, dt_r, dt_e, ALU.mult))
            dve_step(dve.tensor_tensor(dt, dt_m, dt_r, ALU.add))
            dve.wait_ge(a_exp, 1)
            dve_step(dve.tensor_scalar(dt_v, dt, -1.0, None, ALU.mult))
            dve_step(dve.tensor_tensor(by_tile(adt), by_tile(dt_v),
                                       ssd_rows[:, 1, :].unsqueeze(1).broadcast_to([P, 3, SSD_HEADS]), ALU.mult))

    xs, xdt, xd = carve(6336, D), carve(6336 + D, D), carve(6336 + 2 * D, D)
    decay = carve(9636, SSD_HEADS, P)
    steps = carve(11684, 2, 4, P)
    cb = carve(12708, SSD_GROUPS, P)
    b_nat = carve(12964, SSD_GROUPS, STATE)
    state = carve(13220, D)
    y_tmp = carve(14244, D)
    yT = carve(14440, KC, L)
    cums = carve(9408, 4, SSD_HEADS)
    PD = SSD_HEADS // SSD_GROUPS
    HG = D // SSD_GROUPS

    def ssd_jobs():
        order = {}
        for c in ALL:
            kinds = ["sums", "cb", "xs0", "xs1", "b", "row0", "row1", "row2", "row3", "diag0", "diag1"]
            kinds += ["off0", "off1"] if c > 0 else []
            kinds += ["state0", "state1"] if c < 2 else []
            for kind in kinds:
                order[kind, c] = FJ["ssd"] + len(order)
        return order

    SJ = ssd_jobs()
    cums_ready, cums_exp, cb_out, cb_masked, xs_ready, b_ready, step_ready, seg_ready, seg_exp, decay_ready = (
        sem("cums_ready"), sem("cums_exp"), sem("cb_out"), sem("cb_masked"), sem("xs_ready"), sem("b_ready"),
        sem("step_ready"), sem("seg_ready"), sem("seg_exp"), sem("decay_ready"))
    xdt_ready, xd_ready, state_ready, y_done = sem("xdt_ready"), sem("xd_ready"), sem("state_ready"), sem("y_done")

    def per_head(x, n, nh=SSD_HEADS, width=64):
        return x.unsqueeze(2).broadcast_to([n, nh, width])

    def heads_of_row(x, n):
        return x[0:n].rearrange("p (h d) -> p h d", d=64)

    @stage
    def ssd():
        @block.tensor
        def _(pe):
            for c in ALL:
                n, at = TILE_N[c], TILE_AT[c]
                a_c = by_tile(adt)[0:n, c, :]
                j = SJ["sums", c]
                take_bank(j)
                products(bank(j)[:, 0:SSD_HEADS], [(ones[0:n, :], a_c)])
                products(bank(j)[0:n, SSD_HEADS:2 * SSD_HEADS], [(upto[0:n, 0:n], a_c)]).then_inc(job_done, 1)
                j = SJ["cb", c]
                take_bank(j)
                for g in range(SSD_GROUPS):
                    last = products(bank(j)[0:n, g * P:g * P + n],
                                    [(xbcT[:, KC + g, at:at + n], xbcT[:, KC + SSD_GROUPS + g, at:at + n])])
                last.then_inc(job_done, 1)
                for half in range(2):
                    j = SJ[f"xs{half}", c]
                    take_bank(j)
                    for k in range(4):
                        last = pe.transpose(bank(j)[0:n, k * P:k * P + P], xbcT[:, 4 * half + k, at:at + n],
                                            ident[:, :])
                    last.then_inc(job_done, 1)
                j = SJ["b", c]
                take_bank(j)
                for g in range(SSD_GROUPS):
                    last = pe.transpose(bank(j)[0:n, g * P:g * P + P], xbcT[:, KC + g, at:at + n], ident[:, :])
                last.then_inc(job_done, 1)
                for q in range(4):
                    j = SJ[f"row{q}", c]
                    take_bank(j)
                    pe.wait_ge(step_ready, 4 * c + q + 1)
                    products(bank(j)[:, 0:4 * n].rearrange("p (h l) -> p h l", h=4),
                             [(ones[0:n, :], steps[0:n, q % 2, :, 0:n])]).then_inc(job_done, 1)
                for _ in range(QK_AT["rows", c]):
                    qk_products(next(qk_pe))
                pe.wait_ge(decay_ready, 4 * c + 4)
                pe.wait_ge(xdt_ready, c + 1)
                for g in range(SSD_GROUPS):
                    j = SJ[f"diag{g}", c]
                    take_bank(j)
                    for h in range(PD):
                        last = products(bank(j)[0:n, h * 64:h * 64 + 64],
                                        [(decay[0:n, PD * g + h, 0:n],
                                          xdt[0:n, g * HG + h * 64:g * HG + h * 64 + 64])])
                    last.then_inc(job_done, 1)
                for _ in range(QK_AT["diag", c]):
                    qk_products(next(qk_pe))
                if c > 0:
                    pe.wait_ge(state_ready, c)
                    for g in range(SSD_GROUPS):
                        j = SJ[f"off{g}", c]
                        take_bank(j)
                        products(bank(j)[0:n, :], [(xbcT[:, KC + SSD_GROUPS + g, at:at + n],
                                                    state[:, g * HG:g * HG + HG])]).then_inc(job_done, 1)
                if c < 2:
                    pe.wait_ge(xd_ready, c + 1)
                    pe.wait_ge(b_ready, c + 1)
                    for g in range(SSD_GROUPS):
                        j = SJ[f"state{g}", c]
                        take_bank(j)
                        products(bank(j), [(b_nat[0:n, g, :], xd[0:n, g * HG:g * HG + HG])]).then_inc(job_done, 1)

        @block.scalar
        def _(act):
            for c in ALL:
                n = TILE_N[c]
                if c:
                    act.wait_ge(y_done, c)
                j = SJ["cb", c]
                job_ready(act, j)
                act.activation(cb[0:n, :, 0:n], bank(j)[0:n, 0:2 * P].rearrange("p (g l) -> p g l", g=2)[:, :, 0:n],
                               ACT.Copy).then_inc(cb_out, 1)
                act.wait_ge(cb_out, c + 1)
                act.nop().then_inc(bank_free[j % BANKS], 1)
                for half in range(2):
                    j = SJ[f"xs{half}", c]
                    job_ready(act, j)
                    act.activation(xs[0:n, half * 512:half * 512 + 512], bank(j)[0:n, :], ACT.Copy).then_inc(
                        bank_free[j % BANKS], 1)
                act.nop().then_inc(xs_ready, 1)
                j = SJ["b", c]
                job_ready(act, j)
                act.activation(b_nat[0:n, :, :], bank(j)[0:n, 0:2 * P].rearrange("p (g l) -> p g l", g=2),
                               ACT.Copy).then_inc(b_ready, 1)
                act.wait_ge(b_ready, c + 1)
                act.nop().then_inc(bank_free[j % BANKS], 1)
                act.wait_ge(cums_ready, c + 1)
                act.activation(cums[:, 0:3, :], cums[:, 0:3, :], ACT.Exp).then_inc(cums_exp, 1)
                for q in range(4):
                    act.wait_ge(seg_ready, 4 * c + q + 1)
                    m = decay[0:n, 4 * q:4 * q + 4, 0:n]
                    act.activation(m, m, ACT.Exp).then_inc(seg_exp, 1)
                for _ in range(QK_AT["rows", c] + QK_AT["diag", c]):
                    qk_copy(next(qk_act))

        @block.gpsimd
        def _(pool):
            for c in ALL:
                n = TILE_N[c]
                pool.wait_ge(cb_out, c + 1)
                pool.affine_select(out=cb[0:n, :, 0:n], in_=cb[0:n, :, 0:n], compare_op=ALU.is_ge, fill=0.0, base=0,
                                   pattern=[[0, 2], [1, n]], channel_multiplier=-1).then_inc(cb_masked, 1)

        @block.vector
        def _(dve):
            dve_step(dve.memset(cums, 0.0))
            for c in ALL:
                n = TILE_N[c]
                for q in range(4):
                    k = 4 * c + q
                    if k >= 2:
                        job_ready(dve, SJ[f"row{(k - 2) % 4}", (k - 2) // 4])
                    dve.tensor_tensor(steps[0:n, q % 2, :, 0:n],
                                      by_tile(adt)[0:n, c, 4 * q:4 * q + 4].unsqueeze(2).broadcast_to([n, 4, n]),
                                      upto[0:n, 0:n].unsqueeze(1).broadcast_to([n, 4, n]), ALU.mult).then_inc(
                                          step_ready, 1)
                    if q == 1:
                        j = SJ["sums", c]
                        job_ready(dve, j)
                        dve.tensor_copy(cums[:, 2, :], bank(j)[:, 0:SSD_HEADS])
                        dve.tensor_copy(cums[0:n, 3, :], bank(j)[0:n, SSD_HEADS:2 * SSD_HEADS])
                        dve_step(dve.tensor_copy(cums[0:n, 0, :], bank(j)[0:n, SSD_HEADS:2 * SSD_HEADS]))
                        dve.nop().then_inc(bank_free[j % BANKS], 1)
                        dve.tensor_tensor(cums[0:n, 1, :], cums[0:n, 2, :], cums[0:n, 3, :],
                                          ALU.subtract).then_inc(cums_ready, 1)
                    if q >= 1:
                        segment(dve, c, q - 1)
                segment(dve, c, 3)
                dve.wait_ge(xs_ready, c + 1)
                dve.wait_ge(bank_free[SJ["xs1", c] % BANKS], SJ["xs1", c] // BANKS + 1)
                dve.tensor_tensor(heads_of_row(xdt, n), heads_of_row(xs, n),
                                  per_head(by_tile(dt)[0:n, c, :], n), ALU.mult).then_inc(xdt_ready, 1)
                for q in range(4):
                    dve.wait_ge(seg_exp, 4 * c + q + 1)
                    dve.wait_ge(cb_masked, c + 1)
                    m = decay[0:n, 4 * q:4 * q + 4, 0:n]
                    dve.tensor_tensor(m, m, cb[0:n, q // 2, 0:n].unsqueeze(1).broadcast_to([n, 4, n]),
                                      ALU.mult).then_inc(decay_ready, 1)
                dve.wait_ge(cums_exp, c + 1)
                dve.wait_ge(xdt_ready, c + 1)
                dve.tensor_tensor(heads_of_row(xd, n), heads_of_row(xdt, n), per_head(cums[0:n, 1, :], n),
                                  ALU.mult).then_inc(xd_ready, 1)
                y = y_tmp[0:n]
                dve_step(dve.tensor_tensor(heads_of_row(xs, n), heads_of_row(xs, n),
                                           per_head(ssd_rows[0:n, 2, :], n), ALU.mult))
                for g in range(SSD_GROUPS):
                    j = SJ[f"diag{g}", c]
                    job_ready(dve, j)
                    cols = slice(g * HG, g * HG + HG)
                    dve_step(dve.tensor_tensor(y[:, cols], xs[0:n, cols], bank(j)[0:n, :], ALU.add))
                    dve.nop().then_inc(bank_free[j % BANKS], 1)
                if c > 0:
                    for g in range(SSD_GROUPS):
                        j = SJ[f"off{g}", c]
                        job_ready(dve, j)
                        cols = slice(g * HG, g * HG + HG)
                        part = xs[0:n, cols].rearrange("p (h d) -> p h d", d=64)
                        dve_step(dve.tensor_tensor(part, bank(j)[0:n, :].rearrange("p (h d) -> p h d", d=64),
                                                   per_head(cums[0:n, 0, PD * g:PD * g + PD], n, nh=PD), ALU.mult))
                        dve.nop().then_inc(bank_free[j % BANKS], 1)
                        dve_step(dve.tensor_tensor(y[:, cols], y[:, cols], xs[0:n, cols], ALU.add))
                dve_step(dve.tensor_tensor(zs[0:n, c, :], zs[0:n, c, :], y, ALU.mult))
                if c < 2:
                    for g in range(SSD_GROUPS):
                        j = SJ[f"state{g}", c]
                        job_ready(dve, j)
                        cols = slice(g * HG, g * HG + HG)
                        if c == 0:
                            dve_step(dve.tensor_copy(state[:, cols], bank(j)))
                        else:
                            part = state[:, cols].rearrange("p (h d) -> p h d", d=64)
                            dve_step(dve.tensor_tensor(part, part,
                                                       per_head(cums[:, 2, PD * g:PD * g + PD], P, nh=PD), ALU.mult))
                            dve_step(dve.tensor_tensor(state[:, cols], state[:, cols], bank(j), ALU.add))
                        dve.nop().then_inc(bank_free[j % BANKS], 1)
                    dve.nop().then_inc(state_ready, 1)
                dve.nop().then_inc(y_done, 1)

    def segment(dve, c, q):
        n = TILE_N[c]
        j = SJ[f"row{q}", c]
        job_ready(dve, j)
        if q == 0:
            dve.wait_ge(cums_ready, c + 1)
        m = decay[0:n, 4 * q:4 * q + 4, 0:n]
        dve_step(dve.tensor_tensor(m, bank(j)[0:n, 0:4 * n].rearrange("p (h l) -> p h l", h=4),
                                   cums[0:n, 3, 4 * q:4 * q + 4].unsqueeze(2).broadcast_to([n, 4, n]), ALU.subtract))
        dve.nop().then_inc(bank_free[j % BANKS], 1)
        dve.tensor_scalar(m, m, 0.0, None, ALU.min).then_inc(seg_ready, 1)

    @stage
    def ssd_norm():
        rms_to_T("ssd_norm", "y_T", lambda t: zs[:, t, :], lambda t: xn2[:, t, :], yT, "ssd_norm_g_2",
                 lambda pe: [qk_products(next(qk_pe)) for _ in range(QK_AT["norm"])],
                 lambda act: [qk_copy(next(qk_act)) for _ in range(QK_AT["norm"])])

    xn2 = carve(3072, 3, D)

    sv = carve(4352, 3, D)
    soT = carve(7424, KC, L)
    svT = carve(7424, KC, L)
    W1 = 384
    SB_BUFS, SB_BANKS = 3, 4
    soft, wts = carve(10496, SB_BUFS, W1 + L), carve(10496 + SB_BUFS * (W1 + L), SB_BUFS, W1 + L)
    pos = xT[:, :, :].rearrange("p c t -> p (c t)")[:, 0:SB_BUFS * (W1 + L)].rearrange("p (b n) -> p b n", b=SB_BUFS)
    z_ready, neg_abs, soft_exp, soft_ln, soft_sum, soft_ready, expo_ready, w_exp, w_ready, so_ready, soft_cleared, v_ready, so_squared = (
        sem(f"sb_{x}") for x in ("z_ready", "neg_abs", "exp", "ln", "sum", "soft_ready", "expo", "w_exp",
                                 "w_ready", "o_ready", "soft_cleared", "values_ready", "squared"))

    def sb_bank(h):
        return psum[:, 2 * (h % SB_BANKS), 0:W1], psum[0:META, 2 * (h % SB_BANKS) + 1, 0:L]

    def sb_values(h):
        return psum[:, 2 * (h % SB_BANKS), 0:L]

    def sb_parts(x, h):
        return x[:, h % SB_BUFS, 0:W1], x[0:META, h % SB_BUFS, W1:W1 + L]

    @stage
    def stick_breaking():
        @block.tensor
        def _(pe):
            project_turned(FJ["sb_v"], [(unit_at["w_sb_v"], unit_at["w_sb_v"] + 1, xT, None)], svT)
            all_read_out(pe, FJ["w_out"])

            def logits(h):
                rows = slice(64 * (h % 2), 64 * (h % 2) + 64)
                c = h // 2
                main, meta = sb_bank(h)
                if h >= SB_BANKS:
                    pe.wait_ge(so_ready, h - SB_BANKS + 1)
                pe.matmul(main[:, 0:SEQ], skT[rows, c, META:META + P], sqT[rows, c, META:L], start=True, stop=True)
                pe.matmul(main[:, SEQ:W1], skT[rows, c, META + P:L], sqT[rows, c, META + P:L], start=False, stop=True,
                          skip_group_check=True)
                pe.matmul(meta, skT[rows, c, 0:META], sqT[rows, c, :], start=True, stop=True).then_inc(z_ready, 1)

            def exponents(h):
                main, meta = sb_bank(h)
                s1, s0 = sb_parts(soft, h)
                pe.wait_ge(soft_ready, h + 1)
                terms = [(main[:, SEQ:W1], neg_from[:, :], s1[:, SEQ:W1]),
                         (main[:, 0:SEQ], neg_from[:, :], s1[:, 0:SEQ]),
                         (main[:, P:SEQ], neg_ones[:, :], s1[:, SEQ:W1]),
                         (meta, neg_from[0:META, 0:META], s0),
                         (meta[:, META:L], neg_ones[:, 0:META], s1[:, 0:SEQ]),
                         (meta[:, META + P:L], neg_ones[:, 0:META], s1[:, SEQ:W1])]
                for dst, lhsT, rhs in terms:
                    last = pe.matmul(dst, lhsT, rhs, start=False, stop=True, skip_group_check=True)
                last.then_inc(expo_ready, 1)

            def values(h):
                dst = sb_values(h)
                w1, w0 = sb_parts(wts, h)
                cols = slice(P * (h // 2), P * (h // 2) + P)
                pe.wait_ge(w_ready, h + 1)
                pe.matmul(dst, sv[0:META, 0, cols], w0, start=True, stop=True)
                pe.matmul(dst[:, META:L], sv[:, 1, cols], w1[:, 0:SEQ], start=False, stop=True, skip_group_check=True)
                pe.matmul(dst[:, META + P:L], sv[:, 2, cols], w1[:, SEQ:W1], start=False, stop=True,
                          skip_group_check=True).then_inc(v_ready, 1)

            for n in range(SB_HEADS + 3):
                if 2 <= n < SB_HEADS + 2:
                    exponents(n - 2)
                if n < SB_HEADS:
                    logits(n)
                if n >= 3:
                    values(n - 3)

        @block.scalar
        def _(act):
            turned_in(FJ["sb_v"], svT)

            def softplus(h):
                both = soft[:, h % SB_BUFS, :]
                act.wait_ge(neg_abs, h + 1)
                act.activation(both, both, ACT.Exp).then_inc(soft_exp, 1)
                act.wait_ge(soft_exp, h + 1)
                act.activation(both, both, ACT.Ln, bias=1.0).then_inc(soft_ln, 1)

            def squares_of(c):
                act.wait_ge(so_ready, 2 * c + 2)
                act.activation(sqT[:, c, :], soT[:, c, :], ACT.Square).then_inc(so_squared, 1)

            def weights(h):
                act.wait_ge(expo_ready, h + 1)
                if h >= SB_BUFS:
                    act.wait_ge(v_ready, h - SB_BUFS + 1)
                for dst, src in zip(sb_parts(wts, h), sb_bank(h)):
                    act.activation(dst, src, ACT.Exp).then_inc(w_exp, 1)

            act.preload_act_table_set("natural_log_exp_and_others")
            for n in range(SB_HEADS + 2):
                if n >= 2:
                    weights(n - 2)
                if n < SB_HEADS:
                    softplus(n)
                if n >= 7 and n % 2:
                    squares_of(n // 2 - 3)
            squares_of(KC - 2)
            squares_of(KC - 1)

        @block.gpsimd
        def _(pool):
            def masked(x, h):
                main, meta = sb_parts(x, h)
                for part in (main[:, 0:P], main[:, SEQ:W1], meta[:, 0:META]):
                    n = part.shape[1]
                    ins = pool.affine_select(out=part, in_=part, compare_op=ALU.is_gt, fill=0.0, base=0,
                                             pattern=[[1, n]], channel_multiplier=-1)
                return ins

            pool.memset(soft, 0.0).then_inc(soft_cleared, 1)
            for n in range(SB_HEADS + 2):
                if n >= 2:
                    pool.wait_ge(w_exp, 2 * (n - 1))
                    masked(wts, n - 2).then_inc(w_ready, 1)
                if n < SB_HEADS:
                    pool.wait_ge(soft_ln, n + 1)
                    pool.wait_ge(neg_abs, n + 1)
                    for dst, more in zip(sb_parts(soft, n), sb_parts(pos, n)):
                        pool_step(pool.tensor_tensor(dst, dst, more, ALU.add))
                    masked(soft, n).then_inc(soft_ready, 1)

        @block.vector
        def _(dve):
            j = FJ["sb_v"] + KC
            for half in range(2):
                for t in ALL:
                    n = TILE_N[t]
                    job_ready(dve, j)
                    dve.tensor_copy(sv[0:n, t, half * 512:half * 512 + 512], bank(j)[0:n, :]).then_inc(
                        bank_free[j % BANKS], 1)
                    j += 1
            dve.wait_ge(soft_cleared, 1)
            for n in range(SB_HEADS + 4):
                if n >= 4:
                    h = n - 4
                    dve.wait_ge(v_ready, h + 1)
                    rows = slice(64 * (h % 2), 64 * (h % 2) + 64)
                    dve.tensor_copy(soT[rows, h // 2, :], sb_values(h)[rows]).then_inc(so_ready, 1)
                if n < SB_HEADS:
                    dve.wait_ge(z_ready, n + 1)
                    if n >= SB_BUFS:
                        dve.wait_ge(expo_ready, n - SB_BUFS + 1)
                    for m, z in zip(sb_parts(pos, n), sb_bank(n)):
                        dve_step(dve.tensor_scalar(m, z, 0.0, None, ALU.max))
                    for s, m, z in zip(sb_parts(soft, n), sb_parts(pos, n), sb_bank(n)):
                        ins = dve.scalar_tensor_tensor(s, m, -2.0, z, ALU.mult, ALU.add)
                    ins.then_inc(neg_abs, 1)

    mix = carve(4352, 3, D)
    mix_n = carve(7424, 3, D)
    mixT = carve(10496, KC, L)
    sbT = carve(2176, KC, L)
    rms_b = carve(9650, L)
    so_summed, sb_normed = sem("so_summed"), sem("sb_normed")

    mix_added, ffn_added = sem("mix_added"), sem("ffn_added")

    def post_norm(k, name, tiles, src, dst, added, ready=None):
        scaled = sem(f"{name}_scaled")
        rms(name, tiles, src, dst, scaled, gain_rows=k, ready=ready)

        @block.vector
        def _(dve):
            for i, t in enumerate(tiles):
                n = TILE_N[t]
                dve.wait_ge(scaled, i + 1)
                dve.tensor_tensor(x_nat[0:n, t, :], x_nat[0:n, t, :], dst(t)[0:n], ALU.add).then_inc(added, 1)

    @stage
    def project_out():
        root = next_sqrt()

        @block.tensor
        def _(pe):
            products(psum[:, BANKS, 0:L], [(ones[:, :], sqT[:, c, :]) for c in range(KC)]).then_inc(so_summed, 1)
            w = unit_at["w_out"]
            project_turned(FJ["w_out"], [(w, w + 2, yT, None), (w + 1, w + 3, sbT, lambda: pe.wait_ge(sb_normed, 1))],
                           mixT)

        @block.scalar
        def _(act):
            act.preload_act_table(ACT.Sqrt)
            act.wait_ge(so_summed, 1)
            act.activation(rms_b, psum[:, BANKS, 0:L], ACT.Sqrt, bias=eps_cols[:, 1:2], scale=1.0 / D).then_inc(
                std_ready, 1)
            turned_in(FJ["w_out"], mixT)

        @block.vector
        def _(dve):
            reciprocal_of(dve, rms_b, root)
            for c in range(KC):
                ins = dve.scalar_tensor_tensor(sbT[:, c, :], soT[:, c, :], column("sb_norm_g_2", c), rms_b,
                                               ALU.mult, ALU.mult)
            ins.then_inc(sb_normed, 1)

        @block.vector
        def _(dve):
            j = FJ["w_out"] + KC
            for half in range(2):
                for t in ALL:
                    n = TILE_N[t]
                    job_ready(dve, j)
                    dve.tensor_copy(mix[0:n, t, half * 512:half * 512 + 512], bank(j)[0:n, :]).then_inc(
                        bank_free[j % BANKS], 1)
                    j += 1

    @stage
    def mix_post():
        post_norm(4, "mix_post", ALL, lambda t: mix[:, t, :], lambda t: mix_n[:, t, :], mix_added)

    @stage
    def ffn_pre():
        rms_to_T("ffn_pre", "ffn_T", lambda t: x_nat[:, t, :], lambda t: xn[:, t, :], xT, "ffn_pre_g_2",
                 ready=lambda t: nc.scalar.wait_ge(mix_added, t + 1))

    fT = carve(3072, FC, SEQ)
    gate = carve(8800, 4, SEQ)
    act_g = carve(9900, 2, SEQ)
    G0 = META - (FFN_TAPS - 1)
    GW = SEQ + FFN_TAPS - 1
    gconv_step, gelu_ready, f_ready = sem("gconv_step"), sem("gelu_ready"), sem("f_ready")

    def f_out(t):
        return psum[:, BANKS + 2 * t - 2:BANKS + 2 * t, :].rearrange("p b n -> p (b n)")

    f_n = carve(12600, 2, D)

    @stage
    def ffn():
        @block.tensor
        def _(pe):
            for c in range(FC):
                u = unit_at["w_up"] + c // 2
                unit_ready(u)
                for side, (at, width) in enumerate(((G0, GW), (META, SEQ))):
                    j = FJ["up"] + 2 * c + side
                    take_bank(j)
                    cols = side * 256 + (c % 2) * P
                    products(bank(j)[:, 0:width], [(slot_k(u)[:, k, cols:cols + P], xT[:, k, at:at + width])
                                                   for k in range(KC)]).then_inc(job_done, 1)
            for c in range(FC):
                u = unit_at["w_down"] + c // 4
                if c % 4 == 0:
                    unit_ready(u)
                pe.wait_ge(f_ready, c + 1)
                for t in range(2):
                    for half in range(2):
                        last = pe.matmul(psum[:, BANKS + 2 * t + half, :], fT[:, c, t * P:t * P + P],
                                         slot_k(u, D)[:, c % 4, half * 512:half * 512 + 512], start=(c == 0),
                                         stop=(c == FC - 1))
                if c % 4 == 3 or c == FC - 1:
                    last.then_inc(down_ready, 1)

        @block.scalar
        def _(act):
            for c in range(FC):
                act.wait_ge(gconv_step, 3 * c + 3)
                if c >= 2:
                    act.wait_ge(f_ready, c - 1)
                act.activation(act_g[:, c % 2, :], gate[:, c % 4, :], ACT.Gelu_apprx_tanh).then_inc(gelu_ready, 1)

        @block.vector
        def _(dve):
            for c in range(FC):
                j = FJ["up"] + 2 * c
                job_ready(dve, j)
                if c >= 4:
                    dve.wait_ge(gelu_ready, c - 3)
                for tap in range(FFN_TAPS):
                    src = bank(j)[:, tap:tap + SEQ]
                    w = column("ffn_conv_w_2", tap * FC + c)
                    g = gate[:, c % 4, :]
                    if tap == 0:
                        ins = dve.tensor_scalar(g, src, w, column("ffn_conv_b_2", c), ALU.mult, ALU.add)
                    else:
                        dve.wait_ge(gconv_step, 3 * c + tap)
                        ins = dve.scalar_tensor_tensor(g, src, w, g, ALU.mult, ALU.add)
                    ins.then_inc(gconv_step, 1)
                dve.wait_ge(gconv_step, 3 * c + 3)
                dve.nop().then_inc(bank_free[j % BANKS], 1)
                dve.wait_ge(gelu_ready, c + 1)
                job_ready(dve, j + 1)
                dve.tensor_tensor(fT[:, c, :], act_g[:, c % 2, :], bank(j + 1)[:, 0:SEQ], ALU.mult).then_inc(f_ready, 1)
                dve.wait_ge(f_ready, c + 1)
                dve.nop().then_inc(bank_free[(j + 1) % BANKS], 1)

    @stage
    def ffn_post():
        post_norm(5, "ffn_post", (1, 2), f_out, lambda t: f_n[:, t - 1, :], ffn_added,
                  ready=lambda t: nc.scalar.wait_ge(down_ready, DOWN_UNITS))

    next_norm = {
        "constants": (1, a["ln_ffn_g"][0], a["ln_ffn_b"][0]), "route0": (2, a["ln_mix_g"][1], a["ln_mix_b"][1]),
        "attention": (3, a["ln_ffn_g"][1], a["ln_ffn_b"][1]), "route1": (4, a["mix_post_g_2"][0]),
        "pre_norm": (5, a["ffn_post_g_2"][0]),
    }
    table = {f.__name__: f for f in stages}
    for name in ORDER:
        table[name]()
        if name not in RUN_ON:
            next_stage()
        if name in next_norm:
            block.scalar(lambda act, args=next_norm[name]: load_norm(*args))

    @block.sync
    def _(sp):
        for t in (1, 2):
            sp.wait_ge(ffn_added, t)
            sp.dma_start(out[0][(t - 1) * P:t * P, :], x_nat[:, t, :]).then_inc(output_written, 16)
        sp.wait_ge(output_written, 32)
        sp.wait_ge(stage_left, len(compute) * left[0])
        for k in range(2):
            if norm_count[k]:
                sp.wait_ge(norm_loaded[k], norm_count[k])

    ctx.close()


_INS = ["x", "a_w_pw1", "a_b_pw1", "a_w_dw", "a_b_dw", "a_ln_g", "a_ln_b", "a_w_pw2", "a_b_pw2", "w_kv", "b_w_q",
        "b_lambda", "b_subln_g", "b_w_o", "rel_bias", "ln_mix_g", "ln_mix_b", "ln_ffn_g", "ln_ffn_b", "router_w",
        "router_bias", "moe_w_gate", "moe_w_up", "moe_w_down", "meta_tokens_2", "mix_pre_g_2", "w_in_2",
        "ssd_conv_w_2", "ssd_conv_b_2", "ssd_dt_bias_2", "ssd_a_log_2", "ssd_d_2", "ssd_norm_g_2", "sb_norm_g_2",
        "w_out_2", "mix_post_g_2", "ffn_pre_g_2", "w_up_2", "ffn_conv_w_2", "ffn_conv_b_2", "w_down_2",
        "ffn_post_g_2"]


def kernel(**inputs):
    import concourse.bacc as bacc
    from concourse.bass_utils import run_bass_kernel_spmd

    nc = bacc.Bacc("TRN2", target_bir_lowering=False, num_devices=1)
    arrays, aps = {}, {}
    for name in _INS:
        arrays[f"in_{name}"] = np.ascontiguousarray(inputs[name])
    arrays["in_buckets"] = bucket_table()
    for name, arr in arrays.items():
        aps[name[3:]] = nc.dram_tensor(name, arr.shape, mybir.dt.from_np(arr.dtype), kind="ExternalInput").ap()
    out = nc.dram_tensor("out_0", (1, SEQ, D), F32, kind="ExternalOutput").ap()
    program(nc, aps, out)
    r = run_bass_kernel_spmd(nc, [arrays], core_ids=[0])
    return r.results[0]["out_0"]
```
